# Optimizing a Trainium2 kernel written in Bass

```python
import jax, jax.numpy as jnp
from jax import lax
import numpy as np

D_MODEL = 1024
BATCH = 1
SEQ = 512
DEPTH = 1
DEC_BATCH = 8
DEC_SEQ = 8
PAST_LEN = 1024
PAGE_SIZE = 128

N_META = 16
HEAD_DIM = 64
N_HEADS = D_MODEL // 128
N_KV = N_HEADS // 4
Q_PER_KV = N_HEADS // N_KV
WINDOW = 128
ATT_BLOCK = 128
GLA_HEADS = 4
GLA_DK = D_MODEL // 2
GLA_DV = D_MODEL
GLA_HK = GLA_DK // GLA_HEADS
GLA_HV = GLA_DV // GLA_HEADS
GLA_RANK = 16
GLA_TAU = 16.0
GLA_CHUNK = 64
N_GROUPS = 4
EXP_PER_GROUP = 8
N_EXPERTS = N_GROUPS * EXP_PER_GROUP
TOP_K = 2
D_EXPERT = D_MODEL // 4
DN_ALPHA = (2.0 * DEPTH) ** 0.25
DN_BETA = (8.0 * DEPTH) ** -0.25
EPS = 1e-5
IN_WIDTHS = (N_HEADS * HEAD_DIM, N_KV * HEAD_DIM, N_KV * HEAD_DIM, GLA_DK, GLA_DK, GLA_DV, GLA_RANK, GLA_DV, 2 * D_MODEL)

kernel_name = "hybrid_swa_gla_hmoe_decoder_step"

def layer_norm(x, g, b):
    xf = x.astype(jnp.float32)
    mu = jnp.mean(xf, -1, keepdims=True)
    var = jnp.mean(jnp.square(xf - mu), -1, keepdims=True)
    return ((xf - mu) * lax.rsqrt(var + EPS) * g + b).astype(x.dtype)

def alibi_slopes():
    return jnp.exp2(-8.0 * jnp.arange(1, N_HEADS + 1, dtype=jnp.float32) / N_HEADS)

def split_points():
    pts, acc = [], 0
    for w in IN_WIDTHS[:-1]:
        acc += w
        pts.append(acc)
    return pts

def front_pad(a, n):
    return jnp.pad(a, ((0, 0), (n, 0)) + ((0, 0),) * (a.ndim - 2))

def mixer_inputs(u, w_in_l, w_alpha2_l, b_alpha_l):
    z = u @ w_in_l
    q, k, v, gq, gk, gv, ga, gr, gate_pre = jnp.split(z, split_points(), axis=-1)
    lead = u.shape[:-1]
    q = q.reshape(lead + (N_KV, Q_PER_KV, HEAD_DIM))
    k = k.reshape(lead + (N_KV, HEAD_DIM))
    v = v.reshape(lead + (N_KV, HEAD_DIM))
    gq = gq.reshape(lead + (GLA_HEADS, GLA_HK)) * GLA_HK ** -0.5
    gk = gk.reshape(lead + (GLA_HEADS, GLA_HK))
    gv = gv.reshape(lead + (GLA_HEADS, GLA_HV))
    log_a = jax.nn.log_sigmoid((ga @ w_alpha2_l + b_alpha_l).astype(jnp.float32)) / GLA_TAU
    log_a = log_a.reshape(lead + (GLA_HEADS, GLA_HK))
    return q, k, v, gq, gk, gv, log_a, gr, gate_pre

def sink_attention(q, k, v, q_pos, k_pos, sink):
    s = jnp.einsum('...qkgd,...skd->...kgqs', q, k).astype(jnp.float32) * HEAD_DIM ** -0.5
    dist = q_pos[..., :, None] - k_pos[..., None, :]
    mask = (dist >= 0) & (dist < WINDOW) & (k_pos[..., None, :] >= 0)
    slopes = alibi_slopes().reshape(N_KV, Q_PER_KV)[:, :, None, None]
    s = s - slopes * dist.astype(jnp.float32)[..., None, None, :, :]
    s = jnp.where(mask[..., None, None, :, :], s, -jnp.inf)
    sk = jnp.broadcast_to(sink.astype(jnp.float32).reshape(N_KV, Q_PER_KV, 1, 1), s.shape[:-1] + (1,))
    p = jax.nn.softmax(jnp.concatenate([s, sk], -1), axis=-1)[..., :-1]
    return jnp.einsum('...kgqs,...skd->...qkgd', p.astype(v.dtype), v)

def swa_prompt(q, k, v, sink):
    B, L = q.shape[:2]
    pad = (-N_META) % ATT_BLOCK
    Lp = L + pad
    nb = Lp // ATT_BLOCK
    qb = front_pad(q, pad).reshape(B, nb, ATT_BLOCK, N_KV, Q_PER_KV, HEAD_DIM)
    kb = front_pad(k, pad).reshape(B, nb, ATT_BLOCK, N_KV, HEAD_DIM)
    vb = front_pad(v, pad).reshape(B, nb, ATT_BLOCK, N_KV, HEAD_DIM)
    prev = lambda a: jnp.concatenate([jnp.zeros_like(a[:, :1]), a[:, :-1]], 1)
    k_band = jnp.concatenate([prev(kb), kb], 2)
    v_band = jnp.concatenate([prev(vb), vb], 2)
    pos = (jnp.arange(Lp) - pad).reshape(nb, ATT_BLOCK)
    k_pos = jnp.concatenate([pos - ATT_BLOCK, pos], 1)
    o = sink_attention(qb, k_band, v_band, pos, k_pos, sink)
    return o.reshape(B, Lp, N_HEADS * HEAD_DIM)[:, pad:]

def swa_sample(q, k, v, buf_k, buf_v, sink):
    Bd, T = q.shape[:2]
    nbuf = buf_k.shape[1]
    k_all = jnp.concatenate([buf_k.astype(k.dtype), k], 1)
    v_all = jnp.concatenate([buf_v.astype(v.dtype), v], 1)
    k_pos = PAST_LEN - nbuf + jnp.arange(nbuf + T)
    q_pos = PAST_LEN + jnp.arange(T)
    o = sink_attention(q, k_all, v_all, q_pos, k_pos, sink)
    return o.reshape(Bd, T, N_HEADS * HEAD_DIM), k_all[:, -nbuf:], v_all[:, -nbuf:]

def gla_scan(q, k, v, log_a, s0, chunk):
    B, T, H, _ = q.shape
    n = T // chunk
    to_chunks = lambda a: a.astype(jnp.float32).reshape(B, n, chunk, H, a.shape[-1]).transpose(1, 0, 3, 2, 4)
    xs = tuple(to_chunks(a) for a in (q, k, v, log_a))
    causal = jnp.tril(jnp.ones((chunk, chunk), bool))[..., None]

    def step(S, inp):
        qi, ki, vi, ai = inp
        b = jnp.cumsum(ai, axis=-2)
        o_inter = jnp.einsum('bhck,bhkv->bhcv', qi * jnp.exp(b), S)
        decay = jnp.exp(jnp.where(causal, b[..., :, None, :] - b[..., None, :, :], -jnp.inf))
        att = jnp.einsum('bhtk,bhtsk,bhsk->bhts', qi, decay, ki)
        o = o_inter + jnp.einsum('bhts,bhsv->bhtv', att, vi)
        b_last = b[..., -1:, :]
        S_new = S * jnp.exp(b_last[..., 0, :])[..., None] + jnp.einsum('bhck,bhcv->bhkv', ki * jnp.exp(b_last - b), vi)
        return S_new, o

    S_fin, ys = lax.scan(step, s0, xs)
    out = ys.transpose(1, 0, 3, 2, 4).reshape(B, T, H, v.shape[-1])
    return out, S_fin

def gla_output(o, gr, norm_g):
    of = o.astype(jnp.float32)
    of = of * lax.rsqrt(jnp.mean(of * of, -1, keepdims=True) + EPS)
    of = of.reshape(o.shape[:-2] + (GLA_DV,)) * norm_g
    return of.astype(gr.dtype) * jax.nn.silu(gr)

def merge_branches(y_attn, y_gla, gate_pre, b_gate_l, w_attn_br_l, w_gla_br_l, w_out_l):
    g_attn, g_gla = jnp.split(jax.nn.sigmoid(gate_pre + b_gate_l), 2, axis=-1)
    h = g_attn * (y_attn @ w_attn_br_l) + g_gla * (y_gla @ w_gla_br_l)
    return h @ w_out_l

def hier_moe(u, w_rg, b_rg, w_re, b_re, w_g, w_u, w_d):
    shp = u.shape
    t = u.reshape(-1, D_MODEL)
    g_logits = (t @ w_rg + b_rg).astype(jnp.float32)
    g_prob = jax.nn.softmax(g_logits, axis=-1)
    g_idx = jnp.argmax(g_logits, axis=-1)
    e_logits = (t @ w_re + b_re).astype(jnp.float32).reshape(-1, N_GROUPS, EXP_PER_GROUP)
    e_in = jnp.einsum('ng,nge->ne', jax.nn.one_hot(g_idx, N_GROUPS, dtype=jnp.float32), e_logits)
    top_v, top_i = lax.top_k(e_in, TOP_K)
    w = jax.nn.softmax(top_v, axis=-1) * jnp.max(g_prob, axis=-1, keepdims=True)
    e_glob = g_idx[:, None] * EXP_PER_GROUP + top_i
    combine = jnp.sum(jax.nn.one_hot(e_glob, N_EXPERTS, dtype=jnp.float32) * w[..., None], axis=1)
    y = jnp.zeros(t.shape, jnp.float32)
    for e in range(N_EXPERTS):
        he = jax.nn.silu(t @ w_g[e]) * (t @ w_u[e])
        y = y + combine[:, e:e + 1] * (he @ w_d[e])
    return y.astype(u.dtype).reshape(shp)

def setup_inputs(seed: int = 0) -> dict:
    key = jax.random.key(seed)
    ks = iter(jax.random.split(key, 40))
    f32 = jnp.float32

    def nrm(shape, scale):
        return jax.random.normal(next(ks), shape, f32) * scale

    n_buf = min(WINDOW, PAST_LEN)
    d_in = sum(IN_WIDTHS)
    return {
        "x_prompt": nrm((BATCH, SEQ, D_MODEL), 1.0),
        "x_sample": nrm((DEC_BATCH, DEC_SEQ, D_MODEL), 1.0),
        "state_swa_k": nrm((DEPTH, DEC_BATCH, n_buf, N_KV, HEAD_DIM), 1.0),
        "state_swa_v": nrm((DEPTH, DEC_BATCH, n_buf, N_KV, HEAD_DIM), 1.0),
        "state_gla": nrm((DEPTH, DEC_BATCH, GLA_HEADS, GLA_HK, GLA_HV), 0.3),
        "meta_tokens": nrm((N_META, D_MODEL), 1.0),
        "ln_emb_g": 1.0 + nrm((D_MODEL,), 0.02),
        "ln_emb_b": nrm((D_MODEL,), 0.02),
        "w_in": nrm((DEPTH, D_MODEL, d_in), D_MODEL ** -0.5),
        "b_gate": nrm((DEPTH, 2 * D_MODEL), 0.02),
        "attn_sink": nrm((DEPTH, N_HEADS), 0.5),
        "w_alpha2": nrm((DEPTH, GLA_RANK, GLA_DK), GLA_RANK ** -0.5),
        "b_alpha": nrm((DEPTH, GLA_DK), 0.02),
        "gla_norm_g": 1.0 + nrm((DEPTH, GLA_DV), 0.02),
        "w_attn_br": nrm((DEPTH, N_HEADS * HEAD_DIM, D_MODEL), (N_HEADS * HEAD_DIM) ** -0.5),
        "w_gla_br": nrm((DEPTH, GLA_DV, D_MODEL), GLA_DV ** -0.5),
        "w_out": nrm((DEPTH, D_MODEL, D_MODEL), D_MODEL ** -0.5 * DN_BETA),
        "ln1_g": 1.0 + nrm((DEPTH, D_MODEL), 0.02),
        "ln1_b": nrm((DEPTH, D_MODEL), 0.02),
        "w_router_group": nrm((DEPTH, D_MODEL, N_GROUPS), D_MODEL ** -0.5),
        "b_router_group": nrm((DEPTH, N_GROUPS), 0.01),
        "w_router_expert": nrm((DEPTH, D_MODEL, N_EXPERTS), D_MODEL ** -0.5),
        "b_router_expert": nrm((DEPTH, N_EXPERTS), 0.01),
        "w_exp_gate": nrm((DEPTH, N_EXPERTS, D_MODEL, D_EXPERT), D_MODEL ** -0.5),
        "w_exp_up": nrm((DEPTH, N_EXPERTS, D_MODEL, D_EXPERT), D_MODEL ** -0.5),
        "w_exp_down": nrm((DEPTH, N_EXPERTS, D_EXPERT, D_MODEL), D_EXPERT ** -0.5 * DN_BETA),
        "ln2_g": 1.0 + nrm((DEPTH, D_MODEL), 0.02),
        "ln2_b": nrm((DEPTH, D_MODEL), 0.02),
    }

def reference(x_prompt, x_sample, state_swa_k, state_swa_v, state_gla,
              meta_tokens, ln_emb_g, ln_emb_b, w_in, b_gate, attn_sink,
              w_alpha2, b_alpha, gla_norm_g, w_attn_br, w_gla_br, w_out,
              ln1_g, ln1_b, w_router_group, b_router_group, w_router_expert,
              b_router_expert, w_exp_gate, w_exp_up, w_exp_down, ln2_g, ln2_b):
    B = x_prompt.shape[0]
    T_s = x_sample.shape[1]
    meta = jnp.broadcast_to(meta_tokens[None].astype(x_prompt.dtype), (B, N_META, D_MODEL))
    hp = layer_norm(jnp.concatenate([meta, x_prompt], axis=1), ln_emb_g, ln_emb_b)
    hs = layer_norm(x_sample, ln_emb_g, ln_emb_b)
    pad_g = (-N_META) % GLA_CHUNK
    kp_l, vp_l, sp_l, ks_l, vs_l, ss_l = [], [], [], [], [], []
    for l in range(DEPTH):
        q, k, v, gq, gk, gv, log_a, gr, gate_pre = mixer_inputs(hp, w_in[l], w_alpha2[l], b_alpha[l])
        y_attn = swa_prompt(q, k, v, attn_sink[l])
        s0 = jnp.zeros((B, GLA_HEADS, GLA_HK, GLA_HV), jnp.float32)
        og, s_p = gla_scan(front_pad(gq, pad_g), front_pad(gk, pad_g), front_pad(gv, pad_g),
                           front_pad(log_a, pad_g), s0, GLA_CHUNK)
        y_gla = gla_output(og[:, pad_g:], gr, gla_norm_g[l])
        mix = merge_branches(y_attn, y_gla, gate_pre, b_gate[l], w_attn_br[l], w_gla_br[l], w_out[l])
        hp = layer_norm(DN_ALPHA * hp + mix, ln1_g[l], ln1_b[l])
        if l == DEPTH - 1:
            hp = hp[:, N_META:]
        ff = hier_moe(hp, w_router_group[l], b_router_group[l], w_router_expert[l], b_router_expert[l],
                      w_exp_gate[l], w_exp_up[l], w_exp_down[l])
        hp = layer_norm(DN_ALPHA * hp + ff, ln2_g[l], ln2_b[l])
        kp_l.append(k[:, -WINDOW:].astype(state_swa_k.dtype))
        vp_l.append(v[:, -WINDOW:].astype(state_swa_v.dtype))
        sp_l.append(s_p.astype(state_gla.dtype))
        q, k, v, gq, gk, gv, log_a, gr, gate_pre = mixer_inputs(hs, w_in[l], w_alpha2[l], b_alpha[l])
        y_attn, nk, nv = swa_sample(q, k, v, state_swa_k[l], state_swa_v[l], attn_sink[l])
        og, s_s = gla_scan(gq, gk, gv, log_a, state_gla[l].astype(jnp.float32), T_s)
        y_gla = gla_output(og, gr, gla_norm_g[l])
        mix = merge_branches(y_attn, y_gla, gate_pre, b_gate[l], w_attn_br[l], w_gla_br[l], w_out[l])
        hs = layer_norm(DN_ALPHA * hs + mix, ln1_g[l], ln1_b[l])
        ff = hier_moe(hs, w_router_group[l], b_router_group[l], w_router_expert[l], b_router_expert[l],
                      w_exp_gate[l], w_exp_up[l], w_exp_down[l])
        hs = layer_norm(DN_ALPHA * hs + ff, ln2_g[l], ln2_b[l])
        ks_l.append(nk.astype(state_swa_k.dtype))
        vs_l.append(nv.astype(state_swa_v.dtype))
        ss_l.append(s_s.astype(state_gla.dtype))
    y_prompt = hp
    y_sample = hs
    new_swa_k_prompt = jnp.stack(kp_l, 0)
    new_swa_v_prompt = jnp.stack(vp_l, 0)
    new_gla_prompt = jnp.stack(sp_l, 0)
    new_swa_k_sample = jnp.stack(ks_l, 0)
    new_swa_v_sample = jnp.stack(vs_l, 0)
    new_gla_sample = jnp.stack(ss_l, 0)
    return (y_prompt, y_sample, new_swa_k_prompt, new_swa_v_prompt, new_gla_prompt, new_swa_k_sample, new_swa_v_sample, new_gla_sample)


_drawn_inputs = setup_inputs


def setup_inputs(seed=0):
    import zlib

    import numpy as np

    out = dict(_drawn_inputs(seed))
    spreads = {}
    factors = {'b_gate': 8.0,
     'attn_sink': 5.174,
     'b_alpha': 6.591,
     'gla_norm_g': 8.0,
     'b_router_group': 24.575,
     'b_router_expert': 8.0,
     'ln2_g': 7.77,
     'ln2_b': 8.671}
    for name, (base, spread) in spreads.items():
        noise = np.random.default_rng([zlib.crc32(name.encode()), seed]).standard_normal(out[name].shape)
        drawn = base * np.exp(spread * noise) if base else spread * noise
        out[name] = __import__('jax').numpy.asarray(drawn.astype(out[name].dtype))
    for name, factor in factors.items():
        out[name] = (out[name] * factor).astype(out[name].dtype)
    return out
```

```python
import concourse.bass as bass
from concourse import mybir
from contextlib import ExitStack

P = 128
D = 1024
KC = D // P
SEQ, NB_S, T_S, N_META = 512, 8, 8, 16
NS = NB_S * T_S
TQ = SEQ + NS
T = TQ + N_META
TILES = 5
ROWS = [P, P, P, P, NS]
ROWS_ALL = [P, P, P, P, NS + N_META]
HQ = TQ // 2
HA = T // 2
HEADS, N_KV, HD, WINDOW = 8, 2, 64, 128
GH, HK, HV = 4, 128, 256
CH = 64
NCH = SEQ // CH
RANK = 16
N_EXP, N_GRP, EPG, F = 32, 4, 8, 256
EPS = 1e-5
ALPHA = 2.0 ** 0.25
C_Q, C_K, C_V, C_GQ, C_GK, C_GV, C_GA, C_GR, C_GATE = 0, 512, 640, 768, 1280, 1792, 2816, 2832, 3856
MAX_TILES = 44
PAD_ROW = 4096
NBANK = 8
RING = 3

CONST = {}
_at = 0
for _n, _w in (("ident", 128), ("tri", 128), ("ones", 128), ("scan", T), ("bias", 2048), ("sbias", 272),
               ("cmask", 64), ("smask", 64), ("bmask", 8), ("i4", 4), ("i8", 8), ("valid", 5), ("tok", 5), ("pid", 1)):
    CONST[_n] = (_at, _w)
    _at += _w
CONST_W = _at
VEC = {}
_at = 0
for _n, _w in (("sink", 8), ("ssink", 2), ("balpha", 4), ("bgate", 16), ("normg", 8), ("brout", 36)):
    VEC[_n] = (_at, _w)
    _at += _w
VEC_W = _at

UNITS = [("p", j, pair) for j in range(4) for pair in range(4)] + [("s", bg, kv) for bg in range(2) for kv in range(2)]


def job_order():
    o = []
    for i in range(TILES):
        o += [(("hT", i, 0), "A"), (("hT", i, 1), "V")]
    o += [(("q", t, x), "A") for t in range(4) for x in range(2)]
    o += [(("k", x), "A") for x in range(2)]
    o += [(("v", i), "V") for i in range(TILES)]
    o += [(("ga", x), "V") for x in range(2)]
    o += [(("la", g, x), "A") for g in range(GH) for x in range(2)]
    o += [(("gq", g, x), "V") for g in range(GH) for x in range(2)]
    o += [(("gk", g, x), "V") for g in range(GH) for x in range(2)]
    o += [(("gv", x, i), "V") for x in range(2) for i in range(TILES)]
    o += [(("ktok", 0), "V"), (("ktok", 1), "V")]
    o += [(("kbT", x), "A") for x in range(2)]
    n = len(UNITS)
    for u in range(n + 3):
        if u < n:
            o.append((("s", u), "V"))
        if 0 <= u - 2 < n:
            o.append((("pT", u - 2), "A"))
        if 0 <= u - 3 < n:
            o.append((("o", u - 3), "V"))
    for g in range(GH):
        o += [(("keT", g, 0), "A"), (("keT", g, 1), "A"), (("att", g), "V")]
        o += [(("U", g, c), "V") for c in range(-1, NCH)]
        o += [(("go", g, i), "A") for i in range(4)]
        o += [(("gso", g), "A")]
        o += [(("sU", g, x), "V") for x in range(4)]
    o += [(("gr", t, x), "A") for t in range(8) for x in range(2)]
    o += [(("yT", i, x), "V") for i in range(TILES) for x in range(2)]
    for m in range(8):
        for x in range(2):
            o += [(("gA", m, x), "A"), (("gB", m, x), "A"), (("bA", m, x), "V"), (("bB", m, x), "V")]
    o += [(("mix", x, i), "V") for x in range(2) for i in range(TILES)]
    for i in range(TILES):
        o += [(("h1T", i, 0), "A"), (("h1T", i, 1), "A"), (("rt", i), "V")]
    o += [(("cnt",), "V"), (("pos",), "V"), (("lst",), "V")]
    return o


def weight_chunks():
    return ([("q", ("q", 3, 1)), ("kv", ("v", 4)), ("ga", ("ga", 1)), ("gq", ("gq", 3, 1)), ("gk", ("gk", 3, 1)),
             ("gv0", ("gv", 0, 4)), ("gv1", ("gv", 1, 4)), ("gr0", ("gr", 3, 1)), ("gr1", ("gr", 7, 1))]
            + [(f"{n}{y}", ("bB", 2 * y + 1, 1)) for y in range(4) for n in ("gates", "branch")]
            + [(f"wo{x}", ("mix", x, 4)) for x in range(2)])


def layout():
    at = {}
    top = 0
    for n, w in (("const", CONST_W), ("vec", VEC_W), ("lng", D), ("lnb", D), ("wrt", KC * 36), ("small", 256),
                 ("ring", RING * KC * 512), ("hT", KC * T), ("gq", GH * TQ), ("gk", GH * T), ("gv", TILES * D),
                 ("yaT", 4 * TQ), ("osb", TILES * D), ("R", 11200)):
        at[n] = top
        top += -(-w * 4 // 32) * 32
    at["end"] = top

    def inside(base, items):
        x = at[base]
        for n, w in items:
            at[n] = x
            x += -(-w * 4 // 32) * 32
        return x

    e1 = inside("R", [("qT", 4 * SEQ), ("qs", 4 * NS), ("kT", T), ("v", TILES * P), ("vm", P), ("vn", 8 * P), ("ktok", 2 * P), ("X", 0)])
    assert inside("X", [("dx", 2 * T), ("dt", 2 * T), ("den", 2 * T)]) <= top
    assert inside("X", [("S", 3 * 512), ("PT", 3 * 512), ("sbk", 8 * P), ("sbv", 8 * P), ("kbT", 8 * P), ("stat", 3 * 16)]) <= top
    assert inside("R", [("kem", 2 * 5 * P), ("am", 2 * 5 * 64), ("Sp", 9 * 256), ("s0", 8 * 256), ("kes", 8 * P),
                        ("qz", 576), ("junk", 256)]) <= top, "gla"
    assert inside("R", [("sgA", 2 * HQ), ("sgB", 2 * HQ), ("tA", HQ), ("tB", HQ)]) <= top
    inside("R", [("h1", TILES * D)])
    at["gaT"] = at["osb"]
    inside("yaT", [("rs", 4 * TQ)])
    assert inside("hT", [("wgu0", KC * 512), ("wd0", 2048), ("wgu1", KC * 512), ("wd1", 2048)]) <= at["yaT"]
    assert inside("ring", [("Xg", 2 * D), ("XT", 2 * D), ("Yt", 2 * D), ("sil", 2 * F), ("act", 2 * F), ("aT", 2 * F)]) <= at["hT"]
    inside("hT", [("y0", TILES * D)])
    inside("osb", [("y1", TILES * D)])
    return at


def decoder_kernel(nc, A, O):
    f32, i32 = mybir.dt.float32, mybir.dt.int32
    ALU, ACT, AX = mybir.AluOpType, mybir.ActivationFunctionType, mybir.AxisListType
    ORDER = job_order()
    INDEX = {k: n for n, (k, _) in enumerate(ORDER)}
    DRAINER = dict(ORDER)
    DRAINS = {}
    for eng in "AV":
        for n, k in enumerate([k for k, e in ORDER if e == eng]):
            DRAINS[k] = n + 1
    LAST_USE = weight_chunks()
    CHUNKS = [n for n, _ in LAST_USE]
    AT = layout()
    ctx = ExitStack()
    with ctx:
        arena = ctx.enter_context(nc.sbuf_tensor("arena", [P, AT["end"] // 4], f32))

        def sb(name, shape, dt=f32):
            n = 1
            for x in shape[1:]:
                n *= x
            o = AT[name] // 4
            ap = arena[:, o:o + n]
            if dt != f32:
                ap = ap.bitcast(dt)
            if len(shape) == 3:
                ap = ap.rearrange("p (a b) -> p a b", b=shape[2])
            if len(shape) == 4:
                ap = ap.rearrange("p (a b c) -> p a b c", b=shape[2], c=shape[3])
            return ap

        def sem(name):
            return ctx.enter_context(nc.semaphore(name))

        const = sb("const", [P, CONST_W])
        vec = sb("vec", [P, VEC_W])

        def cst(n):
            return const[:, CONST[n][0]:CONST[n][0] + CONST[n][1]]

        def vc(n):
            return vec[:, VEC[n][0]:VEC[n][0] + VEC[n][1]]

        ident, tri, ones = cst("ident"), cst("tri"), cst("ones")
        bias = cst("bias").rearrange("p (h k c) -> p h k c", h=4, k=2)
        sbias = cst("sbias").rearrange("p (k c) -> p k c", k=2)
        lng, lnb = sb("lng", [P, D]), sb("lnb", [P, D])
        wrt = sb("wrt", [P, KC, 36])
        small = sb("small", [P, 256])
        ring = sb("ring", [P, RING, KC * 512])
        hT = sb("hT", [P, KC, T])
        gq, gk = sb("gq", [P, GH, TQ]), sb("gk", [P, GH, T])
        sg = sb("gq", [P, 8, TQ])
        gv, ygT = sb("gv", [P, TILES, D]), sb("gv", [P, 8, TQ])
        h, osb, mixT, h1T = (sb("osb", [P, TILES, D]), sb("osb", [P, TILES, D]), sb("osb", [P, 8, TQ]),
                             sb("osb", [P, 8, TQ]))
        yaT = sb("yaT", [P, 4, TQ])
        qs = sb("qs", [P, NB_S, 4 * T_S])
        qT, kT, v, vm = sb("qT", [P, 4, SEQ]), sb("kT", [P, T]), sb("v", [P, TILES, P]), sb("vm", [P, P])
        vn, ktok = sb("vn", [P, 8, P]), sb("ktok", [P, 2, P])
        gaT = sb("gaT", [P, T])
        dx, dt_, den = sb("dx", [P, 2, T]), sb("dt", [P, 2, T]), sb("den", [P, 2, T])
        S, PT = sb("S", [P, 3, 512]), sb("PT", [P, 3, 4 * P])
        sbk, sbv, kbT = sb("sbk", [P, 8, P]), sb("sbv", [P, 8, P]), sb("kbT", [P, 8, P])
        stat = sb("stat", [P, 3, 16])
        kem, am = sb("kem", [P, 2, 5, P]), sb("am", [P, 2, 5 * 64])
        Sp, s0, kes = sb("Sp", [P, 9, 256]), sb("s0", [P, 8, 256]), sb("kes", [P, 8, P])
        qz, junk = sb("qz", [P, 576]), sb("junk", [P, 256])
        sgA, sgB, tA, tB = sb("sgA", [P, 2, HQ]), sb("sgB", [P, 2, HQ]), sb("tA", [P, HQ]), sb("tB", [P, HQ])
        h1 = sb("h1", [P, TILES, D])
        fin, em = small[:, 0:68].rearrange("p (g c) -> p g c", c=17), small[:, 68:104].rearrange("p (g c) -> p g c", c=9)
        ss, rr = small[:, 104:124], small[:, 124:144]
        bst = small[:, 144:144 + 60].rearrange("p (i c) -> p i c", c=12)
        mv = small[:, 204:214].rearrange("p (i c) -> p i c", c=2)
        rstd = small[:, 214:224]
        wgu = [sb("wgu0", [P, KC, 512]), sb("wgu1", [P, KC, 512])]
        wd = [sb("wd0", [P, 2, D]), sb("wd1", [P, 2, D])]
        Xg, XT, Yt = sb("Xg", [P, 2, D]), sb("XT", [P, 2, KC, P]), sb("Yt", [P, 2, D])
        sil, act_, aT = sb("sil", [P, 2, F]), sb("act", [P, 2, F]), sb("aT", [P, 2, 2, P])
        tb = ctx.enter_context(nc.sbuf_tensor("tb", [P, MAX_TILES, 4], i32))
        w2 = ctx.enter_context(nc.sbuf_tensor("w2", [RANK, GH * HK], f32))
        y0, y1 = sb("y0", [P, TILES, D]), sb("y1", [P, TILES, D])
        lst = ctx.enter_context(nc.sbuf_tensor("lst", [1, 132], i32))
        idx = ctx.enter_context(nc.sbuf_tensor("idx", [P, 4, 4], i32))
        wsel = ctx.enter_context(nc.sbuf_tensor("wsel", [P, 2], f32))
        ent = ctx.enter_context(nc.sbuf_tensor("ent", [P, 2 * TILES, 4], i32))
        rowi = ctx.enter_context(nc.sbuf_tensor("rowi", [P, 2 * TILES], i32))

        rs_off = [0]
        rs_base = sb("rs", [P, 4 * TQ])

        def scratch(n):
            o = rs_off[0]
            rs_off[0] += n
            assert rs_off[0] <= 4 * TQ
            return rs_base[:, o:o + n]

        R = {}
        for n, w in (("lg", 5 * 36), ("gmax", 5), ("gt", 20), ("gmin", 5), ("goh", 20), ("eg", 20), ("gsum", 5),
                     ("pr", 160), ("ein", 40), ("m1", 5), ("t8", 40), ("mn", 5), ("oh1", 40), ("oh2", 40), ("m2", 5),
                     ("ex", 5), ("w1", 5), ("w2", 5), ("M1", 160), ("M2", 160), ("M", 160), ("cnt", 32), ("nt", 32),
                     ("inc", 32), ("pos", 160), ("q", 160), ("t160", 160), ("r1", 10), ("eg1", 1), ("one32", 32)):
            R[n] = scratch(w)

        psum = [ctx.enter_context(nc.psum_tensor(f"bank{n}", [P, 512], f32)) for n in range(NBANK)]

        def bank(key):
            return psum[INDEX[key] % NBANK]

        tbl_d = nc.dram_tensor("slot_table", [P * MAX_TILES, 4], i32, kind="Internal").ap()
        h_d = nc.dram_tensor("h_spill", [TILES * P, D], f32, kind="Internal").ap()
        h1_d = nc.dram_tensor("h1_rows", [TQ, D], f32, kind="Internal").ap()
        y_d = nc.dram_tensor("expert_rows", [2 * TQ, D], f32, kind="Internal").ap()

        w2_in = sem("w2_in")
        wrt_in = sem("wrt_in")
        pool_held = sem("pool_held")
        x_in = sem("x_in")
        const_in = sem("const_in")
        ln_in = sem("ln_in")
        wchunk = [sem(f"wchunk{n}") for n in range(RING)]
        psum_full = sem("psum_full")
        act_drained = sem("act_drained")
        dve_drained = sem("dve_drained")
        dve_chain = sem("dve_chain")
        act_chain = sem("act_chain")
        ln_var = sem("ln_var")
        ln_std = sem("ln_std")
        h_ready = sem("h_ready")
        spilled = sem("spilled")
        h_back = sem("h_back")
        log_ready = sem("log_ready")
        dec_ready = sem("dec_ready")
        exp_ready = sem("exp_ready")
        qk_ready = sem("qk_ready")
        state_in = sem("state_in")
        rows_moved = sem("rows_moved")
        max_ready = sem("max_ready")
        p_exp = sem("p_exp")
        p_norm = sem("p_norm")
        s0_in = sem("s0_in")
        s0_out = sem("s0_out")
        sp_out = sem("sp_out")
        kes_ready = sem("kes_ready")
        att_used = sem("att_used")
        ss_ready = sem("ss_ready")
        rms_ready = sem("rms_ready")
        sp_final = sem("sp_final")
        s0_final = sem("s0_final")
        silu_ready = sem("silu_ready")
        y_norm = sem("y_norm")
        h1_ready = sem("h1_ready")
        h1_stored = sem("h1_stored")
        tbl_init = sem("tbl_init")
        pad_ready = sem("pad_ready")
        rt_exp_in = sem("rt_exp_in")
        rt_exp = sem("rt_exp")
        mask_ready = sem("mask_ready")
        ids_ready = sem("ids_ready")
        rows_ready = sem("rows_ready")
        list_ready = sem("list_ready")
        scattered = sem("scattered")
        tb_in = sem("tb_in")
        wg_in = [sem(f"wg_in{n}") for n in range(2)]
        wd_in = [sem(f"wd_in{n}") for n in range(2)]
        gathered = [sem(f"gathered{n}") for n in range(2)]
        y_sent = [sem(f"y_sent{n}") for n in range(2)]
        gidx_ready, sidx_ready = sem("gidx_ready"), sem("sidx_ready")
        xt_full, gu_full, at_full, dn_full = sem("xt_full"), sem("gu_full"), sem("at_full"), sem("dn_full")
        xt_act, xt_dve = sem("xt_act"), sem("xt_dve")
        silu_done, act_done, at_done = sem("silu_done"), sem("act_done"), sem("at_done")
        w_ready = sem("w_ready")
        dn_act, dn_dve = sem("dn_act"), sem("dn_dve")
        y_back = sem("y_back")
        out_done = sem("out_done")
        y_ready = sem("y_ready")
        loop_done = sem("loop_done")
        x_zero = sem("x_zero")
        OUTS = [0]

        block = ctx.enter_context(nc.Block())

        def wait_job(eng, key):
            eng.wait_ge(act_drained if DRAINER[key] == "A" else dve_drained, DRAINS[key])

        def wait_full(eng, key):
            eng.wait_ge(psum_full, INDEX[key] + 1)

        def chunk_parts(n):
            slot = ring[:, CHUNKS.index(n) % RING, :]
            w_in = A["w_in"][0].rearrange("(k p) n -> p k n", p=P)
            if n == "q":
                place = slot.rearrange("p (k n) -> p k n", n=512)
                return place, [(place, A["w_q"].rearrange("(k p) n -> p k n", p=P))]
            cols = {"kv": (C_K, 256), "ga": (C_GA, 16), "gq": (C_GQ, 512), "gk": (C_GK, 512),
                    "gv0": (C_GV, 512), "gv1": (C_GV + 512, 512), "gr0": (C_GR, 512), "gr1": (C_GR + 512, 512)}
            if n in cols:
                c, m = cols[n]
                place = slot[:, 0:KC * m].rearrange("p (k n) -> p k n", n=m)
                return place, [(place, w_in[:, :, c:c + m])]
            y = int(n[-1])
            if n[:2] == "wo":
                place = slot.rearrange("p (k n) -> p k n", n=512)
                return place, [(place, A["w_out"][0].rearrange("(k p) n -> p k n", p=P)[:, :, 512 * y:512 * y + 512])]
            x = 256 * y
            if n[:5] == "gates":
                place = slot.rearrange("p (k n) -> p k n", n=512)
                return place, [(place[:, :, 256 * i:256 * i + 256], w_in[:, :, C_GATE + D * i + x:C_GATE + D * i + x + 256])
                               for i in range(2)]
            place = slot[:, 0:12 * 256].rearrange("p (k n) -> p k n", n=256)
            wa = A["w_attn_br"][0].rearrange("(v t p) n -> v p t n", v=2, p=HD)
            wb = A["w_gla_br"][0].rearrange("(k p) n -> p k n", p=P)
            return place, [(place[HD * kv:HD * kv + HD, 0:4, :], wa[kv][:, :, x:x + 256]) for kv in range(2)] \
                + [(place[:, 4:12, :], wb[:, :, x:x + 256])]

        def chunk(n):
            return chunk_parts(n)[0]

        def wait_chunk(eng, n):
            c = CHUNKS.index(n)
            total = sum(len(chunk_parts(m)[1]) for k, m in enumerate(CHUNKS[:c + 1]) if k % RING == c % RING)
            eng.wait_ge(wchunk[c % RING], 16 * total)

        @block.sync
        def _(sp):
            for c, n in enumerate(CHUNKS):
                if c >= RING:
                    wait_full(sp, LAST_USE[c - RING][1])
                for place, src in chunk_parts(n)[1]:
                    sp.dma_start(place, src).then_inc(wchunk[c % RING], 16)
            sp.wait_ge(psum_full, INDEX[("bB", 7, 1)] + 1)
            sp.wait_ge(list_ready, 1)
            tiles = sp.value_load(lst[0:1, 128:129], min_val=1, max_val=MAX_TILES - 2)
            with sp.Fori(0, tiles, 2) as g0:
                for s in range(2):
                    e = sp.value_load(lst[0:1, bass.ds(g0 + s, 1)], min_val=0, max_val=N_EXP - 1)
                    sp.wait_ge(gu_full, g0 + s + 1)
                    for half, w in enumerate(("w_exp_gate", "w_exp_up")):
                        sp.dma_start(wgu[s][:, :, half * F:half * F + F],
                                     A[w][0][bass.ds(e, 1), :, :].rearrange("e (k p) f -> p (e k) f", p=P))\
                          .then_inc(wg_in[s], 16)
                    sp.wait_ge(dn_full, g0 + s + 1)
                    sp.dma_start(wd[s][:, :, :],
                                 A["w_exp_down"][0][bass.ds(e, 1), :, :].rearrange("e (k p) n -> p (e k) n", p=P))\
                      .then_inc(wd_in[s], 16)

        @block.gpsimd
        def _(pool):
            pool.dma_start(lng, A["ln_emb_g"].partition_broadcast(P)).then_inc(ln_in, 16)
            pool.dma_start(lnb, A["ln_emb_b"].partition_broadcast(P)).then_inc(ln_in, 16)
            pool.memset(tb[:, :, :], PAD_ROW).then_inc(pad_ready, 1)
            pool.wait_ge(pad_ready, 1)
            pool.dma_start(tbl_d.rearrange("(p g) c -> p g c", p=P), tb[:, :, :]).then_inc(tbl_init, 16)
            pool.dma_start(wrt[:, :, 0:4], A["w_router_group"][0].rearrange("(k p) n -> p k n", p=P)).then_inc(wrt_in, 16)
            pool.dma_start(wrt[:, :, 4:36], A["w_router_expert"][0].rearrange("(k p) n -> p k n", p=P)).then_inc(wrt_in, 16)
            pool.dma_start(w2[:, :], A["w_alpha2"][0]).then_inc(w2_in, 16)
            for b in range(2):
                k, vv = (("state_swa_k", 5), ("state_swa_v", 6))[b]
                s_in = A[k][0]
                pool.dma_start(O[vv][0][:, 0:WINDOW - T_S], s_in[:, T_S:WINDOW]).then_inc(out_done, 16)
                OUTS[0] += 1
            for i in range(TILES):
                pool.wait_ge(h_ready, i + 1)
                pool.dma_start(h_d[i * P:i * P + ROWS[i], :], h[0:ROWS[i], i, :]).then_inc(spilled, 16)
            pool.wait_ge(h_ready, TILES)
            wait_job(pool, ("v", 4))
            pool.dma_start(vm[0:N_META, :], v[NS:NS + N_META, 4, :]).then_inc(rows_moved, 16)
            for b in range(8):
                pool.dma_start(vn[0:T_S, b, :], v[b * T_S:b * T_S + T_S, 4, :]).then_inc(rows_moved, 16)
            wait_job(pool, ("v", 3))
            pool.dma_start(O[3][0, 0].rearrange("t k d -> t (k d)"), v[:, 3, :]).then_inc(out_done, 16)
            pool.dma_start(O[6][0][:, WINDOW - T_S:WINDOW].rearrange("b t k d -> b t (k d)"), v[0:NS, 4, :])\
                .then_inc(out_done, 16)
            pool.wait_ge(qk_ready, GH)
            pool.dma_start(sbk[:, :, :], A["state_swa_k"][0].rearrange("b s k d -> s b (k d)")).then_inc(state_in, 16)
            pool.dma_start(sbv[:, :, :], A["state_swa_v"][0].rearrange("b s k d -> s b (k d)")).then_inc(state_in, 16)
            wait_job(pool, ("ktok", 1))
            pool.dma_start(O[2][0, 0].rearrange("t k d -> t (k d)"), ktok[:, 0, :]).then_inc(out_done, 16)
            pool.dma_start(O[5][0][:, WINDOW - T_S:WINDOW].rearrange("b t k d -> b t (k d)"), ktok[0:NS, 1, :])\
                .then_inc(out_done, 16)
            OUTS[0] += 4
            wait_job(pool, ("o", 19))
            pool.wait_ge(out_done, 16 * OUTS[0])
            for g in range(GH):
                if g:
                    pool.wait_ge(s0_out, 16 * g)
                pool.dma_start(s0[:, :, :], A["state_gla"][0][:, g].rearrange("b k v -> k b v")).then_inc(s0_in, 16)
                pool.wait_ge(sp_final, g + 1)
                pool.dma_start(O[4][0, 0, g], Sp[:, 8, :]).then_inc(sp_out, 16)
                pool.wait_ge(s0_final, g + 1)
                pool.dma_start(O[7][0][:, g].rearrange("b k v -> k b v"), s0[:, :, :]).then_inc(s0_out, 16)
            pool.dma_start(lng, A["ln1_g"][0].partition_broadcast(P)).then_inc(ln_in, 16)
            pool.dma_start(lnb, A["ln1_b"][0].partition_broadcast(P)).then_inc(ln_in, 16)
            wait_job(pool, ("bB", 7, 1))
            for i in range(TILES):
                pool.dma_start(h1[0:ROWS[i], i, :], h_d[i * P:i * P + ROWS[i], :]).then_inc(h_back, 16)
            for i in range(TILES):
                pool.wait_ge(h1_ready, i + 1)
                pool.dma_start(h1_d[i * P:i * P + ROWS[i], :], h1[0:ROWS[i], i, :]).then_inc(h1_stored, 16)
            pool.dma_start(lng, A["ln2_g"][0].partition_broadcast(P)).then_inc(ln_in, 16)
            pool.dma_start(lnb, A["ln2_b"][0].partition_broadcast(P)).then_inc(ln_in, 16)
            pool.wait_ge(tbl_init, 16)
            pool.wait_ge(rows_ready, 1)
            for n in range(2 * TILES):
                r = ROWS[n % TILES]
                pool.indirect_dma_start(out=tbl_d[:, :], out_offset=bass.IndirectOffsetOnAxis(ap=rowi[0:r, n:n + 1], axis=0),
                                        in_=ent[0:r, n, :], in_offset=None).then_inc(scattered, 16)
            pool.wait_ge(scattered, 16 * 2 * TILES)
            pool.dma_start(tb[:, :, :], tbl_d.rearrange("(p g) c -> p g c", p=P)).then_inc(tb_in, 16)
            pool.wait_ge(tb_in, 16)
            pool.wait_ge(h1_stored, 16 * TILES)
            pool.memset(Xg[:, :, :], 0.0).then_inc(x_zero, 1)
            pool.wait_ge(x_zero, 1)
            tiles = pool.value_load(lst[0:1, 128:129], min_val=1, max_val=MAX_TILES - 2)

            pool.memset(idx[:, :, :], PAD_ROW).then_inc(x_zero, 1)
            pool.memset(Yt[:, :, :], 0.0).then_inc(x_zero, 1)
            pool.wait_ge(x_zero, 3)
            for s in range(2):
                pool.indirect_dma_start(out=y_d[:, :], out_offset=bass.IndirectOffsetOnAxis(ap=idx[:, 2 + s, 1:2], axis=0),
                                        in_=Yt[:, s, :], in_offset=None,
                                        bounds_check=2 * TQ - 1, oob_is_err=False).then_inc(y_sent[s], 16)

            def hold():
                pool.sem_inc(pool_held, 1)

            def gather(g, s):
                pool.tensor_copy(idx[:, s:s + 1, :], tb[:, bass.ds(g, 1), :]).then_inc(gidx_ready, 1)
                pool.wait_ge(gidx_ready, g + 1)
                hold()
                pool.indirect_dma_start(out=Xg[:, s, :], out_offset=None, in_=h1_d[:, :],
                                        in_offset=bass.IndirectOffsetOnAxis(ap=idx[:, s, 0:1], axis=0),
                                        bounds_check=TQ - 1, oob_is_err=False).then_inc(gathered[s], 16)

            gather(0, 0)
            with pool.Fori(0, tiles, 2) as g0:
                for s in range(2):
                    g = g0 + s
                    pool.wait_ge(xt_full, g + 1)
                    hold()
                    gather(g + 1, 1 - s)
                    pool.wait_ge(y_sent[s], (g0 + 2) * 8)
                    hold()
                    pool.tensor_copy(idx[:, 2 + s:3 + s, :], tb[:, bass.ds(g, 1), :]).then_inc(sidx_ready, 1)
                    pool.wait_ge(sidx_ready, g + 1)
                    pool.wait_ge(dn_act, g + 2)
                    pool.wait_ge(dn_dve, g + 2)
                    hold()
                    pool.indirect_dma_start(out=y_d[:, :], out_offset=bass.IndirectOffsetOnAxis(ap=idx[:, 2 + s, 1:2], axis=0),
                                            in_=Yt[:, s, :], in_offset=None,
                                            bounds_check=2 * TQ - 1, oob_is_err=False).then_inc(y_sent[s], 16)
            for s in range(2):
                pool.wait_ge(y_sent[s], ((tiles + 1) // 2 + 1) * 16)
                hold()
            for i in range(TILES):
                pool.dma_start(y0[0:ROWS[i], i, :], y_d[i * P:i * P + ROWS[i], :]).then_inc(y_back, 16)
                pool.dma_start(y1[0:ROWS[i], i, :], y_d[TQ + i * P:TQ + i * P + ROWS[i], :]).then_inc(y_back, 16)
            for i in range(TILES):
                pool.wait_ge(y_ready, i + 1)
                dst = O[0][0, i * P:i * P + P, :] if i < 4 else O[1].rearrange("b t d -> (b t) d")
                pool.dma_start(dst, h1[0:ROWS[i], i, :]).then_inc(out_done, 16)
                OUTS[0] += 1
            pool.wait_ge(out_done, 16 * OUTS[0])
            pool.wait_ge(sp_out, 16 * GH)
            pool.wait_ge(s0_out, 16 * GH)

        @block.scalar
        def _(act):
            chain = [0]

            def link(ins):
                chain[0] += 1
                ins.then_inc(act_chain, 1)
                act.wait_ge(act_chain, chain[0])

            for i in range(TILES):
                if i < 4:
                    act.dma_start(h[:, i, :], A["x_prompt"][0, i * P:i * P + P, :]).then_inc(x_in, 16)
                else:
                    act.dma_start(h[0:NS, i, :], A["x_sample"].rearrange("b t d -> (b t) d")).then_inc(x_in, 16)
                    act.dma_start(h[NS:NS + N_META, i, :], A["meta_tokens"]).then_inc(x_in, 16)
                if i == 0:
                    act.dma_start(const, A["const"]).then_inc(const_in, 16)
                    act.dma_start(vec, A["vec"]).then_inc(const_in, 16)

            def drain(key, out, in_, **kw):
                func = kw.pop("func", ACT.Copy)
                wait_full(act, key)
                act.activation(out, in_, func, **kw).then_inc(act_drained, 1)

            def std(n):
                act.wait_ge(ln_var, n + 1)
                act.activation(rstd[:, 5:10], rstd[:, 0:5], ACT.Sqrt).then_inc(ln_std, 1)

            std(0)
            act.wait_ge(const_in, 16 * 2)
            for i in range(TILES):
                r = ROWS_ALL[i]
                drain(("hT", i, 0), hT[:, 0:4, i * P:i * P + r],
                      bank(("hT", i, 0))[:, :].rearrange("p (k c) -> p k c", k=4)[:, :, 0:r])
            for t in range(4):
                drain(("q", t, 0), qT[:, t, 0:HQ], bank(("q", t, 0))[:, 0:HQ], scale=HD ** -0.5)
                wait_full(act, ("q", t, 1))
                act.activation(qT[:, t, HQ:SEQ], bank(("q", t, 1))[:, 0:SEQ - HQ], ACT.Copy, scale=HD ** -0.5)
                act.activation(qs[:, :, t * T_S:t * T_S + T_S],
                               bank(("q", t, 1))[:, SEQ - HQ:HQ].rearrange("p (b t) -> p b t", t=T_S), ACT.Copy,
                               scale=HD ** -0.5).then_inc(act_drained, 1)
            for x in range(2):
                drain(("k", x), kT[:, x * HA:x * HA + HA], bank(("k", x))[:, 0:HA])

            def exps(g):
                b = g % 2
                act.wait_ge(dec_ready, g + 1)
                act.activation(em[:, g, 0:8], dt_[:, b, 31:512:64], ACT.Exp, scale=1 / 16.0)
                link(act.activation(em[:, g, 8:9], dt_[:, b, TQ + 7:TQ + 8], ACT.Exp, scale=1 / 16.0))
                act.activation(den[:, b, :], dx[:, b, :], ACT.Exp, scale=-1 / 16.0)
                act.activation(dt_[:, b, :], dx[:, b, :], ACT.Exp, scale=1 / 16.0).then_inc(exp_ready, 1)

            def logs(g):
                b = g % 2
                if g >= 2:
                    act.wait_ge(qk_ready, g - 1)
                for x in range(2):
                    key = ("la", g, x)
                    wait_full(act, key)
                    act.activation(dx[:, b, x * HA:x * HA + HA], bank(key)[:, 0:HA], ACT.Identity,
                                   bias=vc("balpha")[:, g:g + 1]).then_inc(act_drained, 1)
                act.wait_ge(act_drained, DRAINS[("la", g, 1)])
                link(act.activation(dt_[:, b, :], dx[:, b, :], ACT.Abs))
                link(act.activation(dt_[:, b, :], dt_[:, b, :], ACT.Exp, scale=-1.0))
                act.activation(dt_[:, b, :], dt_[:, b, :], ACT.Ln, bias=1.0).then_inc(log_ready, 1)

            for g in range(2):
                logs(g)
            for g in range(2):
                exps(g)
            for g in range(2, 4):
                logs(g)
                exps(g)
            for x in range(2):
                drain(("kbT", x), kbT[:, 4 * x:4 * x + 4, :], bank(("kbT", x))[:, :].rearrange("p (k c) -> p k c", k=4))

            n = len(UNITS)
            for u in range(n + 2):
                if u < n:
                    kind, a, b = UNITS[u]
                    st = stat[:, u % 3, :]
                    act.wait_ge(max_ready, u + 1)
                    if kind == "p":
                        lo = 0 if a else WINDOW - N_META
                        for kv in range(2):
                            pv = S[:, u % 3, kv * 256 + lo:kv * 256 + 256]
                            act.activation(pv, pv, ACT.Exp, bias=st[:, 2 + kv:3 + kv], accum_out=st[:, 6 + kv:7 + kv])
                        act.activation(st[:, 8:10], st[:, 4:6], ACT.Exp).then_inc(p_exp, 1)
                    else:
                        pv = S[:, u % 3, 0:136]
                        act.activation(pv, pv, ACT.Exp, bias=st[:, 2:3], accum_out=st[:, 6:7])
                        act.activation(st[:, 8:9], st[:, 4:5], ACT.Exp).then_inc(p_exp, 1)
                w = u - 2
                if 0 <= w < n:
                    kind, a, b = UNITS[w]
                    key = ("pT", w)
                    wait_full(act, key)
                    bk = bank(key)[:, :].rearrange("p (a c) -> p a c", a=4)
                    pt = PT[:, w % 3, :].rearrange("p (a c) -> p a c", a=4)
                    if kind == "p" and a:
                        act.activation(pt, bk, ACT.Copy).then_inc(act_drained, 1)
                    elif kind == "p":
                        act.activation(pt[0:N_META, 0:3:2], bk[0:N_META, 0:3:2], ACT.Copy)
                        act.activation(pt[:, 1:4:2], bk[:, 1:4:2], ACT.Copy).then_inc(act_drained, 1)
                    else:
                        act.activation(pt[0:T_S, 1], bk[0:T_S, 1], ACT.Copy)
                        act.activation(pt[:, 0], bk[:, 0], ACT.Copy).then_inc(act_drained, 1)

            wait_job(act, ("o", 19))
            act.wait_ge(out_done, 16 * 6)
            act.wait_ge(spilled, 16 * TILES)
            for g in range(GH):
                if g >= 2:
                    act.wait_ge(kes_ready, g - 1)
                drain(("keT", g, 0), kem[:, g % 2, 0:4, :], bank(("keT", g, 0))[:, :].rearrange("p (k c) -> p k c", k=4))
                r = ROWS_ALL[4]
                drain(("keT", g, 1), kem[0:r, g % 2, 4, :], bank(("keT", g, 1))[0:r, 0:P])
                for i in range(5):
                    key = ("go", g, i) if i < 4 else ("gso", g)
                    r = ROWS[i]
                    drain(key, osb[0:r, i, g * HV:g * HV + HV], bank(key)[0:r, 0:HV])
                    act.wait_ge(act_drained, DRAINS[key])
                    ins = act.activation(junk[0:r, :], osb[0:r, i, g * HV:g * HV + HV], ACT.Square,
                                         accum_out=ss[0:r, 4 * i + g:4 * i + g + 1])
            ins.then_inc(ss_ready, 1)
            act.wait_ge(rms_ready, 1)
            act.activation(rr[:, :], rr[:, :], ACT.Sqrt).then_inc(ss_ready, 1)
            for t in range(8):
                for x in range(2):
                    drain(("gr", t, x), sg[:, t, x * HQ:x * HQ + HQ], bank(("gr", t, x))[:, 0:HQ], func=ACT.Silu)
            act.wait_ge(sp_out, 16 * GH)
            act.wait_ge(s0_out, 16 * GH)
            for m in range(8):
                for x in range(2):
                    n = 2 * m + x
                    for name, dst, o in (("gA", sgA, 0), ("gB", sgB, 8)):
                        if n >= 2:
                            wait_job(act, ("bB", (n - 2) // 2, n % 2))
                        drain((name, m, x), dst[:, n % 2, :], bank((name, m, x))[:, 0:HQ], func=ACT.Sigmoid,
                              bias=vc("bgate")[:, o + m:o + m + 1])
            std(1)
            for i in range(TILES):
                for x in range(2):
                    r = ROWS[i]
                    drain(("h1T", i, x), h1T[:, 4 * x:4 * x + 4, i * P:i * P + r],
                          bank(("h1T", i, x))[:, :].rearrange("p (k c) -> p k c", k=4)[:, :, 0:r])
            act.wait_ge(rt_exp_in, 1)
            act.activation(R["eg"], R["eg"], ACT.Exp)
            act.activation(R["ex"], R["ex"], ACT.Exp).then_inc(rt_exp, 1)

            act.wait_ge(list_ready, 1)
            tiles = act.value_load(lst[0:1, 128:129], min_val=1, max_val=MAX_TILES - 2)

            def drain_xt(g, s):
                act.wait_ge(xt_full, g + 1 + 1)
                act.activation(XT[:, s, 0:4, :], psum[0][:, :].rearrange("p (k c) -> p k c", k=4), ACT.Copy)\
                   .then_inc(xt_act, 1)

            drain_xt(0, 0)
            with act.Fori(0, tiles, 2) as g0:
                for s in range(2):
                    g = g0 + s
                    act.wait_ge(gu_full, g + 3)
                    act.activation(sil[:, s, :], psum[2 + s][:, 0:F], ACT.Silu).then_inc(silu_done, 1)
                    drain_xt(g + 1, 1 - s)
                    act.wait_ge(at_full, g + 1)
                    act.activation(aT[:, s, :, :], psum[4][:, 0:F].rearrange("p (k c) -> p k c", k=2), ACT.Copy)\
                       .then_inc(at_done, 1)
                    act.wait_ge(dn_full, g + 3)
                    act.wait_ge(w_ready, g + 1)
                    act.wait_ge(y_sent[s], (g0 + 2) * 8)
                    act.activation(Yt[:, s, 0:512], psum[5][:, :], ACT.Copy, scale=wsel[:, s:s + 1]).then_inc(dn_act, 1)
            std(2)

        @block.vector
        def _(dve):
            chain = [0]

            def link(ins):
                chain[0] += 1
                ins.then_inc(dve_chain, 1)
                dve.wait_ge(dve_chain, chain[0])

            def layer_norm(n, src, dst, rows, tail):
                link(dve.memset(rstd[:, :], 1.0))
                for i in range(TILES):
                    r = rows[i]
                    for x in range(2):
                        link(dve.bn_stats(bst[0:r, i, 6 * x:6 * x + 6], src[0:r, i, 512 * x:512 * x + 512]))
                    link(dve.bn_aggr(mv[0:r, i, :], bst[0:r, i, :]))
                    ins = dve.tensor_scalar(rstd[0:r, i:i + 1], mv[0:r, i, 1:2], EPS, None, ALU.add)
                ins.then_inc(ln_var, 1)
                dve.wait_ge(ln_std, n + 1)
                link(dve.reciprocal(rstd[:, 0:5], rstd[:, 5:10]))
                dve.wait_ge(ln_in, 32 * (n + 1))
                for i in range(TILES):
                    r = rows[i]
                    link(dve.tensor_scalar(dst[0:r, i, :], src[0:r, i, :], mv[0:r, i, 0:1], rstd[0:r, i:i + 1],
                                           ALU.subtract, ALU.mult))
                    link(dve.tensor_tensor(dst[0:r, i, :], dst[0:r, i, :], lng[0:r, :], ALU.mult))
                    dve.tensor_tensor(dst[0:r, i, :], dst[0:r, i, :], lnb[0:r, :], ALU.add).then_inc(tail, 1)

            def drain(key, out, in_):
                wait_full(dve, key)
                dve.tensor_copy(out, in_).then_inc(dve_drained, 1)

            dve.wait_ge(x_in, 16 * 6)
            dve.wait_ge(const_in, 16 * 2)
            layer_norm(0, h, h, ROWS_ALL, h_ready)
            for i in range(TILES):
                r = ROWS_ALL[i]
                drain(("hT", i, 1), hT[:, 4:8, i * P:i * P + r],
                      bank(("hT", i, 1))[:, :].rearrange("p (k c) -> p k c", k=4)[:, :, 0:r])
            for i in range(TILES):
                r = ROWS_ALL[i]
                drain(("v", i), v[0:r, i, :], bank(("v", i))[0:r, 0:P])
            dve.wait_ge(spilled, 16 * TILES)
            for x in range(2):
                drain(("ga", x), gaT[0:RANK, x * HA:x * HA + HA], bank(("ga", x))[0:RANK, 0:HA])

            def decay(g):
                b = g % 2
                dve.wait_ge(log_ready, g + 1)
                link(dve.scalar_tensor_tensor(dx[:, b, :], dx[:, b, :], 0.0, dt_[:, b, :], ALU.min, ALU.subtract))
                link(dve.tensor_tensor_scan(dt_[:, b, :], cst("scan"), dx[:, b, :], 0.0, ALU.mult, ALU.add))
                bp = dt_[:, b, 0:SEQ].rearrange("p (c t) -> p c t", t=CH)
                dve.tensor_tensor(dx[:, b, 0:SEQ].rearrange("p (c t) -> p c t", t=CH), bp,
                                  bp[:, :, 31:32].broadcast_to([P, NCH, CH]), ALU.subtract)
                dve.tensor_tensor(dx[:, b, TQ:T], dt_[:, b, TQ:T], dt_[:, b, TQ + 7:TQ + 8].broadcast_to([P, N_META]),
                                  ALU.subtract)
                link(dve.tensor_copy(dx[:, b, SEQ:TQ], dt_[:, b, SEQ:TQ]))
                dve.tensor_scalar(dx[:, b, :], dx[:, b, :], 1200.0, -1200.0, ALU.min, ALU.max).then_inc(dec_ready, 1)

            def apply_decay(g):
                b = g % 2
                dve.wait_ge(exp_ready, g + 1)
                dve.tensor_copy(fin[:, g, 0:8], dt_[:, b, 63:512:64])
                dve.tensor_copy(fin[:, g, 8:16], dt_[:, b, 519:576:8])
                dve.tensor_copy(fin[:, g, 16:17], dt_[:, b, T - 1:T])
                dve.tensor_copy(gq[:, g, :], dt_[:, b, 0:TQ])
                dve.tensor_copy(gk[:, g, :], den[:, b, :]).then_inc(qk_ready, 1)

            decay(0)
            decay(1)
            apply_decay(0)
            apply_decay(1)
            for g in range(2, 4):
                decay(g)
                apply_decay(g)
            dve.wait_ge(qk_ready, GH)
            for n, dst, w in (("gq", gq, HQ), ("gk", gk, HA)):
                for g in range(GH):
                    for x in range(2):
                        key = (n, g, x)
                        wait_full(dve, key)
                        c = dst[:, g, x * w:x * w + w]
                        dve.scalar_tensor_tensor(c, bank(key)[:, 0:w], HK ** -0.5 if n == "gq" else 1.0, c, ALU.mult,
                                                 ALU.mult).then_inc(dve_drained, 1)
            for x in range(2):
                for i in range(TILES):
                    r = ROWS_ALL[i]
                    drain(("gv", x, i), gv[0:r, i, 512 * x:512 * x + 512], bank(("gv", x, i))[0:r, :])
            drain(("ktok", 0), ktok[:, 0, :], bank(("ktok", 0))[:, 0:P])
            drain(("ktok", 1), ktok[0:NS, 1, :], bank(("ktok", 1))[0:NS, 0:P])

            n = len(UNITS)
            for u in range(n + 3):
                if u < n:
                    kind, a, b = UNITS[u]
                    st = stat[:, u % 3, :]
                    key = ("s", u)
                    wait_full(dve, key)
                    if kind == "p":
                        lo = 0 if a else WINDOW - N_META
                        sv = S[:, u % 3, :].rearrange("p (k c) -> p k c", k=2)[:, :, lo:256]
                        dve.tensor_tensor(sv, bank(key)[:, :].rearrange("p (k c) -> p k c", k=2)[:, :, lo:256],
                                          bias[:, b, :, lo:256], ALU.add).then_inc(dve_drained, 1)
                        m, sink = 2, vc("sink")[:, 2 * b:2 * b + 2]
                    else:
                        sv = S[:, u % 3, 0:136].rearrange("p (k c) -> p k c", k=1)
                        dve.tensor_tensor(sv[:, 0, :], bank(key)[:, 0:136], sbias[:, b, :], ALU.add)\
                           .then_inc(dve_drained, 1)
                        m, sink = 1, vc("ssink")[:, b:b + 1]
                    dve.wait_ge(dve_drained, DRAINS[key])
                    link(dve.tensor_reduce(st[:, 0:m], sv, AX.X, ALU.max))
                    link(dve.tensor_tensor(st[:, 0:m], st[:, 0:m], sink, ALU.max))
                    dve.tensor_tensor(st[:, 4:4 + m], sink, st[:, 0:m], ALU.subtract)
                    dve.tensor_scalar(st[:, 2:2 + m], st[:, 0:m], -1.0, None, ALU.mult).then_inc(max_ready, 1)
                w = u - 1
                if 0 <= w < n:
                    kind, a, b = UNITS[w]
                    st = stat[:, w % 3, :]
                    dve.wait_ge(p_exp, w + 1)
                    m = 2 if kind == "p" else 1
                    link(dve.tensor_tensor(st[:, 10:10 + m], st[:, 6:6 + m], st[:, 8:8 + m], ALU.add))
                    link(dve.reciprocal(st[:, 12:12 + m], st[:, 10:10 + m]))
                    if kind == "p":
                        lo = 0 if a else WINDOW - N_META
                        sv = S[:, w % 3, :].rearrange("p (k c) -> p k c", k=2)[:, :, lo:256]
                        dve.tensor_tensor(sv, sv, st[:, 12:14].rearrange("p (k c) -> p k c", c=1)
                                          .broadcast_to([P, 2, 256 - lo]), ALU.mult).then_inc(p_norm, 1)
                    else:
                        dve.tensor_scalar(S[:, w % 3, 0:136], S[:, w % 3, 0:136], st[:, 12:13], None, ALU.mult)\
                           .then_inc(p_norm, 1)
                w = u - 3
                if 0 <= w < n:
                    kind, a, b = UNITS[w]
                    kv = b // 2 if kind == "p" else b
                    rows = slice(HD * kv, HD * kv + HD)
                    src = bank(("o", w))
                    if kind == "p":
                        hl = 2 * (b % 2)
                        drain(("o", w), yaT[rows, hl:hl + 2, a * P:a * P + P],
                              src[rows, 0:2 * P].rearrange("p (x c) -> p x c", x=2))
                    else:
                        dst = yaT[rows, :, SEQ + 32 * a:SEQ + 32 * a + 32].rearrange("p h (b t) -> p b h t", t=T_S)
                        src = src[rows, 0:P].rearrange("p (b h t) -> p b h t", h=4, t=T_S)
                        wait_full(dve, ("o", w))
                        for bb in range(4):
                            ins = dve.tensor_copy(dst[:, bb], src[:, bb])
                        ins.then_inc(dve_drained, 1)

            dve.wait_ge(out_done, 16 * 6)
            link(dve.memset(qz[:, :], 0.0))
            dve.memset(ss[:, :], 1.0)
            link(dve.memset(am[:, :, :], 0.0))
            for g in range(GH):
                b = g % 2
                wait_job(dve, ("keT", g, 1))
                if g:
                    wait_full(dve, ("sU", g - 1, 3))
                dve.tensor_tensor(kes[0:NS, :, :], kem[0:NS, b, 4:5, :].broadcast_to([NS, 8, P]),
                                  cst("bmask")[0:NS, :].rearrange("p (b c) -> p b c", c=1).broadcast_to([NS, 8, P]),
                                  ALU.mult)
                dve.tensor_copy(qz[:, :].rearrange("p (b r) -> p b r", r=72)[:, :, 0:T_S],
                                gq[:, g, SEQ:TQ].rearrange("p (b t) -> p b t", t=T_S)).then_inc(kes_ready, 1)
                key = ("att", g)
                wait_full(dve, key)
                bk = bank(key)[:, 0:320].rearrange("p (i t) -> p i t", t=64)
                av = am[:, b, :].rearrange("p (i t) -> p i t", t=64)
                dve.tensor_tensor(av[:, 0:4, :], bk[:, 0:4, :],
                                  cst("cmask").rearrange("p (a t) -> p a t", a=1).broadcast_to([P, 4, 64]), ALU.mult)
                dve.tensor_tensor(av[0:NS, 4, :], bk[0:NS, 4, :], cst("smask")[0:NS, :], ALU.mult)\
                   .then_inc(dve_drained, 1)
                if g:
                    wait_full(dve, ("gso", g - 1))
                for c in range(-1, NCH):
                    key = ("U", g, c)
                    wait_full(dve, key)
                    if c < 0:
                        dve.tensor_scalar(Sp[:, 0, :], bank(key)[:, 0:HV], fin[:, g, 16:17], em[:, g, 0:1], ALU.mult,
                                          ALU.mult).then_inc(dve_drained, 1)
                        dve.wait_ge(dve_drained, DRAINS[key])
                    else:
                        if c == 7 and g:
                            dve.wait_ge(sp_out, 16 * g)
                        dve.tensor_tensor(Sp[:, c + 1, :], bank(key)[:, 0:HV], Sp[:, c, :], ALU.add)\
                           .then_inc(dve_drained, 1)
                        dve.wait_ge(dve_drained, DRAINS[key])
                        if c < NCH - 1:
                            link(dve.tensor_scalar(Sp[:, c + 1, :], Sp[:, c + 1, :], fin[:, g, c:c + 1],
                                                   em[:, g, c + 1:c + 2], ALU.mult, ALU.mult))
                        else:
                            dve.tensor_scalar(Sp[:, 8, :], Sp[:, 8, :], fin[:, g, 7:8], None, ALU.mult)\
                               .then_inc(sp_final, 1)
                dve.wait_ge(s0_in, 16 * (g + 1))
                for x in range(4):
                    key = ("sU", g, x)
                    wait_full(dve, key)
                    sv = s0[:, 2 * x:2 * x + 2, :]
                    dve.tensor_tensor(sv, bank(key)[:, :].rearrange("p (b c) -> p b c", b=2), sv, ALU.add)\
                       .then_inc(dve_drained, 1)
                    dve.wait_ge(dve_drained, DRAINS[key])
                    ins = dve.tensor_tensor(sv, sv, fin[:, g, 8 + 2 * x:10 + 2 * x].rearrange("p (b c) -> p b c", c=1)
                                            .broadcast_to([P, 2, HV]), ALU.mult)
                    if x == 3:
                        ins.then_inc(s0_final, 1)
            dve.wait_ge(ss_ready, 1)
            dve.tensor_scalar(rr[:, :], ss[:, :], 1.0 / HV, EPS, ALU.mult, ALU.add).then_inc(rms_ready, 1)
            dve.wait_ge(ss_ready, 2)
            link(dve.reciprocal(rr[:, :], rr[:, :]))
            for i in range(TILES):
                r = ROWS[i]
                ov = osb[0:r, i, :].rearrange("p (g c) -> p g c", g=GH)
                dve.tensor_tensor(ov, ov, rr[0:r, 4 * i:4 * i + 4].rearrange("p (g c) -> p g c", c=1)
                                  .broadcast_to([r, GH, HV]), ALU.mult).then_inc(y_norm, 1)
            for t in range(8):
                wait_job(dve, ("gr", t, 1))
                link(dve.tensor_scalar(sg[:, t, :], sg[:, t, :], vc("normg")[:, t:t + 1], None, ALU.mult))
            for i in range(TILES):
                r = ROWS[i]
                for x in range(2):
                    key = ("yT", i, x)
                    wait_full(dve, key)
                    dve.tensor_tensor(ygT[:, 4 * x:4 * x + 4, i * P:i * P + r],
                                      bank(key)[:, :].rearrange("p (k c) -> p k c", k=4)[:, :, 0:r],
                                      sg[:, 4 * x:4 * x + 4, i * P:i * P + r], ALU.mult).then_inc(dve_drained, 1)
            for m in range(8):
                for x in range(2):
                    n = 2 * m + x
                    key = ("bA", m, x)
                    wait_full(dve, key)
                    wait_job(dve, ("gA", m, x))
                    if n:
                        wait_job(dve, ("bB", (n - 1) // 2, (n - 1) % 2))
                    dve.tensor_tensor(tA[:, :], bank(key)[:, 0:HQ], sgA[:, n % 2, :], ALU.mult).then_inc(dve_drained, 1)
                    key = ("bB", m, x)
                    wait_full(dve, key)
                    wait_job(dve, ("gB", m, x))
                    link(dve.tensor_tensor(tB[:, :], bank(key)[:, 0:HQ], sgB[:, n % 2, :], ALU.mult))
                    dve.tensor_tensor(mixT[:, m, x * HQ:x * HQ + HQ], tA[:, :], tB[:, :], ALU.add)\
                       .then_inc(dve_drained, 1)
            dve.wait_ge(h_back, 16 * TILES)
            for x in range(2):
                for i in range(TILES):
                    r = ROWS[i]
                    key = ("mix", x, i)
                    wait_full(dve, key)
                    hv = h1[0:r, i, 512 * x:512 * x + 512]
                    dve.scalar_tensor_tensor(hv, hv, ALPHA, bank(key)[0:r, :], ALU.mult, ALU.add)\
                       .then_inc(dve_drained, 1)
            wait_job(dve, ("mix", 1, 4))
            layer_norm(1, h1, h1, ROWS, h1_ready)

            def v3(n, b):
                return R[n].rearrange("p (i b) -> p i b", b=b)

            def bc(n, b):
                return R[n].rearrange("p (i b) -> p i b", b=1).broadcast_to([P, TILES, b])

            def tab(n, b):
                return cst(n).rearrange("p (i b) -> p i b", i=1).broadcast_to([P, TILES, b])

            lg = v3("lg", 36)
            wait_full(dve, ("rt", 0))
            link(dve.memset(R["lg"], 0.0))
            for i in range(TILES):
                r = ROWS[i]
                key = ("rt", i)
                wait_full(dve, key)
                dve.tensor_tensor(lg[0:r, i, :], bank(key)[0:r, 0:36], vc("brout")[0:r, :], ALU.add)\
                   .then_inc(dve_drained, 1)
            wait_job(dve, ("rt", 4))

            def first_max(vals, w, mx, tmp, mn, oh, table):
                link(dve.tensor_reduce(R[mx], vals, AX.X, ALU.max))
                link(dve.tensor_tensor(v3(tmp, w), vals, bc(mx, w), ALU.is_equal))
                link(dve.tensor_tensor(v3(tmp, w), v3(tmp, w), tab(table, w), ALU.mult))
                link(dve.tensor_reduce(R[mn], v3(tmp, w), AX.X, ALU.min))
                link(dve.tensor_tensor(v3(oh, w), bc(mn, w), tab(table, w), ALU.is_equal))

            first_max(lg[:, :, 0:4], 4, "gmax", "gt", "gmin", "goh", "i4")
            link(dve.tensor_tensor(v3("eg", 4), lg[:, :, 0:4], bc("gmax", 4), ALU.subtract))
            for i in range(TILES):
                link(dve.tensor_tensor(R["pr"].rearrange("p (i g e) -> p i g e", g=4, e=8)[:, i],
                                       lg[:, i, 4:36].rearrange("p (g e) -> p g e", g=4),
                                       R["goh"].rearrange("p (i g e) -> p i g e", g=4, e=1)[:, i].broadcast_to([P, 4, 8]),
                                       ALU.mult))
                link(dve.tensor_reduce(v3("ein", 8)[:, i, :],
                                       R["pr"].rearrange("p (i g e) -> p i e g", g=4, e=8)[:, i], AX.X, ALU.add))
            first_max(v3("ein", 8), 8, "m1", "t8", "mn", "oh1", "i8")
            link(dve.scalar_tensor_tensor(R["ein"], R["oh1"], -1e30, R["ein"], ALU.mult, ALU.add))
            first_max(v3("ein", 8), 8, "m2", "t8", "mn", "oh2", "i8")
            dve.tensor_tensor(R["ex"], R["m2"], R["m1"], ALU.subtract).then_inc(rt_exp_in, 1)
            for n, oh in (("M1", "oh1"), ("M2", "oh2")):
                for i in range(TILES):
                    link(dve.tensor_tensor(R[n].rearrange("p (i g e) -> p i g e", g=4, e=8)[:, i],
                                           R["goh"].rearrange("p (i g e) -> p i g e", g=4, e=1)[:, i].broadcast_to([P, 4, 8]),
                                           R[oh].rearrange("p (i g e) -> p i g e", g=1, e=8)[:, i].broadcast_to([P, 4, 8]),
                                           ALU.mult))
            link(dve.tensor_tensor(R["M"], R["M1"], R["M2"], ALU.add))
            dve.tensor_tensor(v3("M", 32), v3("M", 32), cst("valid").rearrange("p (i b) -> p i b", b=1)
                              .broadcast_to([P, TILES, 32]), ALU.mult).then_inc(mask_ready, 1)
            dve.wait_ge(rt_exp, 1)
            link(dve.tensor_reduce(R["gsum"], v3("eg", 4), AX.X, ALU.add))
            link(dve.tensor_scalar(R["w1"], R["ex"], 1.0, None, ALU.add))
            link(dve.tensor_tensor(R["w1"], R["w1"], R["gsum"], ALU.mult))
            link(dve.reciprocal(R["w1"], R["w1"]))
            link(dve.tensor_tensor(R["w2"], R["w1"], R["ex"], ALU.mult))
            key = ("cnt",)
            wait_full(dve, key)
            dve.tensor_copy(R["cnt"], bank(key)[:, 0:32]).then_inc(dve_drained, 1)
            wait_job(dve, key)
            link(dve.memset(R["nt"], 0.0))
            for k in range(5):
                link(dve.scalar_tensor_tensor(R["nt"], R["cnt"], 128.0 * k, R["nt"], ALU.is_gt, ALU.add))
            link(dve.memset(R["one32"], 1.0))
            link(dve.tensor_tensor_scan(R["inc"], R["one32"], R["nt"], 0.0, ALU.mult, ALU.add))
            link(dve.tensor_scalar(R["cnt"], R["inc"], cst("pid"), None, ALU.is_le))
            link(dve.tensor_reduce(R["eg1"], R["cnt"], AX.X, ALU.add))
            dve.tensor_scalar(R["eg1"], R["eg1"], float(N_EXP - 1), None, ALU.min).then_inc(ids_ready, 1)
            key = ("lst",)
            wait_full(dve, ("pos",))
            dve.tensor_copy(R["pos"], bank(("pos",))[:, 0:160]).then_inc(dve_drained, 1)
            wait_full(dve, key)
            dve.tensor_copy(lst[0:1, 0:128], bank(key)[0:1, 0:128]).then_inc(dve_drained, 1)
            dve.tensor_copy(lst[0:1, 128:129], R["inc"][0:1, 31:32]).then_inc(list_ready, 1)
            link(dve.memset(R["q"], 0.0))
            for k in range(1, 5):
                link(dve.scalar_tensor_tensor(R["q"], R["pos"], 128.0 * k, R["q"], ALU.is_ge, ALU.add))
            link(dve.tensor_scalar(R["q"], R["q"], 1.0 - 128.0 * MAX_TILES, None, ALU.mult))
            link(dve.scalar_tensor_tensor(R["q"], R["pos"], float(MAX_TILES), R["q"], ALU.mult, ALU.add))
            link(dve.tensor_tensor(R["inc"], R["inc"], R["nt"], ALU.subtract))
            link(dve.tensor_tensor(v3("q", 32), v3("q", 32), R["inc"].rearrange("p (i b) -> p i b", i=1)
                                   .broadcast_to([P, TILES, 32]), ALU.add))
            for n, m in enumerate(("M1", "M2")):
                link(dve.tensor_tensor(R["t160"], R["q"], R[m], ALU.mult))
                link(dve.tensor_reduce(R["r1"][:, 5 * n:5 * n + 5], v3("t160", 32), AX.X, ALU.add))
            link(dve.tensor_copy(rowi[:, :], R["r1"]))
            link(dve.memset(ent[:, :, :], 0))
            for n in range(2):
                dve.tensor_copy(ent[:, 5 * n:5 * n + 5, 0], cst("tok"))
                link(dve.tensor_scalar(ent[:, 5 * n:5 * n + 5, 1], cst("tok"), float(TQ * n), None, ALU.add))
                link(dve.tensor_copy(ent[:, 5 * n:5 * n + 5, 2].bitcast(f32), R[f"w{n + 1}"]))
            dve.memset(R["q"], 0.0).then_inc(rows_ready, 1)

            dve.wait_ge(list_ready, 1)
            tiles = dve.value_load(lst[0:1, 128:129], min_val=1, max_val=MAX_TILES - 2)

            def drain_xt(g, s):
                dve.wait_ge(xt_full, g + 1 + 1)
                dve.tensor_copy(XT[:, s, 4:8, :], psum[1][:, :].rearrange("p (k c) -> p k c", k=4)).then_inc(xt_dve, 1)

            dve.wait_ge(tb_in, 16)
            drain_xt(0, 0)
            with dve.Fori(0, tiles, 2) as g0:
                for s in range(2):
                    g = g0 + s
                    dve.wait_ge(silu_done, g + 1)
                    dve.tensor_tensor(act_[:, s, :], psum[2 + s][:, F:2 * F], sil[:, s, :], ALU.mult).then_inc(act_done, 1)
                    drain_xt(g + 1, 1 - s)
                    dve.tensor_copy(wsel[:, s:s + 1], tb[:, bass.ds(g, 1), 2].bitcast(f32)).then_inc(w_ready, 1)
                    dve.wait_ge(dn_full, g + 3)
                    dve.wait_ge(w_ready, g + 1)
                    dve.wait_ge(y_sent[s], (g0 + 2) * 8)
                    dve.tensor_scalar(Yt[:, s, 512:1024], psum[6][:, :], wsel[:, s:s + 1], None, ALU.mult)\
                       .then_inc(dn_dve, 1)
            dve.wait_ge(y_back, 32 * TILES)
            for i in range(TILES):
                r = ROWS[i]
                link(dve.tensor_tensor(y0[0:r, i, :], y0[0:r, i, :], y1[0:r, i, :], ALU.add))
                link(dve.scalar_tensor_tensor(h1[0:r, i, :], h1[0:r, i, :], ALPHA, y0[0:r, i, :], ALU.mult, ALU.add))
            layer_norm(2, h1, h1, ROWS, y_ready)

        @block.tensor
        def _(pe):
            def open_bank(key):
                n = INDEX[key]
                if n >= NBANK:
                    wait_job(pe, ORDER[n - NBANK][0])
                return bank(key)

            def full(ins):
                ins.then_inc(psum_full, 1)

            def feature_job(key, w, cols, lo, n):
                bk = open_bank(key)
                m = cols.stop - cols.start
                for kc in range(KC):
                    ins = pe.matmul(bk[0:m, 0:n], w[:, kc, cols], hT[:, kc, lo:lo + n], start=(kc == 0),
                                    stop=(kc == KC - 1))
                full(ins)

            pe.wait_ge(const_in, 16 * 2)
            pe.wait_ge(wrt_in, 16 * 2)
            for i in range(TILES):
                r = ROWS_ALL[i]
                pe.wait_ge(h_ready, i + 1)
                for x in range(2):
                    bk = open_bank(("hT", i, x))
                    for k in range(4):
                        c = (4 * x + k) * P
                        ins = pe.transpose(bk[:, k * P:k * P + r], h[0:r, i, c:c + P], ident[0:r, 0:r])
                    full(ins)
            wait_job(pe, ("hT", 4, 0))
            wait_job(pe, ("hT", 4, 1))
            wait_chunk(pe, "q")
            w = chunk("q")
            for t in range(4):
                for x in range(2):
                    key = ("q", t, x)
                    bk = open_bank(key)
                    for kc in range(KC):
                        ins = pe.matmul(bk[:, 0:HQ], w[:, kc, t * P:t * P + P], hT[:, kc, x * HQ:x * HQ + HQ], start=(kc == 0),
                                        stop=(kc == KC - 1))
                    full(ins)
            wait_chunk(pe, "kv")
            w = chunk("kv")
            for x in range(2):
                feature_job(("k", x), w, slice(0, P), x * HA, HA)
            for i in range(TILES):
                r = ROWS_ALL[i]
                bk = open_bank(("v", i))
                for kc in range(KC):
                    ins = pe.matmul(bk[0:r, 0:P], hT[:, kc, i * P:i * P + r], w[:, kc, P:2 * P], start=(kc == 0),
                                    stop=(kc == KC - 1))
                full(ins)
            wait_chunk(pe, "ga")
            w = chunk("ga")
            for x in range(2):
                feature_job(("ga", x), w, slice(0, RANK), x * HA, HA)
            wait_job(pe, ("ga", 1))
            pe.wait_ge(w2_in, 16)
            for g in range(GH):
                for x in range(2):
                    bk = open_bank(("la", g, x))
                    full(pe.matmul(bk[:, 0:HA], w2[0:RANK, g * P:g * P + P], gaT[0:RANK, x * HA:x * HA + HA], start=True,
                                   stop=True))
            for n, wd_ in (("gq", HQ), ("gk", HA)):
                wait_chunk(pe, n)
                w = chunk(n)
                for g in range(GH):
                    for x in range(2):
                        feature_job((n, g, x), w, slice(g * P, g * P + P), x * wd_, wd_)
            for x in range(2):
                wait_chunk(pe, f"gv{x}")
                w = chunk(f"gv{x}")
                for i in range(TILES):
                    r = ROWS_ALL[i]
                    bk = open_bank(("gv", x, i))
                    for kc in range(KC):
                        ins = pe.matmul(bk[0:r, :], hT[:, kc, i * P:i * P + r], w[:, kc, :], start=(kc == 0),
                                        stop=(kc == KC - 1))
                    full(ins)
            wait_job(pe, ("k", 1))
            full(pe.transpose(open_bank(("ktok", 0))[:, 0:P], kT[:, 384:512], ident[:, :]))
            full(pe.transpose(open_bank(("ktok", 1))[0:NS, 0:P], kT[:, SEQ:TQ], ident[:, :]))
            pe.wait_ge(state_in, 32)
            for x in range(2):
                bk = open_bank(("kbT", x))
                for b in range(4):
                    ins = pe.transpose(bk[:, b * P:b * P + P], sbk[:, 4 * x + b, :], ident[:, :])
                full(ins)

            def scores(u):
                kind, a, b = UNITS[u]
                bk = open_bank(("s", u))
                if kind == "p":
                    rows = slice(HD * (b // 2), HD * (b // 2) + HD)
                    for x in range(2):
                        q = qT[rows, 2 * (b % 2) + x, a * P:a * P + P]
                        c = x * 256
                        if a:
                            ins = pe.matmul(bk[:, c:c + 256], q, kT[rows, (a - 1) * P:(a + 1) * P], start=True, stop=True)
                        else:
                            pe.matmul(bk[:, c + P - N_META:c + P], q, kT[rows, TQ:T], start=True, stop=True)
                            ins = pe.matmul(bk[:, c + P:c + 256], q, kT[rows, 0:P], start=True, stop=True)
                else:
                    for bb in range(4):
                        s = 4 * a + bb
                        q = qs[HD * b:HD * b + HD, s, :]
                        pe.matmul(bk[32 * bb:32 * bb + 32, 0:P], q, kbT[HD * b:HD * b + HD, s, :], start=True, stop=True)
                        ins = pe.matmul(bk[32 * bb:32 * bb + 32, P:P + T_S], q,
                                        kT[HD * b:HD * b + HD, SEQ + T_S * s:SEQ + T_S * s + T_S], start=True, stop=True)
                full(ins)

            def turn(u):
                kind, a, b = UNITS[u]
                pe.wait_ge(p_norm, u + 1)
                bk = open_bank(("pT", u))
                if kind == "p":
                    for kv in range(2):
                        c = kv * 256
                        if a:
                            pe.transpose(bk[:, c:c + P], S[:, u % 3, c:c + P], ident[:, :])
                        else:
                            pe.transpose(bk[0:N_META, c:c + P], S[:, u % 3, c + P - N_META:c + P], ident[:, :])
                        ins = pe.transpose(bk[:, c + P:c + 256], S[:, u % 3, c + P:c + 256], ident[:, :])
                else:
                    pe.transpose(bk[:, 0:P], S[:, u % 3, 0:P], ident[:, :])
                    ins = pe.transpose(bk[0:T_S, P:2 * P], S[:, u % 3, P:P + T_S], ident[:, :])
                full(ins)

            def values(u):
                kind, a, b = UNITS[u]
                wait_job(pe, ("pT", u))
                bk = open_bank(("o", u))
                kv = b // 2 if kind == "p" else b
                rows = bk[HD * kv:HD * kv + HD, :]
                cols = slice(HD * kv, HD * kv + HD)
                if kind == "p":
                    for x in range(2):
                        pt = PT[:, u % 3, x * 256:x * 256 + 256]
                        out = rows[:, x * P:x * P + P]
                        if a:
                            pe.matmul(out, v[:, a - 1, cols], pt[:, 0:P], start=True, stop=False)
                        else:
                            pe.matmul(out, vm[0:N_META, cols], pt[0:N_META, 0:P], start=True, stop=False)
                        ins = pe.matmul(out, v[:, a, cols], pt[:, P:2 * P], start=False, stop=True)
                else:
                    pt = PT[:, u % 3, :]
                    for bb in range(4):
                        s = 4 * a + bb
                        o = rows[:, 32 * bb:32 * bb + 32]
                        pe.matmul(o, sbv[:, s, cols], pt[:, 32 * bb:32 * bb + 32], start=True, stop=False)
                        ins = pe.matmul(o, vn[0:T_S, s, cols], pt[0:T_S, P + 32 * bb:P + 32 * bb + 32], start=False,
                                        stop=True)
                full(ins)

            wait_job(pe, ("kbT", 1))
            pe.wait_ge(rows_moved, 16 * 9)
            n = len(UNITS)
            for u in range(n + 3):
                if u < n:
                    scores(u)
                if 0 <= u - 2 < n:
                    turn(u - 2)
                if 0 <= u - 3 < n:
                    values(u - 3)

            for g in range(GH):
                b = g % 2
                wait_job(pe, ("gk", g, 1))
                bk = open_bank(("keT", g, 0))
                for i in range(4):
                    ins = pe.transpose(bk[:, i * P:i * P + P], gk[:, g, i * P:i * P + P], ident[:, :])
                full(ins)
                full(pe.transpose(open_bank(("keT", g, 1))[0:NS + N_META, 0:P], gk[:, g, SEQ:T], ident[:, :]))
                bk = open_bank(("att", g))
                for c in range(NCH):
                    r, i = 64 * (c % 2), c // 2
                    pe.matmul(bk[r:r + 64, 64 * i:64 * i + 64], gk[:, g, CH * c:CH * c + CH], gq[:, g, CH * c:CH * c + CH],
                              start=True, stop=True)
                full(pe.matmul(bk[0:NS, 256:320], gk[:, g, SEQ:TQ], gq[:, g, SEQ:TQ], start=True, stop=True))
                wait_job(pe, ("keT", g, 1))
                gcol = slice(g * HV, g * HV + HV)
                for c in range(-1, NCH):
                    bk = open_bank(("U", g, c))
                    if c < 0:
                        ins = pe.matmul(bk[:, 0:HV], kem[NS:NS + N_META, b, 4, :], gv[NS:NS + N_META, 4, gcol], start=True,
                                        stop=True)
                    else:
                        r = 64 * (c % 2)
                        ins = pe.matmul(bk[:, 0:HV], kem[r:r + 64, b, c // 2, :], gv[r:r + 64, c // 2, gcol], start=True,
                                        stop=True)
                    full(ins)
                pe.wait_ge(sp_final, g + 1)
                for i in range(4):
                    bk = open_bank(("go", g, i))
                    for c in (2 * i, 2 * i + 1):
                        r = 64 * (c % 2)
                        pe.matmul(bk[r:r + 64, 0:HV], am[r:r + 64, b, 64 * i:64 * i + 64], gv[r:r + 64, i, gcol],
                                  start=True, stop=False)
                        ins = pe.matmul(bk[r:r + 64, 0:HV], gq[:, g, CH * c:CH * c + CH], Sp[:, c, :], start=False,
                                        stop=True)
                    full(ins)
                pe.wait_ge(s0_in, 16 * (g + 1))
                pe.wait_ge(kes_ready, g + 1)
                bk = open_bank(("gso", g))
                pe.matmul(bk[0:NS, 0:HV], am[0:NS, b, 256:320], gv[0:NS, 4, gcol], start=True, stop=False)
                for s in range(8):
                    ins = pe.matmul(bk[0:NS, 0:HV], qz[:, 64 * s:64 * s + 64], s0[:, s, :], start=False, stop=(s == 7))
                full(ins)
                for x in range(4):
                    bk = open_bank(("sU", g, x))
                    for s in range(2):
                        ins = pe.matmul(bk[:, s * HV:s * HV + HV], kes[0:NS, 2 * x + s, :], gv[0:NS, 4, gcol], start=True,
                                        stop=True)
                    full(ins)

            for t in range(8):
                if t % 4 == 0:
                    wait_chunk(pe, f"gr{t // 4}")
                    w = chunk(f"gr{t // 4}")
                for x in range(2):
                    feature_job(("gr", t, x), w, slice(t % 4 * P, t % 4 * P + P), x * HQ, HQ)
            for i in range(TILES):
                r = ROWS[i]
                pe.wait_ge(y_norm, i + 1)
                for x in range(2):
                    bk = open_bank(("yT", i, x))
                    for k in range(4):
                        c = (4 * x + k) * P
                        ins = pe.transpose(bk[:, k * P:k * P + r], osb[0:r, i, c:c + P], ident[0:r, 0:r])
                    full(ins)
            wait_job(pe, ("yT", 4, 1))
            for m in range(8):
                y, c = m // 2, m % 2 * P
                if m % 2 == 0:
                    wait_chunk(pe, f"gates{y}")
                    wait_chunk(pe, f"branch{y}")
                for x in range(2):
                    feature_job(("gA", m, x), chunk(f"gates{y}"), slice(c, c + P), x * HQ, HQ)
                    feature_job(("gB", m, x), chunk(f"gates{y}"), slice(256 + c, 256 + c + P), x * HQ, HQ)
                    w = chunk(f"branch{y}")
                    for nme, src, k0, nk in (("a", yaT, 0, 4), ("b", ygT, 4, 8)):
                        key = ("b" + nme.upper(), m, x)
                        bk = open_bank(key)
                        for kc in range(nk):
                            ins = pe.matmul(bk[:, 0:HQ], w[:, k0 + kc, c:c + P], src[:, kc, x * HQ:x * HQ + HQ],
                                            start=(kc == 0), stop=(kc == nk - 1))
                        full(ins)
            wait_job(pe, ("bB", 7, 1))
            for x in range(2):
                wait_chunk(pe, f"wo{x}")
                w = chunk(f"wo{x}")
                for i in range(TILES):
                    r = ROWS[i]
                    bk = open_bank(("mix", x, i))
                    for kc in range(KC):
                        ins = pe.matmul(bk[0:r, :], mixT[:, kc, i * P:i * P + r], w[:, kc, :], start=(kc == 0),
                                        stop=(kc == KC - 1))
                    full(ins)
            for i in range(TILES):
                r = ROWS[i]
                pe.wait_ge(h1_ready, i + 1)
                for x in range(2):
                    bk = open_bank(("h1T", i, x))
                    for k in range(4):
                        c = (4 * x + k) * P
                        ins = pe.transpose(bk[:, k * P:k * P + r], h1[0:r, i, c:c + P], ident[0:r, 0:r])
                    full(ins)
                wait_job(pe, ("h1T", i, 1))
                bk = open_bank(("rt", i))
                for kc in range(KC):
                    ins = pe.matmul(bk[0:r, 0:36], h1T[:, kc, i * P:i * P + r], wrt[:, kc, :], start=(kc == 0),
                                    stop=(kc == KC - 1))
                full(ins)
            pe.wait_ge(mask_ready, 1)
            M = R["M"].rearrange("p (i e) -> p i e", e=32)
            bk = open_bank(("cnt",))
            for i in range(TILES):
                ins = pe.matmul(bk[:, 0:32], ones, M[:, i, :], start=(i == 0), stop=(i == TILES - 1))
            full(ins)
            bk = open_bank(("pos",))
            for i in range(TILES):
                for j in range(i + 1):
                    ins = pe.matmul(bk[:, 32 * i:32 * i + 32], tri if j == i else ones, M[:, j, :], start=(j == 0),
                                    stop=(j == i))
            full(ins)
            pe.wait_ge(ids_ready, 1)
            full(pe.matmul(open_bank(("lst",))[0:1, 0:128], R["eg1"], ident, start=True, stop=True))

            wait_job(pe, ("lst",))
            pe.wait_ge(list_ready, 1)
            tiles = pe.value_load(lst[0:1, 128:129], min_val=1, max_val=MAX_TILES - 2)
            pe.sem_inc(gu_full, 2)
            pe.sem_inc(dn_full, 2)
            pe.sem_inc(xt_full, 1)
            pe.sem_inc(dn_act, 1)
            pe.sem_inc(dn_dve, 1)

            def turn_x(g, s, n):
                pe.wait_ge(gathered[s], n)
                for k in range(KC):
                    ins = pe.transpose(psum[k // 4][:, k % 4 * P:k % 4 * P + P], Xg[:, s, k * P:k * P + P], ident)
                ins.then_inc(xt_full, 1)

            turn_x(0, 0, 16)
            with pe.Fori(0, tiles, 2) as g0:
                for s in range(2):
                    g = g0 + s
                    pe.wait_ge(xt_act, g + 1)
                    pe.wait_ge(xt_dve, g + 1)
                    pe.wait_ge(wg_in[s], (g0 + 2) * 16)
                    for kc in range(KC):
                        ins = pe.matmul(psum[2 + s][:, :], XT[:, s, kc, :], wgu[s][:, kc, :], start=(kc == 0),
                                        stop=(kc == KC - 1))
                    ins.then_inc(gu_full, 1)
                    turn_x(g + 1, 1 - s, (g0 + 2) * 8 + (16 if s else 0))
                    pe.wait_ge(act_done, g + 1)
                    for k in range(2):
                        ins = pe.transpose(psum[4][:, k * P:k * P + P], act_[:, s, k * P:k * P + P], ident)
                    ins.then_inc(at_full, 1)
                    pe.wait_ge(at_done, g + 1)
                    pe.wait_ge(wd_in[s], (g0 + 2) * 8)
                    pe.wait_ge(dn_act, g + 1)
                    pe.wait_ge(dn_dve, g + 1)
                    for half in range(2):
                        for k in range(2):
                            ins = pe.matmul(psum[5 + half][:, :], aT[:, s, k, :], wd[s][:, k, 512 * half:512 * half + 512],
                                            start=(k == 0), stop=(k == 1))
                    ins.then_inc(dn_full, 1)


def constants():
    import numpy as np

    c = np.zeros((P, CONST_W), np.float32)

    def put(n, a):
        o, w = CONST[n]
        c[:, o:o + w] = np.asarray(a, np.float32).reshape(a.shape[0], -1) if a.shape[0] == P else a

    p = np.arange(P)
    put("ident", np.eye(P))
    put("tri", (p[:, None] < p[None, :]) * 1.0)
    put("ones", np.ones((P, P)))
    scan = np.ones(T)
    scan[0:SEQ:CH] = 0
    scan[SEQ:TQ:T_S] = 0
    scan[TQ] = 0
    put("scan", np.tile(scan, (P, 1)))
    slope = 2.0 ** -np.arange(1, HEADS + 1)

    def alibi(dist, s):
        return np.where((dist >= 0) & (dist < WINDOW), -s * dist, -1e30)

    dist = p[:, None] + WINDOW - np.arange(256)[None, :]
    b = np.zeros((P, HEADS, 256))
    for n in range(HEADS):
        b[:, n] = alibi(dist, slope[n])
    put("bias", b)
    rows_t, rows_h = p % T_S, p // T_S % 4
    dist = rows_t[:, None] + WINDOW - np.arange(WINDOW + T_S)[None, :]
    b = np.zeros((P, 2, WINDOW + T_S))
    for kv in range(2):
        b[:, kv] = alibi(dist, slope[4 * kv + rows_h][:, None])
    put("sbias", b)
    t = np.arange(64)
    put("cmask", (p[:, None] % 64 <= t[None, :]) * 1.0)
    put("smask", ((p[:, None] // T_S == t[None, :] // T_S) & (p[:, None] <= t[None, :])) * 1.0)
    put("bmask", (p[:, None] // T_S == np.arange(8)[None, :]) * 1.0)
    put("i4", np.tile(np.arange(4) - 99.0, (P, 1)))
    put("i8", np.tile(np.arange(8) - 99.0, (P, 1)))
    tok = p[:, None] + P * np.arange(TILES)[None, :]
    put("valid", (tok < TQ) * 1.0)
    put("tok", tok)
    put("pid", p[:, None])
    return c


_INS = ["x_prompt", "x_sample", "state_swa_k", "state_swa_v", "state_gla", "meta_tokens", "ln_emb_g", "ln_emb_b", "w_in",
        "w_alpha2", "w_attn_br", "w_gla_br", "w_out", "ln1_g", "ln1_b", "w_router_group", "w_router_expert", "w_exp_gate",
        "w_exp_up", "w_exp_down", "ln2_g", "ln2_b"]
_OUTS = [(1, SEQ, D), (NB_S, T_S, D), (1, 1, WINDOW, N_KV, HD), (1, 1, WINDOW, N_KV, HD), (1, 1, GH, HK, HV),
         (1, NB_S, WINDOW, N_KV, HD), (1, NB_S, WINDOW, N_KV, HD), (1, NB_S, GH, HK, HV)]


def kernel(**inputs):
    import numpy as _np
    import concourse.bacc as _bacc
    from concourse import mybir as _mybir
    from concourse.bass_utils import run_bass_kernel_spmd as _run

    arrays = {n: _np.ascontiguousarray(inputs[n]) for n in _INS}
    arrays["const"] = constants()
    arrays["w_q"] = _np.ascontiguousarray(_np.asarray(inputs["w_in"])[0, :, 0:512].reshape(D, 2, 4, HD)
                                          .transpose(0, 2, 1, 3).reshape(D, 512))
    v = _np.zeros((P, VEC_W), _np.float32)

    def put(n, a):
        v[:, VEC[n][0]:VEC[n][0] + VEC[n][1]] = a

    sink = _np.asarray(inputs["attn_sink"])[0]
    put("sink", _np.broadcast_to(sink, (P, HEADS)))
    put("ssink", _np.tile(_np.repeat(sink.reshape(2, 4), T_S, axis=1), (1, 4)).T)
    put("balpha", _np.asarray(inputs["b_alpha"])[0].reshape(4, P).T)
    put("bgate", _np.asarray(inputs["b_gate"])[0].reshape(16, P).T)
    put("normg", _np.asarray(inputs["gla_norm_g"])[0].reshape(8, P).T)
    put("brout", _np.broadcast_to(_np.concatenate([_np.asarray(inputs["b_router_group"])[0],
                                                   _np.asarray(inputs["b_router_expert"])[0]]), (P, 36)))
    arrays["vec"] = v
    nc = _bacc.Bacc("TRN2", target_bir_lowering=False, num_devices=1)
    A = {n: nc.dram_tensor(f"in_{n}", a.shape, _mybir.dt.from_np(a.dtype), kind="ExternalInput").ap()
         for n, a in arrays.items()}
    O = [nc.dram_tensor(f"out_{i}", shape, _mybir.dt.float32, kind="ExternalOutput").ap()
         for i, shape in enumerate(_OUTS)]
    decoder_kernel(nc, A, O)
    r = _run(nc, [{f"in_{n}": a for n, a in arrays.items()}], core_ids=[0])
    return tuple(r.results[0][f"out_{i}"] for i in range(len(_OUTS)))
```

```python
import concourse.bass as bass
from concourse import mybir
from contextlib import ExitStack

P = 128
D = 1024
KC = D // P
SEQ, NB_S, T_S, N_META = 512, 8, 8, 16
NS = NB_S * T_S
TQ = SEQ + NS
T = TQ + N_META
TILES = 5
ROWS = [P, P, P, P, NS]
ROWS_ALL = [P, P, P, P, NS + N_META]
HQ = TQ // 2
HA = T // 2
HEADS, N_KV, HD, WINDOW = 8, 2, 64, 128
GH, HK, HV = 4, 128, 256
CH = 64
NCH = SEQ // CH
RANK = 16
N_EXP, N_GRP, EPG, F = 32, 4, 8, 256
EPS = 1e-5
ALPHA = 2.0 ** 0.25
C_Q, C_K, C_V, C_GQ, C_GK, C_GV, C_GA, C_GR, C_GATE = 0, 512, 640, 768, 1280, 1792, 2816, 2832, 3856
MAX_TILES = 44
PAD_ROW = 4096
NBANK = 8
RING = 3

CONST = {}
_at = 0
for _n, _w in (("ident", 128), ("tri", 128), ("ones", 128), ("scan", T), ("bias", 2048), ("sbias", 272),
               ("cmask", 64), ("smask", 64), ("bmask", 8), ("i4", 4), ("i8", 8), ("valid", 5), ("tok", 5), ("pid", 1), ("plow", 1), ("eid", 32), ("e31", 32), ("evens", 5)):
    CONST[_n] = (_at, _w)
    _at += _w
CONST_W = _at
VEC = {}
_at = 0
for _n, _w in (("sink", 8), ("ssink", 2), ("balpha", 4), ("bgate", 16), ("normg", 8), ("brout", 36), ("embg", 8), ("embb", 8)):
    VEC[_n] = (_at, _w)
    _at += _w
VEC_W = _at

UNITS = [("p", j, pair) for j in range(4) for pair in range(4)] + [("s", bg, kv) for bg in range(2) for kv in range(2)]


def job_order():
    o = []
    for i in range(TILES):
        o += [(("hT", i, 0), "A"), (("hT", i, 1), "V")]
    o += [(("q", t, x), "A") for t in range(4) for x in range(2)]
    o += [(("k", x), "A") for x in range(2)]
    o += [(("v", i), "V") for i in range(TILES)]
    o += [(("ga", x), "V") for x in range(2)]
    o += [(("la", g, x), "A") for g in range(GH) for x in range(2)]
    o += [(("gq", g, x), "V") for g in range(GH) for x in range(2)]
    o += [(("gk", g, x), "V") for g in range(GH) for x in range(2)]
    o += [(("gv", x, i), "V") for x in range(2) for i in range(TILES)]
    o += [(("ktok", 0), "V"), (("ktok", 1), "V")]
    o += [(("kbT", x), "A") for x in range(2)]
    n = len(UNITS)
    for u in range(n + 3):
        if u < n:
            o.append((("s", u), "V"))
        if 0 <= u - 2 < n:
            o.append((("pT", u - 2), "A"))
        if 0 <= u - 3 < n:
            o.append((("o", u - 3), "V"))
    for g in range(GH):
        o += [(("keT", g, 0), "A"), (("keT", g, 1), "A"), (("att", g), "V")]
        o += [(("U", g, c), "V") for c in range(-1, NCH)]
        o += [(("go", g, i), "A") for i in range(4)]
        o += [(("gso", g), "A")]
        o += [(("sU", g, x), "V") for x in range(4)]
    o += [(("gr", t, x), "A") for t in range(8) for x in range(2)]
    o += [(("yT", i, x), "V") for i in range(TILES) for x in range(2)]
    for m in range(8):
        for x in range(2):
            o += [(("gA", m, x), "A"), (("gB", m, x), "A"), (("bA", m, x), "V"), (("bB", m, x), "V")]
    for i in range(TILES + 1):
        if i < TILES:
            o += [(("mix", x, i), "V") for x in range(2)]
        if i:
            o += [(("h1T", i - 1, 0), "A"), (("h1T", i - 1, 1), "A"), (("rt", i - 1), "V")]
    o += [(("cnt",), "V"), (("pos",), "V"), (("lst",), "V")]
    return o


def weight_chunks():
    return ([("q", ("q", 3, 1)), ("kv", ("v", 4)), ("ga", ("ga", 1)), ("gq", ("gq", 3, 1)), ("gk", ("gk", 3, 1)),
             ("gv0", ("gv", 0, 4)), ("gv1", ("gv", 1, 4)), ("gr0", ("gr", 3, 1)), ("gr1", ("gr", 7, 1))]
            + [(f"{n}{y}", ("bB", 2 * y + 1, 1)) for y in range(4) for n in ("gates", "branch")]
            + [(f"wo{x}", ("mix", x, 4)) for x in range(2)])


def layout():
    at = {}
    top = 0
    for n, w in (("const", CONST_W), ("vec", VEC_W), ("lng", D), ("lnb", D), ("wrt", KC * 36), ("small", 256),
                 ("ring", RING * KC * 512), ("hT", KC * T), ("gq", GH * TQ), ("gk", GH * T), ("gv", TILES * D),
                 ("yaT", 4 * TQ), ("osb", TILES * D), ("R", 11200)):
        at[n] = top
        top += -(-w * 4 // 32) * 32
    at["end"] = top

    def inside(base, items):
        x = at[base]
        for n, w in items:
            at[n] = x
            x += -(-w * 4 // 32) * 32
        return x

    e1 = inside("R", [("qT", 4 * SEQ), ("qs", 4 * NS), ("kT", T), ("v", TILES * P), ("vm", P), ("vn", 8 * P), ("ktok", 2 * P), ("X", 0)])
    assert inside("X", [("dx", 2 * T), ("dt", 2 * T), ("den", 2 * T)]) <= top
    assert inside("X", [("S", 3 * 512), ("PT", 3 * 512), ("sbk", 8 * P), ("sbv", 8 * P), ("kbT", 8 * P), ("stat", 3 * 16)]) <= top
    assert inside("R", [("kem", 2 * 5 * P), ("am", 2 * 5 * 64), ("Sp", 9 * 256), ("s0", 8 * 256), ("kes", 8 * P),
                        ("qz", 576), ("junk", 256)]) <= top, "gla"
    assert inside("R", [("sgA", 2 * HQ), ("sgB", 2 * HQ), ("tA", HQ), ("tB", HQ)]) <= top
    assert inside("R", [("h1", TILES * D), ("h1T", 8 * TQ)]) <= top
    at["gaT"] = at["yaT"]
    inside("yaT", [("rs", 4 * TQ)])
    assert inside("hT", [("wgu0", KC * 512), ("wd0", 2048), ("wgu1", KC * 512), ("wd1", 2048)]) <= at["yaT"]
    assert inside("ring", [("Xg", 2 * D), ("XT", 2 * D), ("Yt", 2 * D), ("sil", 2 * F), ("act", 2 * F), ("aT", 2 * F)]) <= at["hT"]
    inside("hT", [("y0", TILES * D)])
    inside("osb", [("y1", TILES * D)])
    return at


def decoder_kernel(nc, A, O):
    f32, i32 = mybir.dt.float32, mybir.dt.int32
    ALU, ACT, AX = mybir.AluOpType, mybir.ActivationFunctionType, mybir.AxisListType
    ORDER = job_order()
    INDEX = {k: n for n, (k, _) in enumerate(ORDER)}
    DRAINER = dict(ORDER)
    DRAINS = {}
    for eng in "AV":
        for n, k in enumerate([k for k, e in ORDER if e == eng]):
            DRAINS[k] = n + 1
    LAST_USE = weight_chunks()
    CHUNKS = [n for n, _ in LAST_USE]
    AT = layout()
    ctx = ExitStack()
    with ctx:
        arena = ctx.enter_context(nc.sbuf_tensor("arena", [P, AT["end"] // 4], f32))

        def sb(name, shape, dt=f32):
            n = 1
            for x in shape[1:]:
                n *= x
            o = AT[name] // 4
            ap = arena[:, o:o + n]
            if dt != f32:
                ap = ap.bitcast(dt)
            if len(shape) == 3:
                ap = ap.rearrange("p (a b) -> p a b", b=shape[2])
            if len(shape) == 4:
                ap = ap.rearrange("p (a b c) -> p a b c", b=shape[2], c=shape[3])
            return ap

        def sem(name):
            return ctx.enter_context(nc.semaphore(name))

        const = sb("const", [P, CONST_W])
        vec = sb("vec", [P, VEC_W])

        def cst(n):
            return const[:, CONST[n][0]:CONST[n][0] + CONST[n][1]]

        def vc(n):
            return vec[:, VEC[n][0]:VEC[n][0] + VEC[n][1]]

        ident, tri, ones = cst("ident"), cst("tri"), cst("ones")
        bias = cst("bias").rearrange("p (h k c) -> p h k c", h=4, k=2)
        sbias = cst("sbias").rearrange("p (k c) -> p k c", k=2)
        lng, lnb = sb("lng", [P, D]), sb("lnb", [P, D])
        wrt = sb("wrt", [P, KC, 36])
        small = sb("small", [P, 256])
        ring = sb("ring", [P, RING, KC * 512])
        hT = sb("hT", [P, KC, T])
        gq, gk = sb("gq", [P, GH, TQ]), sb("gk", [P, GH, T])
        sg = sb("gq", [P, 8, TQ])
        gv, ygT = sb("gv", [P, TILES, D]), sb("gv", [P, 8, TQ])
        h, osb, mixT = sb("osb", [P, TILES, D]), sb("osb", [P, TILES, D]), sb("osb", [P, 8, TQ])
        h1T = sb("h1T", [P, 8, TQ])
        yaT = sb("yaT", [P, 4, TQ])
        qs = sb("qs", [P, NB_S, 4 * T_S])
        qT, kT, v, vm = sb("qT", [P, 4, SEQ]), sb("kT", [P, T]), sb("v", [P, TILES, P]), sb("vm", [P, P])
        vn, ktok = sb("vn", [P, 8, P]), sb("ktok", [P, 2, P])
        gaT = sb("gaT", [P, T])
        dx, dt_, den = sb("dx", [P, 2, T]), sb("dt", [P, 2, T]), sb("den", [P, 2, T])
        S, PT = sb("S", [P, 3, 512]), sb("PT", [P, 3, 4 * P])
        sbk, sbv, kbT = sb("sbk", [P, 8, P]), sb("sbv", [P, 8, P]), sb("kbT", [P, 8, P])
        stat = sb("stat", [P, 3, 16])
        kem, am = sb("kem", [P, 2, 5, P]), sb("am", [P, 2, 5 * 64])
        Sp, s0, kes = sb("Sp", [P, 9, 256]), sb("s0", [P, 8, 256]), sb("kes", [P, 8, P])
        qz, junk = sb("qz", [P, 576]), sb("junk", [P, 256])
        sgA, sgB, tA, tB = sb("sgA", [P, 2, HQ]), sb("sgB", [P, 2, HQ]), sb("tA", [P, HQ]), sb("tB", [P, HQ])
        h1 = sb("h1", [P, TILES, D])
        fin, em = small[:, 0:68].rearrange("p (g c) -> p g c", c=17), small[:, 68:104].rearrange("p (g c) -> p g c", c=9)
        ss, rr = small[:, 104:124], small[:, 124:144]
        bst = small[:, 144:144 + 60].rearrange("p (i c) -> p i c", c=12)
        mv = small[:, 204:214].rearrange("p (i c) -> p i c", c=2)
        rstd = small[:, 214:224]
        epsc = small[:, 224:225]
        wgu = [sb("wgu0", [P, KC, 512]), sb("wgu1", [P, KC, 512])]
        wd = [sb("wd0", [P, 2, D]), sb("wd1", [P, 2, D])]
        Xg, XT, Yt = sb("Xg", [P, 2, D]), sb("XT", [P, 2, KC, P]), sb("Yt", [P, 2, D])
        sil, act_, aT = sb("sil", [P, 2, F]), sb("act", [P, 2, F]), sb("aT", [P, 2, 2, P])
        tb = ctx.enter_context(nc.sbuf_tensor("tb", [P, MAX_TILES, 4], i32))
        w2 = ctx.enter_context(nc.sbuf_tensor("w2", [RANK, GH * HK], f32))
        y0, y1 = sb("y0", [P, TILES, D]), sb("y1", [P, TILES, D])
        lst = ctx.enter_context(nc.sbuf_tensor("lst", [1, 132], i32))
        idx = ctx.enter_context(nc.sbuf_tensor("idx", [P, 4, 4], i32))
        wsel = ctx.enter_context(nc.sbuf_tensor("wsel", [P, 2], f32))
        ent = ctx.enter_context(nc.sbuf_tensor("ent", [P, 2 * TILES, 4], i32))
        rowi = ctx.enter_context(nc.sbuf_tensor("rowi", [P, 2 * TILES], i32))

        rs_off = [0]
        rs_base = sb("rs", [P, 4 * TQ])

        def scratch(n):
            o = rs_off[0]
            rs_off[0] += n
            assert rs_off[0] <= 4 * TQ
            return rs_base[:, o:o + n]

        R = {}
        for n, w in (("lg", 5 * 36), ("gmax", 5), ("gt", 20), ("gmin", 5), ("goh", 20), ("eg", 20), ("gsum", 5),
                     ("pr", 160), ("ein", 40), ("m1", 5), ("t8", 40), ("mn", 5), ("oh1", 40), ("oh2", 40), ("m2", 5),
                     ("ex", 5), ("w1", 5), ("w2", 5), ("M1", 160), ("M2", 160), ("M", 160), ("cnt", 32), ("nt", 32),
                     ("inc", 32), ("pos", 160), ("q", 160), ("t160", 160), ("r1", 10), ("eg1", 1), ("t5", 5)):
            R[n] = scratch(w)

        psum = [ctx.enter_context(nc.psum_tensor(f"bank{n}", [P, 512], f32)) for n in range(NBANK)]

        def bank(key):
            return psum[INDEX[key] % NBANK]

        tbl_d = nc.dram_tensor("slot_table", [P * MAX_TILES, 4], i32, kind="Internal").ap()
        h_d = nc.dram_tensor("h_spill", [TILES * P, D], f32, kind="Internal").ap()
        h1_d = nc.dram_tensor("h1_rows", [TQ, D], f32, kind="Internal").ap()
        y_d = nc.dram_tensor("expert_rows", [2 * TQ, D], f32, kind="Internal").ap()

        w2_in = sem("w2_in")
        h_scaled = sem("h_scaled")
        xn_ready = sem("xn_ready")
        y_part = sem("y_part")
        y_sum = sem("y_sum")
        y_sq = sem("y_sq")
        y_scale = sem("y_scale")
        y_xn = sem("y_xn")
        y_g = sem("y_g")
        h1_scaled = sem("h1_scaled")
        wrt_in = sem("wrt_in")
        pool_held = sem("pool_held")
        x_in = sem("x_in")
        const_in = sem("const_in")
        tables_in = sem("tables_in")
        ln_in = sem("ln_in")
        wchunk = [sem(f"wchunk{n}") for n in range(RING)]
        psum_full = sem("psum_full")
        act_drained = sem("act_drained")
        dve_drained = sem("dve_drained")
        dve_chain = sem("dve_chain")
        act_chain = sem("act_chain")
        ln_var = sem("ln_var")
        ln_std = sem("ln_std")
        h_ready = sem("h_ready")
        spilled = sem("spilled")
        h_back = sem("h_back")
        log_ready = sem("log_ready")
        dec_ready = sem("dec_ready")
        exp_ready = sem("exp_ready")
        qk_ready = sem("qk_ready")
        state_in = sem("state_in")
        rows_moved = sem("rows_moved")
        max_ready = sem("max_ready")
        p_exp = sem("p_exp")
        p_norm = sem("p_norm")
        s0_in = sem("s0_in")
        s0_out = sem("s0_out")
        sp_out = sem("sp_out")
        kes_ready = sem("kes_ready")
        att_used = sem("att_used")
        ss_ready = sem("ss_ready")
        rms_ready = sem("rms_ready")
        sp_final = sem("sp_final")
        s0_final = sem("s0_final")
        silu_ready = sem("silu_ready")
        y_norm = sem("y_norm")
        h1_ready = sem("h1_ready")
        h1_stored = sem("h1_stored")
        tbl_init = sem("tbl_init")
        pad_ready = sem("pad_ready")
        rt_exp_in = sem("rt_exp_in")
        rt_exp = sem("rt_exp")
        mask_ready = sem("mask_ready")
        ids_ready = sem("ids_ready")
        rows_ready = sem("rows_ready")
        list_ready = sem("list_ready")
        scattered = sem("scattered")
        tb_in = sem("tb_in")
        wg_in = [sem(f"wg_in{n}") for n in range(2)]
        wd_in = [sem(f"wd_in{n}") for n in range(2)]
        gathered = [sem(f"gathered{n}") for n in range(2)]
        y_sent = [sem(f"y_sent{n}") for n in range(2)]
        gidx_ready, sidx_ready = sem("gidx_ready"), sem("sidx_ready")
        xt_full, gu_full, at_full, dn_full = sem("xt_full"), sem("gu_full"), sem("at_full"), sem("dn_full")
        xt_act, xt_dve = sem("xt_act"), sem("xt_dve")
        silu_done, act_done, at_done = sem("silu_done"), sem("act_done"), sem("at_done")
        w_ready = sem("w_ready")
        dn_act, dn_dve = sem("dn_act"), sem("dn_dve")
        y_back = [sem(f"y_back{i}") for i in range(TILES)]
        y_out = sem("y_out")
        out_done = sem("out_done")
        y_ready = sem("y_ready")
        loop_done = sem("loop_done")
        x_zero = sem("x_zero")
        OUTS = [0]

        block = ctx.enter_context(nc.Block())

        def wait_job(eng, key):
            eng.wait_ge(act_drained if DRAINER[key] == "A" else dve_drained, DRAINS[key])

        def wait_full(eng, key):
            eng.wait_ge(psum_full, INDEX[key] + 1)

        def chunk_parts(n):
            slot = ring[:, CHUNKS.index(n) % RING, :]
            w_in = A["w_in"][0].rearrange("(k p) n -> p k n", p=P)
            if n == "q":
                place = slot.rearrange("p (k n) -> p k n", n=512)
                return place, [(place, A["w_q"].rearrange("(k p) n -> p k n", p=P))]
            cols = {"kv": (C_K, 256), "ga": (C_GA, 16), "gq": (C_GQ, 512), "gk": (C_GK, 512),
                    "gv0": (C_GV, 512), "gv1": (C_GV + 512, 512), "gr0": (C_GR, 512), "gr1": (C_GR + 512, 512)}
            if n in cols:
                c, m = cols[n]
                place = slot[:, 0:KC * m].rearrange("p (k n) -> p k n", n=m)
                return place, [(place, w_in[:, :, c:c + m])]
            y = int(n[-1])
            if n[:2] == "wo":
                place = slot.rearrange("p (k n) -> p k n", n=512)
                return place, [(place, A["w_out"][0].rearrange("(k p) n -> p k n", p=P)[:, :, 512 * y:512 * y + 512])]
            x = 256 * y
            if n[:5] == "gates":
                place = slot.rearrange("p (k n) -> p k n", n=512)
                return place, [(place[:, :, 256 * i:256 * i + 256], w_in[:, :, C_GATE + D * i + x:C_GATE + D * i + x + 256])
                               for i in range(2)]
            place = slot[:, 0:12 * 256].rearrange("p (k n) -> p k n", n=256)
            wa = A["w_attn_br"][0].rearrange("(v t p) n -> v p t n", v=2, p=HD)
            wb = A["w_gla_br"][0].rearrange("(k p) n -> p k n", p=P)
            return place, [(place[HD * kv:HD * kv + HD, 0:4, :], wa[kv][:, :, x:x + 256]) for kv in range(2)] \
                + [(place[:, 4:12, :], wb[:, :, x:x + 256])]

        def chunk(n):
            return chunk_parts(n)[0]

        def wait_chunk(eng, n):
            c = CHUNKS.index(n)
            total = sum(len(chunk_parts(m)[1]) for k, m in enumerate(CHUNKS[:c + 1]) if k % RING == c % RING)
            eng.wait_ge(wchunk[c % RING], 16 * total)

        @block.sync
        def _(sp):
            for c, n in enumerate(CHUNKS):
                if c == 1:
                    sp.wait_ge(x_in, 16 * 6)
                if c >= RING:
                    wait_full(sp, LAST_USE[c - RING][1])
                for place, src in chunk_parts(n)[1]:
                    sp.dma_start(place, src).then_inc(wchunk[c % RING], 16)

            def gate_up_in(e, s):
                for half, w in enumerate(("w_exp_gate", "w_exp_up")):
                    sp.dma_start(wgu[s][:, :, half * F:half * F + F],
                                 A[w][0][e, :, :].rearrange("e (p k) f -> p (e k) f", p=P)).then_inc(wg_in[s], 16)

            def down_in(e, s):
                sp.dma_start(wd[s][:, :, :], A["w_exp_down"][0][e, :, :].rearrange("e (p k) n -> p (e k) n", p=P))\
                  .then_inc(wd_in[s], 16)

            def expert_of(g):
                return bass.ds(sp.value_load(lst[0:1, bass.ds(g, 1)], min_val=0, max_val=N_EXP - 1), 1)

            def step(g, s, more):
                here, after = expert_of(g), expert_of(g + 1)
                if more:
                    sp.wait_ge(gu_full, g)
                    gate_up_in(after, 1 - s)
                sp.wait_ge(dn_full, g)
                down_in(here, s)

            wait_full(sp, ("bB", 7, 1))
            for s in range(2):
                gate_up_in(slice(s, s + 1), s)
                down_in(slice(s, s + 1), s)
            sp.wait_ge(gu_full, 1)
            gate_up_in(slice(2, 3), 0)
            sp.wait_ge(list_ready, 1)
            last = sp.value_load(lst[0:1, 128:129], min_val=N_EXP - 2, max_val=MAX_TILES - 4)
            with sp.Fori(2, last, 2) as g0:
                for s in range(2):
                    step(g0 + s, s, True)
            step(last, 0, True)
            step(last + 1, 1, False)
            sp.wait_ge(loop_done, 1)
            for i in range(TILES):
                r = ROWS[i]
                sp.dma_start(y0[0:r, i, :], y_d[i * P:i * P + r, :]).then_inc(y_back[i], 16)
                sp.dma_start(y1[0:r, i, :], y_d[TQ + i * P:TQ + i * P + r, :]).then_inc(y_back[i], 16)
            for i in range(TILES):
                sp.wait_ge(y_ready, i + 1)
                dst = O[0][0, i * P:i * P + P, :] if i < 4 else O[1].rearrange("b t d -> (b t) d")
                sp.dma_start(dst, h1[0:ROWS[i], i, :]).then_inc(y_out, 16)
            sp.wait_ge(y_out, 16 * TILES)

        def earlier(b):
            return b * 8

        def finish_rows(pool, i):
            r = ROWS[i]
            pool.wait_ge(y_g, i + 1)
            pool.tensor_tensor(h1[0:r, i, :], h1[0:r, i, :], lnb[0:r, :], ALU.add).then_inc(y_ready, 1)

        @block.gpsimd
        def _(pool):
            pool.memset(tb[:, :, :], PAD_ROW).then_inc(pad_ready, 1)
            pool.wait_ge(x_in, 16 * 6)
            pool.dma_start(w2[:, :], A["w_alpha2"][0]).then_inc(w2_in, 16)
            pool.dma_start(lng, A["ln_emb_g"].partition_broadcast(P)).then_inc(ln_in, 16)
            pool.dma_start(lnb, A["ln_emb_b"].partition_broadcast(P)).then_inc(ln_in, 16)
            pool.wait_ge(ln_in, 32)
            for i in range(TILES):
                r = ROWS[i]
                wait_full(pool, ("hT", i, 1))
                pool.tensor_tensor(h[0:r, i, :], h[0:r, i, :], lng[0:r, :], ALU.mult).then_inc(h_scaled, 1)
                pool.wait_ge(h_scaled, 2 * i + 1)
                pool.tensor_tensor(h[0:r, i, :], h[0:r, i, :], lnb[0:r, :], ALU.add).then_inc(h_scaled, 1)
                pool.wait_ge(h_scaled, 2 * i + 2)
                pool.dma_start(h_d[i * P:i * P + r, :], h[0:r, i, :]).then_inc(spilled, 16)
            pool.wait_ge(pad_ready, 1)
            pool.dma_start(tbl_d.rearrange("(p g) c -> p g c", p=P), tb[:, :, :]).then_inc(tbl_init, 16)
            pool.dma_start(wrt[:, :, 0:4], A["w_router_group"][0].rearrange("(k p) n -> p k n", p=P)).then_inc(wrt_in, 16)
            pool.dma_start(wrt[:, :, 4:36], A["w_router_expert"][0].rearrange("(k p) n -> p k n", p=P)).then_inc(wrt_in, 16)
            for b in range(2):
                k, vv = (("state_swa_k", 5), ("state_swa_v", 6))[b]
                s_in = A[k][0]
                pool.dma_start(O[vv][0][:, 0:WINDOW - T_S], s_in[:, T_S:WINDOW]).then_inc(out_done, 16)
                OUTS[0] += 1
            wait_job(pool, ("v", 4))
            pool.dma_start(vm[0:N_META, :], v[NS:NS + N_META, 4, :]).then_inc(rows_moved, 16)
            for b in range(8):
                pool.dma_start(vn[0:T_S, b, :], v[b * T_S:b * T_S + T_S, 4, :]).then_inc(rows_moved, 16)
            wait_job(pool, ("v", 3))
            pool.dma_start(O[3][0, 0].rearrange("t k d -> t (k d)"), v[:, 3, :]).then_inc(out_done, 16)
            pool.dma_start(O[6][0][:, WINDOW - T_S:WINDOW].rearrange("b t k d -> b t (k d)"), v[0:NS, 4, :])\
                .then_inc(out_done, 16)
            pool.wait_ge(qk_ready, GH)
            pool.dma_start(sbk[:, :, :], A["state_swa_k"][0].rearrange("b s k d -> s b (k d)")).then_inc(state_in, 16)
            pool.dma_start(sbv[:, :, :], A["state_swa_v"][0].rearrange("b s k d -> s b (k d)")).then_inc(state_in, 16)
            wait_job(pool, ("ktok", 1))
            pool.dma_start(O[2][0, 0].rearrange("t k d -> t (k d)"), ktok[:, 0, :]).then_inc(out_done, 16)
            pool.dma_start(O[5][0][:, WINDOW - T_S:WINDOW].rearrange("b t k d -> b t (k d)"), ktok[0:NS, 1, :])\
                .then_inc(out_done, 16)
            OUTS[0] += 4
            wait_job(pool, ("o", 19))
            pool.wait_ge(out_done, 16 * OUTS[0])
            for g in range(GH):
                if g:
                    pool.wait_ge(s0_out, 16 * g)
                pool.dma_start(s0[:, :, :], A["state_gla"][0][:, g].rearrange("b k v -> k b v")).then_inc(s0_in, 16)
                pool.wait_ge(sp_final, g + 1)
                pool.dma_start(O[4][0, 0, g], Sp[:, 8, :]).then_inc(sp_out, 16)
                pool.wait_ge(s0_final, g + 1)
                pool.dma_start(O[7][0][:, g].rearrange("b k v -> k b v"), s0[:, :, :]).then_inc(s0_out, 16)
            pool.dma_start(lng, A["ln1_g"][0].partition_broadcast(P)).then_inc(ln_in, 16)
            pool.dma_start(lnb, A["ln1_b"][0].partition_broadcast(P)).then_inc(ln_in, 16)
            wait_job(pool, ("bB", 7, 1))
            for i in range(TILES):
                pool.dma_start(h1[0:ROWS[i], i, :], h_d[i * P:i * P + ROWS[i], :]).then_inc(h_back, 16)
            for i in range(TILES):
                pool.wait_ge(h1_ready, i + 1)
                pool.dma_start(h1_d[i * P:i * P + ROWS[i], :], h1[0:ROWS[i], i, :]).then_inc(h1_stored, 16)
            pool.dma_start(lng, A["ln2_g"][0].partition_broadcast(P)).then_inc(ln_in, 16)
            pool.dma_start(lnb, A["ln2_b"][0].partition_broadcast(P)).then_inc(ln_in, 16)
            pool.wait_ge(tbl_init, 16)
            pool.wait_ge(rows_ready, 1)
            for n in range(2 * TILES):
                r = ROWS[n % TILES]
                pool.indirect_dma_start(out=tbl_d[:, :], out_offset=bass.IndirectOffsetOnAxis(ap=rowi[0:r, n:n + 1], axis=0),
                                        in_=ent[0:r, n, :], in_offset=None).then_inc(scattered, 16)
            pool.wait_ge(scattered, 16 * 2 * TILES)
            pool.dma_start(tb[:, :, :], tbl_d.rearrange("(p g) c -> p g c", p=P)).then_inc(tb_in, 16)
            pool.wait_ge(tb_in, 16)
            pool.wait_ge(h1_stored, 16 * TILES)
            pool.memset(Xg[:, :, :], 0.0).then_inc(x_zero, 1)
            pool.wait_ge(x_zero, 1)

            pool.memset(idx[:, :, :], PAD_ROW).then_inc(x_zero, 1)
            pool.memset(Yt[:, :, :], 0.0).then_inc(x_zero, 1)
            pool.wait_ge(x_zero, 3)
            for s in range(2):
                pool.indirect_dma_start(out=y_d[:, :], out_offset=bass.IndirectOffsetOnAxis(ap=idx[:, 2 + s, 1:2], axis=0),
                                        in_=Yt[:, s, :], in_offset=None,
                                        bounds_check=2 * TQ - 1, oob_is_err=False).then_inc(y_sent[s], 16)

            def hold():
                pool.sem_inc(pool_held, 1)

            def gather(g, s):
                pool.tensor_copy(idx[:, s:s + 1, :], tb[:, bass.ds(g, 1), :]).then_inc(gidx_ready, 1)
                pool.wait_ge(gidx_ready, g + 1)
                hold()
                pool.indirect_dma_start(out=Xg[:, s, :], out_offset=None, in_=h1_d[:, :],
                                        in_offset=bass.IndirectOffsetOnAxis(ap=idx[:, s, 0:1], axis=0),
                                        bounds_check=TQ - 1, oob_is_err=False).then_inc(gathered[s], 16)

            def send(b, s):
                g = b + s
                pool.wait_ge(y_sent[s], earlier(b) + 16)
                hold()
                pool.tensor_copy(idx[:, 2 + s:3 + s, :], tb[:, bass.ds(g, 1), :]).then_inc(sidx_ready, 1)
                pool.wait_ge(sidx_ready, g + 1)
                pool.wait_ge(dn_act, g + 2)
                pool.wait_ge(dn_dve, g + 2)
                hold()
                pool.indirect_dma_start(out=y_d[:, :], out_offset=bass.IndirectOffsetOnAxis(ap=idx[:, 2 + s, 1:2], axis=0),
                                        in_=Yt[:, s, :], in_offset=None,
                                        bounds_check=2 * TQ - 1, oob_is_err=False).then_inc(y_sent[s], 16)

            gather(0, 0)
            gather(1, 1)
            pool.wait_ge(xt_full, 1)
            gather(2, 0)
            last = pool.value_load(lst[0:1, 128:129], min_val=N_EXP - 2, max_val=MAX_TILES - 4)
            with pool.Fori(0, last, 2) as g0:
                for s in range(2):
                    pool.wait_ge(xt_full, g0 + s + 2)
                    hold()
                    gather(g0 + s + 3, 1 - s)
                    send(g0, s)
            for s in range(2):
                send(last, s)
            pool.wait_ge(gathered[0], earlier(last) + 32)
            hold()
            for s in range(2):
                pool.wait_ge(y_sent[s], earlier(last) + 32)
                hold()
            pool.sem_inc(loop_done, 1)
            for i in range(TILES):
                r = ROWS[i]
                pool.wait_ge(y_back[i], 32)
                pool.tensor_tensor(y0[0:r, i, :], y0[0:r, i, :], y1[0:r, i, :], ALU.add).then_inc(y_part, 1)
            for i in range(TILES):
                finish_rows(pool, i)
            pool.wait_ge(out_done, 16 * OUTS[0])
            pool.wait_ge(sp_out, 16 * GH)
            pool.wait_ge(s0_out, 16 * GH)

        @block.scalar
        def _(act):
            chain = [0]

            def link(ins):
                chain[0] += 1
                ins.then_inc(act_chain, 1)
                act.wait_ge(act_chain, chain[0])

            for i in range(TILES):
                if i < 4:
                    act.dma_start(h[:, i, :], A["x_prompt"][0, i * P:i * P + P, :]).then_inc(x_in, 16)
                else:
                    act.dma_start(h[0:NS, i, :], A["x_sample"].rearrange("b t d -> (b t) d")).then_inc(x_in, 16)
                    act.dma_start(h[NS:NS + N_META, i, :], A["meta_tokens"]).then_inc(x_in, 16)
            act.dma_start(const[:, 0:384], A["const"][:, 0:384]).then_inc(const_in, 16)
            act.dma_start(vec, A["vec"]).then_inc(const_in, 16)
            act.wait_ge(x_in, 16 * 6)
            act.dma_start(const[:, 384:CONST_W], A["const"][:, 384:CONST_W]).then_inc(tables_in, 16)

            def drain(key, out, in_, **kw):
                func = kw.pop("func", ACT.Copy)
                wait_full(act, key)
                act.activation(out, in_, func, **kw).then_inc(act_drained, 1)

            def std(n, i):
                act.wait_ge(ln_var, TILES * n + i + 1)
                act.activation(rstd[:, 5 + i:6 + i], rstd[:, i:i + 1], ACT.Sqrt).then_inc(ln_std, 1)

            for i in range(TILES):
                std(0, i)
            act.wait_ge(const_in, 16 * 2)
            for i in range(TILES):
                r = ROWS_ALL[i]
                wait_full(act, ("hT", i, 0))
                for k in range(4):
                    ins = act.activation(hT[:, k, i * P:i * P + r], bank(("hT", i, 0))[:, k * P:k * P + r], ACT.Identity,
                                         scale=vc("embg")[:, k:k + 1], bias=vc("embb")[:, k:k + 1])
                ins.then_inc(act_drained, 1)
            act.wait_ge(tables_in, 16)
            for t in range(4):
                drain(("q", t, 0), qT[:, t, 0:HQ], bank(("q", t, 0))[:, 0:HQ], scale=HD ** -0.5)
                wait_full(act, ("q", t, 1))
                act.activation(qT[:, t, HQ:SEQ], bank(("q", t, 1))[:, 0:SEQ - HQ], ACT.Copy, scale=HD ** -0.5)
                act.activation(qs[:, :, t * T_S:t * T_S + T_S],
                               bank(("q", t, 1))[:, SEQ - HQ:HQ].rearrange("p (b t) -> p b t", t=T_S), ACT.Copy,
                               scale=HD ** -0.5).then_inc(act_drained, 1)
            for x in range(2):
                drain(("k", x), kT[:, x * HA:x * HA + HA], bank(("k", x))[:, 0:HA])

            def exps(g):
                b = g % 2
                act.wait_ge(dec_ready, g + 1)
                act.activation(em[:, g, 0:8], dt_[:, b, 31:512:64], ACT.Exp, scale=1 / 16.0)
                link(act.activation(em[:, g, 8:9], dt_[:, b, TQ + 7:TQ + 8], ACT.Exp, scale=1 / 16.0))
                act.activation(den[:, b, :], dx[:, b, :], ACT.Exp, scale=-1 / 16.0)
                act.activation(dt_[:, b, :], dx[:, b, :], ACT.Exp, scale=1 / 16.0).then_inc(exp_ready, 1)

            def logs(g):
                b = g % 2
                if g >= 2:
                    act.wait_ge(qk_ready, g - 1)
                for x in range(2):
                    key = ("la", g, x)
                    wait_full(act, key)
                    act.activation(dx[:, b, x * HA:x * HA + HA], bank(key)[:, 0:HA], ACT.Identity,
                                   bias=vc("balpha")[:, g:g + 1]).then_inc(act_drained, 1)
                act.wait_ge(act_drained, DRAINS[("la", g, 1)])
                link(act.activation(dt_[:, b, :], dx[:, b, :], ACT.Abs))
                link(act.activation(dt_[:, b, :], dt_[:, b, :], ACT.Exp, scale=-1.0))
                act.activation(dt_[:, b, :], dt_[:, b, :], ACT.Ln, bias=1.0).then_inc(log_ready, 1)

            for g in range(2):
                logs(g)
            for g in range(2):
                exps(g)
            for g in range(2, 4):
                logs(g)
                exps(g)
            for x in range(2):
                drain(("kbT", x), kbT[:, 4 * x:4 * x + 4, :], bank(("kbT", x))[:, :].rearrange("p (k c) -> p k c", k=4))

            n = len(UNITS)
            for u in range(n + 2):
                if u < n:
                    kind, a, b = UNITS[u]
                    st = stat[:, u % 3, :]
                    act.wait_ge(max_ready, u + 1)
                    if kind == "p":
                        lo = 0 if a else WINDOW - N_META
                        for kv in range(2):
                            pv = S[:, u % 3, kv * 256 + lo:kv * 256 + 256]
                            act.activation(pv, pv, ACT.Exp, bias=st[:, 2 + kv:3 + kv], accum_out=st[:, 6 + kv:7 + kv])
                        act.activation(st[:, 8:10], st[:, 4:6], ACT.Exp).then_inc(p_exp, 1)
                    else:
                        pv = S[:, u % 3, 0:136]
                        act.activation(pv, pv, ACT.Exp, bias=st[:, 2:3], accum_out=st[:, 6:7])
                        act.activation(st[:, 8:9], st[:, 4:5], ACT.Exp).then_inc(p_exp, 1)
                w = u - 2
                if 0 <= w < n:
                    kind, a, b = UNITS[w]
                    key = ("pT", w)
                    wait_full(act, key)
                    bk = bank(key)[:, :].rearrange("p (a c) -> p a c", a=4)
                    pt = PT[:, w % 3, :].rearrange("p (a c) -> p a c", a=4)
                    if kind == "p" and a:
                        act.activation(pt, bk, ACT.Copy).then_inc(act_drained, 1)
                    elif kind == "p":
                        act.activation(pt[0:N_META, 0:3:2], bk[0:N_META, 0:3:2], ACT.Copy)
                        act.activation(pt[:, 1:4:2], bk[:, 1:4:2], ACT.Copy).then_inc(act_drained, 1)
                    else:
                        act.activation(pt[0:T_S, 1], bk[0:T_S, 1], ACT.Copy)
                        act.activation(pt[:, 0], bk[:, 0], ACT.Copy).then_inc(act_drained, 1)

            wait_job(act, ("o", 19))
            act.wait_ge(out_done, 16 * 6)
            act.wait_ge(spilled, 16 * TILES)
            for g in range(GH):
                if g >= 2:
                    act.wait_ge(kes_ready, g - 1)
                drain(("keT", g, 0), kem[:, g % 2, 0:4, :], bank(("keT", g, 0))[:, :].rearrange("p (k c) -> p k c", k=4))
                r = ROWS_ALL[4]
                drain(("keT", g, 1), kem[0:r, g % 2, 4, :], bank(("keT", g, 1))[0:r, 0:P])
                for i in range(5):
                    key = ("go", g, i) if i < 4 else ("gso", g)
                    r = ROWS[i]
                    drain(key, osb[0:r, i, g * HV:g * HV + HV], bank(key)[0:r, 0:HV])
                    act.wait_ge(act_drained, DRAINS[key])
                    ins = act.activation(junk[0:r, :], osb[0:r, i, g * HV:g * HV + HV], ACT.Square,
                                         accum_out=ss[0:r, 4 * i + g:4 * i + g + 1])
            ins.then_inc(ss_ready, 1)
            act.wait_ge(rms_ready, 1)
            act.activation(rr[:, :], rr[:, :], ACT.Sqrt).then_inc(ss_ready, 1)
            for t in range(8):
                for x in range(2):
                    drain(("gr", t, x), sg[:, t, x * HQ:x * HQ + HQ], bank(("gr", t, x))[:, 0:HQ], func=ACT.Silu)
            act.wait_ge(sp_out, 16 * GH)
            act.wait_ge(s0_out, 16 * GH)
            for m in range(8):
                for x in range(2):
                    n = 2 * m + x
                    for name, dst, o in (("gA", sgA, 0), ("gB", sgB, 8)):
                        if n >= 2:
                            wait_job(act, ("bB", (n - 2) // 2, n % 2))
                        drain((name, m, x), dst[:, n % 2, :], bank((name, m, x))[:, 0:HQ], func=ACT.Sigmoid,
                              bias=vc("bgate")[:, o + m:o + m + 1])
            for i in range(TILES + 1):
                if i < TILES:
                    std(1, i)
                if i:
                    r = ROWS[i - 1]
                    for x in range(2):
                        drain(("h1T", i - 1, x), h1T[:, 4 * x:4 * x + 4, (i - 1) * P:(i - 1) * P + r],
                              bank(("h1T", i - 1, x))[:, :].rearrange("p (k c) -> p k c", k=4)[:, :, 0:r])
            act.wait_ge(rt_exp_in, 1)
            act.activation(R["eg"], R["eg"], ACT.Exp)
            act.activation(R["ex"], R["ex"], ACT.Exp).then_inc(rt_exp, 1)

            act.wait_ge(list_ready, 1)
            last = act.value_load(lst[0:1, 128:129], min_val=N_EXP - 2, max_val=MAX_TILES - 4)

            def drain_xt(g, s):
                act.wait_ge(xt_full, g + 1)
                act.activation(XT[:, s, 0:4, :], psum[0][:, :].rearrange("p (k c) -> p k c", k=4), ACT.Copy)\
                   .then_inc(xt_act, 1)

            def silu(g, s):
                act.wait_ge(gu_full, g + 1)
                act.activation(sil[:, s, :], psum[2 + s][:, 0:F], ACT.Silu).then_inc(silu_done, 1)

            def tile(b, s, left):
                g = b + s
                if left:
                    silu(g + 1, 1 - s)
                act.wait_ge(at_full, g + 1)
                act.activation(aT[:, s, :, :], psum[4][:, 0:F].rearrange("p (k c) -> p k c", k=2), ACT.Copy)\
                   .then_inc(at_done, 1)
                if left > 1:
                    drain_xt(g + 2, s)
                act.wait_ge(dn_full, g + 2)
                act.wait_ge(w_ready, g + 1)
                act.wait_ge(y_sent[s], earlier(b) + 16)
                act.activation(Yt[:, s, 0:512], psum[5][:, :], ACT.Copy, scale=wsel[:, s:s + 1]).then_inc(dn_act, 1)

            drain_xt(0, 0)
            silu(0, 0)
            drain_xt(1, 1)
            with act.Fori(0, last, 2) as g0:
                for s in range(2):
                    tile(g0, s, 2)
            for s in range(2):
                tile(last, s, 1 - s)
            for i in range(TILES + 1):
                if i < TILES:
                    r = ROWS[i]
                    act.wait_ge(y_sum, i + 1)
                    link(act.activation(y1[0:r, i, :], y0[0:r, i, :], ACT.Square, bias=mv[0:r, i, 0:1],
                                        accum_out=mv[0:r, i, 1:2]))
                    act.activation(rstd[0:r, i:i + 1], mv[0:r, i, 1:2], ACT.Sqrt, scale=1.0 / D, bias=epsc[0:r, :])\
                       .then_inc(y_sq, 1)
                if i:
                    r = ROWS[i - 1]
                    act.wait_ge(y_scale, i)
                    act.activation(h1[0:r, i - 1, :], y0[0:r, i - 1, :], ACT.Identity, scale=rstd[0:r, 4 + i:5 + i],
                                   bias=mv[0:r, i - 1, 0:1]).then_inc(y_xn, 1)

        @block.vector
        def _(dve):
            chain = [0]

            def link(ins):
                chain[0] += 1
                ins.then_inc(dve_chain, 1)
                dve.wait_ge(dve_chain, chain[0])

            def statistics(buf, i, r):
                for x in range(2):
                    link(dve.bn_stats(bst[0:r, i, 6 * x:6 * x + 6], buf[0:r, i, 512 * x:512 * x + 512]))
                link(dve.bn_aggr(mv[0:r, i, :], bst[0:r, i, :]))
                dve.tensor_scalar(rstd[0:r, i:i + 1], mv[0:r, i, 1:2], EPS, None, ALU.add).then_inc(ln_var, 1)

            def normalise(n, buf, i, r):
                dve.wait_ge(ln_std, TILES * n + i + 1)
                link(dve.reciprocal(rstd[0:r, i:i + 1], rstd[0:r, 5 + i:6 + i]))
                return dve.tensor_scalar(buf[0:r, i, :], buf[0:r, i, :], mv[0:r, i, 0:1], rstd[0:r, i:i + 1],
                                         ALU.subtract, ALU.mult)

            def drain(key, out, in_):
                wait_full(dve, key)
                dve.tensor_copy(out, in_).then_inc(dve_drained, 1)

            link(dve.memset(rstd[:, :], 1.0))
            dve.memset(epsc[:, :], EPS)
            dve.wait_ge(x_in, 16 * 6)
            for i in range(TILES):
                statistics(h, i, ROWS_ALL[i])
                if i:
                    normalise(0, h, i - 1, ROWS_ALL[i - 1]).then_inc(xn_ready, 1)
            normalise(0, h, TILES - 1, ROWS_ALL[TILES - 1]).then_inc(xn_ready, 1)
            dve.wait_ge(const_in, 16 * 2)
            for i in range(TILES):
                r = ROWS_ALL[i]
                wait_full(dve, ("hT", i, 1))
                for k in range(4):
                    ins = dve.tensor_scalar(hT[:, 4 + k, i * P:i * P + r], bank(("hT", i, 1))[:, k * P:k * P + r],
                                            vc("embg")[:, 4 + k:5 + k], vc("embb")[:, 4 + k:5 + k], ALU.mult, ALU.add)
                ins.then_inc(dve_drained, 1)
            dve.wait_ge(tables_in, 16)
            for i in range(TILES):
                r = ROWS_ALL[i]
                drain(("v", i), v[0:r, i, :], bank(("v", i))[0:r, 0:P])
            for x in range(2):
                drain(("ga", x), gaT[0:RANK, x * HA:x * HA + HA], bank(("ga", x))[0:RANK, 0:HA])

            def decay(g):
                b = g % 2
                dve.wait_ge(log_ready, g + 1)
                link(dve.scalar_tensor_tensor(dx[:, b, :], dx[:, b, :], 0.0, dt_[:, b, :], ALU.min, ALU.subtract))
                link(dve.tensor_tensor_scan(dt_[:, b, :], cst("scan"), dx[:, b, :], 0.0, ALU.mult, ALU.add))
                bp = dt_[:, b, 0:SEQ].rearrange("p (c t) -> p c t", t=CH)
                dve.tensor_tensor(dx[:, b, 0:SEQ].rearrange("p (c t) -> p c t", t=CH), bp,
                                  bp[:, :, 31:32].broadcast_to([P, NCH, CH]), ALU.subtract)
                dve.tensor_tensor(dx[:, b, TQ:T], dt_[:, b, TQ:T], dt_[:, b, TQ + 7:TQ + 8].broadcast_to([P, N_META]),
                                  ALU.subtract)
                link(dve.tensor_copy(dx[:, b, SEQ:TQ], dt_[:, b, SEQ:TQ]))
                dve.tensor_scalar(dx[:, b, :], dx[:, b, :], 1200.0, -1200.0, ALU.min, ALU.max).then_inc(dec_ready, 1)

            def apply_decay(g):
                b = g % 2
                dve.wait_ge(exp_ready, g + 1)
                dve.tensor_copy(fin[:, g, 0:8], dt_[:, b, 63:512:64])
                dve.tensor_copy(fin[:, g, 8:16], dt_[:, b, 519:576:8])
                dve.tensor_copy(fin[:, g, 16:17], dt_[:, b, T - 1:T])
                dve.tensor_copy(gq[:, g, :], dt_[:, b, 0:TQ])
                dve.tensor_copy(gk[:, g, :], den[:, b, :]).then_inc(qk_ready, 1)

            decay(0)
            decay(1)
            apply_decay(0)
            apply_decay(1)
            for g in range(2, 4):
                decay(g)
                apply_decay(g)
            dve.wait_ge(qk_ready, GH)
            for n, dst, w in (("gq", gq, HQ), ("gk", gk, HA)):
                for g in range(GH):
                    for x in range(2):
                        key = (n, g, x)
                        wait_full(dve, key)
                        c = dst[:, g, x * w:x * w + w]
                        dve.scalar_tensor_tensor(c, bank(key)[:, 0:w], HK ** -0.5 if n == "gq" else 1.0, c, ALU.mult,
                                                 ALU.mult).then_inc(dve_drained, 1)
            for x in range(2):
                for i in range(TILES):
                    r = ROWS_ALL[i]
                    drain(("gv", x, i), gv[0:r, i, 512 * x:512 * x + 512], bank(("gv", x, i))[0:r, :])
            drain(("ktok", 0), ktok[:, 0, :], bank(("ktok", 0))[:, 0:P])
            drain(("ktok", 1), ktok[0:NS, 1, :], bank(("ktok", 1))[0:NS, 0:P])

            n = len(UNITS)
            for u in range(n + 3):
                if u < n:
                    kind, a, b = UNITS[u]
                    st = stat[:, u % 3, :]
                    key = ("s", u)
                    wait_full(dve, key)
                    if kind == "p":
                        lo = 0 if a else WINDOW - N_META
                        sv = S[:, u % 3, :].rearrange("p (k c) -> p k c", k=2)[:, :, lo:256]
                        dve.tensor_tensor(sv, bank(key)[:, :].rearrange("p (k c) -> p k c", k=2)[:, :, lo:256],
                                          bias[:, b, :, lo:256], ALU.add).then_inc(dve_drained, 1)
                        m, sink = 2, vc("sink")[:, 2 * b:2 * b + 2]
                    else:
                        sv = S[:, u % 3, 0:136].rearrange("p (k c) -> p k c", k=1)
                        dve.tensor_tensor(sv[:, 0, :], bank(key)[:, 0:136], sbias[:, b, :], ALU.add)\
                           .then_inc(dve_drained, 1)
                        m, sink = 1, vc("ssink")[:, b:b + 1]
                    dve.wait_ge(dve_drained, DRAINS[key])
                    link(dve.tensor_reduce(st[:, 0:m], sv, AX.X, ALU.max))
                    link(dve.tensor_tensor(st[:, 0:m], st[:, 0:m], sink, ALU.max))
                    dve.tensor_tensor(st[:, 4:4 + m], sink, st[:, 0:m], ALU.subtract)
                    dve.tensor_scalar(st[:, 2:2 + m], st[:, 0:m], -1.0, None, ALU.mult).then_inc(max_ready, 1)
                w = u - 1
                if 0 <= w < n:
                    kind, a, b = UNITS[w]
                    st = stat[:, w % 3, :]
                    dve.wait_ge(p_exp, w + 1)
                    m = 2 if kind == "p" else 1
                    link(dve.tensor_tensor(st[:, 10:10 + m], st[:, 6:6 + m], st[:, 8:8 + m], ALU.add))
                    link(dve.reciprocal(st[:, 12:12 + m], st[:, 10:10 + m]))
                    if kind == "p":
                        lo = 0 if a else WINDOW - N_META
                        sv = S[:, w % 3, :].rearrange("p (k c) -> p k c", k=2)[:, :, lo:256]
                        dve.tensor_tensor(sv, sv, st[:, 12:14].rearrange("p (k c) -> p k c", c=1)
                                          .broadcast_to([P, 2, 256 - lo]), ALU.mult).then_inc(p_norm, 1)
                    else:
                        dve.tensor_scalar(S[:, w % 3, 0:136], S[:, w % 3, 0:136], st[:, 12:13], None, ALU.mult)\
                           .then_inc(p_norm, 1)
                w = u - 3
                if 0 <= w < n:
                    kind, a, b = UNITS[w]
                    kv = b // 2 if kind == "p" else b
                    rows = slice(HD * kv, HD * kv + HD)
                    src = bank(("o", w))
                    if kind == "p":
                        hl = 2 * (b % 2)
                        drain(("o", w), yaT[rows, hl:hl + 2, a * P:a * P + P],
                              src[rows, 0:2 * P].rearrange("p (x c) -> p x c", x=2))
                    else:
                        dst = yaT[rows, :, SEQ + 32 * a:SEQ + 32 * a + 32].rearrange("p h (b t) -> p b h t", t=T_S)
                        src = src[rows, 0:P].rearrange("p (b h t) -> p b h t", h=4, t=T_S)
                        wait_full(dve, ("o", w))
                        for bb in range(4):
                            ins = dve.tensor_copy(dst[:, bb], src[:, bb])
                        ins.then_inc(dve_drained, 1)

            dve.wait_ge(out_done, 16 * 6)
            link(dve.memset(qz[:, :], 0.0))
            dve.memset(ss[:, :], 1.0)
            link(dve.memset(am[:, :, :], 0.0))
            for g in range(GH):
                b = g % 2
                wait_job(dve, ("keT", g, 1))
                if g:
                    wait_full(dve, ("sU", g - 1, 3))
                dve.tensor_tensor(kes[0:NS, :, :], kem[0:NS, b, 4:5, :].broadcast_to([NS, 8, P]),
                                  cst("bmask")[0:NS, :].rearrange("p (b c) -> p b c", c=1).broadcast_to([NS, 8, P]),
                                  ALU.mult)
                dve.tensor_copy(qz[:, :].rearrange("p (b r) -> p b r", r=72)[:, :, 0:T_S],
                                gq[:, g, SEQ:TQ].rearrange("p (b t) -> p b t", t=T_S)).then_inc(kes_ready, 1)
                key = ("att", g)
                wait_full(dve, key)
                bk = bank(key)[:, 0:320].rearrange("p (i t) -> p i t", t=64)
                av = am[:, b, :].rearrange("p (i t) -> p i t", t=64)
                dve.tensor_tensor(av[:, 0:4, :], bk[:, 0:4, :],
                                  cst("cmask").rearrange("p (a t) -> p a t", a=1).broadcast_to([P, 4, 64]), ALU.mult)
                dve.tensor_tensor(av[0:NS, 4, :], bk[0:NS, 4, :], cst("smask")[0:NS, :], ALU.mult)\
                   .then_inc(dve_drained, 1)
                if g:
                    wait_full(dve, ("gso", g - 1))
                for c in range(-1, NCH):
                    key = ("U", g, c)
                    wait_full(dve, key)
                    if c < 0:
                        dve.tensor_scalar(Sp[:, 0, :], bank(key)[:, 0:HV], fin[:, g, 16:17], em[:, g, 0:1], ALU.mult,
                                          ALU.mult).then_inc(dve_drained, 1)
                        dve.wait_ge(dve_drained, DRAINS[key])
                    else:
                        if c == 7 and g:
                            dve.wait_ge(sp_out, 16 * g)
                        dve.tensor_tensor(Sp[:, c + 1, :], bank(key)[:, 0:HV], Sp[:, c, :], ALU.add)\
                           .then_inc(dve_drained, 1)
                        dve.wait_ge(dve_drained, DRAINS[key])
                        if c < NCH - 1:
                            link(dve.tensor_scalar(Sp[:, c + 1, :], Sp[:, c + 1, :], fin[:, g, c:c + 1],
                                                   em[:, g, c + 1:c + 2], ALU.mult, ALU.mult))
                        else:
                            dve.tensor_scalar(Sp[:, 8, :], Sp[:, 8, :], fin[:, g, 7:8], None, ALU.mult)\
                               .then_inc(sp_final, 1)
                dve.wait_ge(s0_in, 16 * (g + 1))
                for x in range(4):
                    key = ("sU", g, x)
                    wait_full(dve, key)
                    sv = s0[:, 2 * x:2 * x + 2, :]
                    dve.tensor_tensor(sv, bank(key)[:, :].rearrange("p (b c) -> p b c", b=2), sv, ALU.add)\
                       .then_inc(dve_drained, 1)
                    dve.wait_ge(dve_drained, DRAINS[key])
                    ins = dve.tensor_tensor(sv, sv, fin[:, g, 8 + 2 * x:10 + 2 * x].rearrange("p (b c) -> p b c", c=1)
                                            .broadcast_to([P, 2, HV]), ALU.mult)
                    if x == 3:
                        ins.then_inc(s0_final, 1)
            dve.wait_ge(ss_ready, 1)
            dve.tensor_scalar(rr[:, :], ss[:, :], 1.0 / HV, EPS, ALU.mult, ALU.add).then_inc(rms_ready, 1)
            dve.wait_ge(ss_ready, 2)
            link(dve.reciprocal(rr[:, :], rr[:, :]))
            for i in range(TILES):
                r = ROWS[i]
                ov = osb[0:r, i, :].rearrange("p (g c) -> p g c", g=GH)
                dve.tensor_tensor(ov, ov, rr[0:r, 4 * i:4 * i + 4].rearrange("p (g c) -> p g c", c=1)
                                  .broadcast_to([r, GH, HV]), ALU.mult).then_inc(y_norm, 1)
            for t in range(8):
                wait_job(dve, ("gr", t, 1))
                link(dve.tensor_scalar(sg[:, t, :], sg[:, t, :], vc("normg")[:, t:t + 1], None, ALU.mult))
            for i in range(TILES):
                r = ROWS[i]
                for x in range(2):
                    key = ("yT", i, x)
                    wait_full(dve, key)
                    dve.tensor_tensor(ygT[:, 4 * x:4 * x + 4, i * P:i * P + r],
                                      bank(key)[:, :].rearrange("p (k c) -> p k c", k=4)[:, :, 0:r],
                                      sg[:, 4 * x:4 * x + 4, i * P:i * P + r], ALU.mult).then_inc(dve_drained, 1)
            for m in range(8):
                for x in range(2):
                    n = 2 * m + x
                    key = ("bA", m, x)
                    wait_full(dve, key)
                    wait_job(dve, ("gA", m, x))
                    if n:
                        wait_job(dve, ("bB", (n - 1) // 2, (n - 1) % 2))
                    dve.tensor_tensor(tA[:, :], bank(key)[:, 0:HQ], sgA[:, n % 2, :], ALU.mult).then_inc(dve_drained, 1)
                    key = ("bB", m, x)
                    wait_full(dve, key)
                    wait_job(dve, ("gB", m, x))
                    link(dve.tensor_tensor(tB[:, :], bank(key)[:, 0:HQ], sgB[:, n % 2, :], ALU.mult))
                    dve.tensor_tensor(mixT[:, m, x * HQ:x * HQ + HQ], tA[:, :], tB[:, :], ALU.add)\
                       .then_inc(dve_drained, 1)
            lg = R["lg"].rearrange("p (i b) -> p i b", b=36)
            wait_full(dve, ("mix", 0, 0))
            link(dve.memset(R["lg"], 0.0))
            dve.wait_ge(h_back, 16 * TILES)
            dve.wait_ge(ln_in, 64)
            for i in range(TILES + 1):
                if i < TILES:
                    r = ROWS[i]
                    for x in range(2):
                        key = ("mix", x, i)
                        wait_full(dve, key)
                        hv = h1[0:r, i, 512 * x:512 * x + 512]
                        dve.scalar_tensor_tensor(hv, hv, ALPHA, bank(key)[0:r, :], ALU.mult, ALU.add)\
                           .then_inc(dve_drained, 1)
                    wait_job(dve, ("mix", 1, i))
                    statistics(h1, i, r)
                    link(normalise(1, h1, i, r))
                    link(dve.tensor_tensor(h1[0:r, i, :], h1[0:r, i, :], lng[0:r, :], ALU.mult))
                    dve.tensor_tensor(h1[0:r, i, :], h1[0:r, i, :], lnb[0:r, :], ALU.add).then_inc(h1_ready, 1)
                if i:
                    r = ROWS[i - 1]
                    key = ("rt", i - 1)
                    wait_full(dve, key)
                    dve.tensor_tensor(lg[0:r, i - 1, :], bank(key)[0:r, 0:36], vc("brout")[0:r, :], ALU.add)\
                       .then_inc(dve_drained, 1)
            wait_job(dve, ("rt", 4))

            def v3(n, b):
                return R[n].rearrange("p (i b) -> p i b", b=b)

            def bc(n, b):
                return R[n].rearrange("p (i b) -> p i b", b=1).broadcast_to([P, TILES, b])

            def tab(n, b):
                return cst(n).rearrange("p (i b) -> p i b", i=1).broadcast_to([P, TILES, b])

            def first_max(vals, w, mx, tmp, mn, oh, table):
                link(dve.tensor_reduce(R[mx], vals, AX.X, ALU.max))
                link(dve.tensor_tensor(v3(tmp, w), vals, bc(mx, w), ALU.is_equal))
                link(dve.tensor_tensor(v3(tmp, w), v3(tmp, w), tab(table, w), ALU.mult))
                link(dve.tensor_reduce(R[mn], v3(tmp, w), AX.X, ALU.min))
                link(dve.tensor_tensor(v3(oh, w), bc(mn, w), tab(table, w), ALU.is_equal))

            first_max(lg[:, :, 0:4], 4, "gmax", "gt", "gmin", "goh", "i4")
            link(dve.tensor_tensor(v3("eg", 4), lg[:, :, 0:4], bc("gmax", 4), ALU.subtract))
            def group_hot():
                return R["goh"].rearrange("p (i g e) -> p i g e", g=4, e=1).broadcast_to([P, TILES, 4, 8])

            def by_group(n):
                return R[n].rearrange("p (i g e) -> p i g e", g=4, e=8)

            link(dve.tensor_tensor(by_group("pr"), lg[:, :, 4:36].rearrange("p i (g e) -> p i g e", g=4), group_hot(),
                                   ALU.mult))
            link(dve.tensor_reduce(v3("ein", 8), R["pr"].rearrange("p (i g e) -> p i e g", g=4, e=8), AX.X, ALU.add))
            first_max(v3("ein", 8), 8, "m1", "t8", "mn", "oh1", "i8")
            link(dve.scalar_tensor_tensor(R["ein"], R["oh1"], -1e30, R["ein"], ALU.mult, ALU.add))
            first_max(v3("ein", 8), 8, "m2", "t8", "mn", "oh2", "i8")
            dve.tensor_tensor(R["ex"], R["m2"], R["m1"], ALU.subtract).then_inc(rt_exp_in, 1)
            for n, oh in (("M1", "oh1"), ("M2", "oh2")):
                link(dve.tensor_tensor(by_group(n), group_hot(), R[oh].rearrange("p (i g e) -> p i g e", g=1, e=8)
                                       .broadcast_to([P, TILES, 4, 8]), ALU.mult))
            link(dve.tensor_tensor(R["M"], R["M1"], R["M2"], ALU.add))
            dve.tensor_tensor(v3("M", 32), v3("M", 32), cst("valid").rearrange("p (i b) -> p i b", b=1)
                              .broadcast_to([P, TILES, 32]), ALU.mult).then_inc(mask_ready, 1)
            dve.wait_ge(rt_exp, 1)
            link(dve.tensor_reduce(R["gsum"], v3("eg", 4), AX.X, ALU.add))
            link(dve.tensor_scalar(R["w1"], R["ex"], 1.0, None, ALU.add))
            link(dve.tensor_tensor(R["w1"], R["w1"], R["gsum"], ALU.mult))
            link(dve.reciprocal(R["w1"], R["w1"]))
            link(dve.tensor_tensor(R["w2"], R["w1"], R["ex"], ALU.mult))
            dve.memset(ent[:, :, 3], 0)
            for n in range(2):
                dve.tensor_copy(ent[:, 5 * n:5 * n + 5, 0], cst("tok"))
                dve.tensor_scalar(ent[:, 5 * n:5 * n + 5, 1], cst("tok"), float(TQ * n), None, ALU.add)
                dve.tensor_copy(ent[:, 5 * n:5 * n + 5, 2].bitcast(f32), R[f"w{n + 1}"])
            key = ("cnt",)
            wait_full(dve, key)
            dve.tensor_copy(R["cnt"], bank(key)[:, 0:32]).then_inc(dve_drained, 1)
            wait_job(dve, key)
            link(dve.tensor_scalar(R["nt"], R["cnt"], 128.0, None, ALU.is_gt))
            for k in range(2, 5):
                link(dve.scalar_tensor_tensor(R["nt"], R["cnt"], 128.0 * k, R["nt"], ALU.is_gt, ALU.add))
            link(dve.tensor_tensor_scan(R["inc"], ones[:, 0:32], R["nt"], 0.0, ALU.mult, ALU.add))
            link(dve.tensor_scalar(R["t5"], cst("evens"), R["inc"][:, 31:32], None, ALU.is_lt))
            link(dve.tensor_reduce(R["r1"][:, 0:1], R["t5"], AX.X, ALU.add))
            dve.tensor_scalar(lst[0:1, 128:129], R["r1"][0:1, 0:1], 2.0, float(N_EXP - 2), ALU.mult, ALU.add)
            link(dve.tensor_scalar(R["cnt"], R["inc"], cst("pid"), None, ALU.is_le))
            link(dve.tensor_reduce(R["eg1"], R["cnt"], AX.X, ALU.add))
            dve.tensor_scalar(R["eg1"], R["eg1"], cst("plow"), float(N_EXP - 1), ALU.add, ALU.min).then_inc(ids_ready, 1)
            wait_full(dve, ("pos",))
            dve.tensor_copy(R["pos"], bank(("pos",))[:, 0:160]).then_inc(dve_drained, 1)
            wait_job(dve, ("pos",))
            link(dve.tensor_scalar(R["q"], R["pos"], 128.0, None, ALU.is_ge))
            link(dve.tensor_tensor(R["inc"], R["inc"], R["nt"], ALU.subtract))
            link(dve.tensor_tensor(R["inc"], R["inc"], cst("e31"), ALU.add))
            dve.tensor_tensor(v3("t160", 32), v3("q", 32), R["inc"].rearrange("p (i b) -> p i b", i=1)
                              .broadcast_to([P, TILES, 32]), ALU.mult)
            for k in range(2, 5):
                link(dve.scalar_tensor_tensor(R["q"], R["pos"], 128.0 * k, R["q"], ALU.is_ge, ALU.add))
            link(dve.scalar_tensor_tensor(R["q"], R["q"], 1.0 - 128.0 * MAX_TILES, R["t160"], ALU.mult, ALU.add))
            link(dve.scalar_tensor_tensor(R["q"], R["pos"], float(MAX_TILES), R["q"], ALU.mult, ALU.add))
            link(dve.tensor_tensor(v3("q", 32), v3("q", 32), cst("eid").rearrange("p (i b) -> p i b", i=1)
                                   .broadcast_to([P, TILES, 32]), ALU.add))
            for n, m in enumerate(("M1", "M2")):
                link(dve.tensor_tensor(R["t160"], R["q"], R[m], ALU.mult))
                link(dve.tensor_reduce(R["r1"][:, 5 * n:5 * n + 5], v3("t160", 32), AX.X, ALU.add))
            dve.tensor_copy(rowi[:, :], R["r1"]).then_inc(rows_ready, 1)
            key = ("lst",)
            wait_full(dve, key)
            dve.tensor_copy(lst[0:1, 0:128], bank(key)[0:1, 0:128]).then_inc(dve_drained, 1)
            wait_job(dve, key)
            dve.sem_inc(list_ready, 1)

            last = dve.value_load(lst[0:1, 128:129], min_val=N_EXP - 2, max_val=MAX_TILES - 4)

            def drain_xt(g, s):
                dve.wait_ge(xt_full, g + 1)
                dve.tensor_copy(XT[:, s, 4:8, :], psum[1][:, :].rearrange("p (k c) -> p k c", k=4)).then_inc(xt_dve, 1)

            def gate(g, s):
                dve.wait_ge(silu_done, g + 1)
                dve.tensor_tensor(act_[:, s, :], psum[2 + s][:, F:2 * F], sil[:, s, :], ALU.mult).then_inc(act_done, 1)

            def tile(b, s, left):
                g = b + s
                if left:
                    gate(g + 1, 1 - s)
                dve.tensor_copy(wsel[:, s:s + 1], tb[:, bass.ds(g, 1), 2].bitcast(f32)).then_inc(w_ready, 1)
                if left > 1:
                    drain_xt(g + 2, s)
                dve.wait_ge(dn_full, g + 2)
                dve.wait_ge(w_ready, g + 1)
                dve.wait_ge(y_sent[s], earlier(b) + 16)
                dve.tensor_scalar(Yt[:, s, 512:1024], psum[6][:, :], wsel[:, s:s + 1], None, ALU.mult)\
                   .then_inc(dn_dve, 1)

            dve.wait_ge(h1_stored, 16 * TILES)
            for i in range(TILES):
                r = ROWS[i]
                dve.tensor_scalar(h1[0:r, i, :], h1[0:r, i, :], ALPHA, None, ALU.mult).then_inc(h1_scaled, 1)
            dve.wait_ge(tb_in, 16)
            drain_xt(0, 0)
            gate(0, 0)
            drain_xt(1, 1)
            with dve.Fori(0, last, 2) as g0:
                for s in range(2):
                    tile(g0, s, 2)
            for s in range(2):
                tile(last, s, 1 - s)
            dve.wait_ge(h1_scaled, TILES)
            dve.wait_ge(ln_in, 96)
            for i in range(TILES + 2):
                if i < TILES:
                    r = ROWS[i]
                    dve.wait_ge(y_part, i + 1)
                    link(dve.scalar_tensor_tensor(y0[0:r, i, :], h1[0:r, i, :], 1.0, y0[0:r, i, :], ALU.mult, ALU.add,
                                                  accum_out=mv[0:r, i, 0:1]))
                    dve.tensor_scalar(mv[0:r, i, 0:1], mv[0:r, i, 0:1], -1.0 / D, None, ALU.mult).then_inc(y_sum, 1)
                if 1 <= i <= TILES:
                    j = i - 1
                    r = ROWS[j]
                    dve.wait_ge(y_sq, j + 1)
                    link(dve.reciprocal(rstd[0:r, 5 + j:6 + j], rstd[0:r, j:j + 1]))
                    dve.tensor_tensor(mv[0:r, j, 0:1], mv[0:r, j, 0:1], rstd[0:r, 5 + j:6 + j], ALU.mult)\
                       .then_inc(y_scale, 1)
                if i >= 2:
                    j = i - 2
                    r = ROWS[j]
                    dve.wait_ge(y_xn, j + 1)
                    dve.tensor_tensor(h1[0:r, j, :], h1[0:r, j, :], lng[0:r, :], ALU.mult).then_inc(y_g, 1)

        @block.tensor
        def _(pe):
            def open_bank(key):
                n = INDEX[key]
                if n >= NBANK:
                    wait_job(pe, ORDER[n - NBANK][0])
                return bank(key)

            def full(ins):
                ins.then_inc(psum_full, 1)

            def feature_job(key, w, cols, lo, n):
                bk = open_bank(key)
                m = cols.stop - cols.start
                for kc in range(KC):
                    ins = pe.matmul(bk[0:m, 0:n], w[:, kc, cols], hT[:, kc, lo:lo + n], start=(kc == 0),
                                    stop=(kc == KC - 1))
                full(ins)

            pe.wait_ge(const_in, 16 * 2)
            for i in range(TILES):
                r = ROWS_ALL[i]
                pe.wait_ge(xn_ready, i + 1)
                for x in range(2):
                    bk = open_bank(("hT", i, x))
                    for k in range(4):
                        c = (4 * x + k) * P
                        ins = pe.transpose(bk[:, k * P:k * P + r], h[0:r, i, c:c + P], ident[0:r, 0:r])
                    full(ins)
            wait_job(pe, ("hT", 4, 0))
            wait_job(pe, ("hT", 4, 1))
            wait_chunk(pe, "q")
            w = chunk("q")
            for t in range(4):
                for x in range(2):
                    key = ("q", t, x)
                    bk = open_bank(key)
                    for kc in range(KC):
                        ins = pe.matmul(bk[:, 0:HQ], w[:, kc, t * P:t * P + P], hT[:, kc, x * HQ:x * HQ + HQ], start=(kc == 0),
                                        stop=(kc == KC - 1))
                    full(ins)
            wait_chunk(pe, "kv")
            w = chunk("kv")
            for x in range(2):
                feature_job(("k", x), w, slice(0, P), x * HA, HA)
            for i in range(TILES):
                r = ROWS_ALL[i]
                bk = open_bank(("v", i))
                for kc in range(KC):
                    ins = pe.matmul(bk[0:r, 0:P], hT[:, kc, i * P:i * P + r], w[:, kc, P:2 * P], start=(kc == 0),
                                    stop=(kc == KC - 1))
                full(ins)
            wait_chunk(pe, "ga")
            w = chunk("ga")
            for x in range(2):
                feature_job(("ga", x), w, slice(0, RANK), x * HA, HA)
            wait_job(pe, ("ga", 1))
            pe.wait_ge(w2_in, 16)
            for g in range(GH):
                for x in range(2):
                    bk = open_bank(("la", g, x))
                    full(pe.matmul(bk[:, 0:HA], w2[0:RANK, g * P:g * P + P], gaT[0:RANK, x * HA:x * HA + HA], start=True,
                                   stop=True))
            for n, wd_ in (("gq", HQ), ("gk", HA)):
                wait_chunk(pe, n)
                w = chunk(n)
                for g in range(GH):
                    for x in range(2):
                        feature_job((n, g, x), w, slice(g * P, g * P + P), x * wd_, wd_)
            for x in range(2):
                wait_chunk(pe, f"gv{x}")
                w = chunk(f"gv{x}")
                for i in range(TILES):
                    r = ROWS_ALL[i]
                    bk = open_bank(("gv", x, i))
                    for kc in range(KC):
                        ins = pe.matmul(bk[0:r, :], hT[:, kc, i * P:i * P + r], w[:, kc, :], start=(kc == 0),
                                        stop=(kc == KC - 1))
                    full(ins)
            wait_job(pe, ("k", 1))
            full(pe.transpose(open_bank(("ktok", 0))[:, 0:P], kT[:, 384:512], ident[:, :]))
            full(pe.transpose(open_bank(("ktok", 1))[0:NS, 0:P], kT[:, SEQ:TQ], ident[:, :]))
            pe.wait_ge(state_in, 32)
            for x in range(2):
                bk = open_bank(("kbT", x))
                for b in range(4):
                    ins = pe.transpose(bk[:, b * P:b * P + P], sbk[:, 4 * x + b, :], ident[:, :])
                full(ins)

            def scores(u):
                kind, a, b = UNITS[u]
                bk = open_bank(("s", u))
                if kind == "p":
                    rows = slice(HD * (b // 2), HD * (b // 2) + HD)
                    for x in range(2):
                        q = qT[rows, 2 * (b % 2) + x, a * P:a * P + P]
                        c = x * 256
                        if a:
                            ins = pe.matmul(bk[:, c:c + 256], q, kT[rows, (a - 1) * P:(a + 1) * P], start=True, stop=True)
                        else:
                            pe.matmul(bk[:, c + P - N_META:c + P], q, kT[rows, TQ:T], start=True, stop=True)
                            ins = pe.matmul(bk[:, c + P:c + 256], q, kT[rows, 0:P], start=True, stop=True)
                else:
                    for bb in range(4):
                        s = 4 * a + bb
                        q = qs[HD * b:HD * b + HD, s, :]
                        pe.matmul(bk[32 * bb:32 * bb + 32, 0:P], q, kbT[HD * b:HD * b + HD, s, :], start=True, stop=True)
                        ins = pe.matmul(bk[32 * bb:32 * bb + 32, P:P + T_S], q,
                                        kT[HD * b:HD * b + HD, SEQ + T_S * s:SEQ + T_S * s + T_S], start=True, stop=True)
                full(ins)

            def turn(u):
                kind, a, b = UNITS[u]
                pe.wait_ge(p_norm, u + 1)
                bk = open_bank(("pT", u))
                if kind == "p":
                    for kv in range(2):
                        c = kv * 256
                        if a:
                            pe.transpose(bk[:, c:c + P], S[:, u % 3, c:c + P], ident[:, :])
                        else:
                            pe.transpose(bk[0:N_META, c:c + P], S[:, u % 3, c + P - N_META:c + P], ident[:, :])
                        ins = pe.transpose(bk[:, c + P:c + 256], S[:, u % 3, c + P:c + 256], ident[:, :])
                else:
                    pe.transpose(bk[:, 0:P], S[:, u % 3, 0:P], ident[:, :])
                    ins = pe.transpose(bk[0:T_S, P:2 * P], S[:, u % 3, P:P + T_S], ident[:, :])
                full(ins)

            def values(u):
                kind, a, b = UNITS[u]
                wait_job(pe, ("pT", u))
                bk = open_bank(("o", u))
                kv = b // 2 if kind == "p" else b
                rows = bk[HD * kv:HD * kv + HD, :]
                cols = slice(HD * kv, HD * kv + HD)
                if kind == "p":
                    for x in range(2):
                        pt = PT[:, u % 3, x * 256:x * 256 + 256]
                        out = rows[:, x * P:x * P + P]
                        if a:
                            pe.matmul(out, v[:, a - 1, cols], pt[:, 0:P], start=True, stop=False)
                        else:
                            pe.matmul(out, vm[0:N_META, cols], pt[0:N_META, 0:P], start=True, stop=False)
                        ins = pe.matmul(out, v[:, a, cols], pt[:, P:2 * P], start=False, stop=True)
                else:
                    pt = PT[:, u % 3, :]
                    for bb in range(4):
                        s = 4 * a + bb
                        o = rows[:, 32 * bb:32 * bb + 32]
                        pe.matmul(o, sbv[:, s, cols], pt[:, 32 * bb:32 * bb + 32], start=True, stop=False)
                        ins = pe.matmul(o, vn[0:T_S, s, cols], pt[0:T_S, P + 32 * bb:P + 32 * bb + 32], start=False,
                                        stop=True)
                full(ins)

            wait_job(pe, ("kbT", 1))
            pe.wait_ge(rows_moved, 16 * 9)
            n = len(UNITS)
            for u in range(n + 3):
                if u < n:
                    scores(u)
                if 0 <= u - 2 < n:
                    turn(u - 2)
                if 0 <= u - 3 < n:
                    values(u - 3)

            for g in range(GH):
                b = g % 2
                wait_job(pe, ("gk", g, 1))
                bk = open_bank(("keT", g, 0))
                for i in range(4):
                    ins = pe.transpose(bk[:, i * P:i * P + P], gk[:, g, i * P:i * P + P], ident[:, :])
                full(ins)
                full(pe.transpose(open_bank(("keT", g, 1))[0:NS + N_META, 0:P], gk[:, g, SEQ:T], ident[:, :]))
                bk = open_bank(("att", g))
                for c in range(NCH):
                    r, i = 64 * (c % 2), c // 2
                    pe.matmul(bk[r:r + 64, 64 * i:64 * i + 64], gk[:, g, CH * c:CH * c + CH], gq[:, g, CH * c:CH * c + CH],
                              start=True, stop=True)
                full(pe.matmul(bk[0:NS, 256:320], gk[:, g, SEQ:TQ], gq[:, g, SEQ:TQ], start=True, stop=True))
                wait_job(pe, ("keT", g, 1))
                gcol = slice(g * HV, g * HV + HV)
                for c in range(-1, NCH):
                    bk = open_bank(("U", g, c))
                    if c < 0:
                        ins = pe.matmul(bk[:, 0:HV], kem[NS:NS + N_META, b, 4, :], gv[NS:NS + N_META, 4, gcol], start=True,
                                        stop=True)
                    else:
                        r = 64 * (c % 2)
                        ins = pe.matmul(bk[:, 0:HV], kem[r:r + 64, b, c // 2, :], gv[r:r + 64, c // 2, gcol], start=True,
                                        stop=True)
                    full(ins)
                pe.wait_ge(sp_final, g + 1)
                for i in range(4):
                    bk = open_bank(("go", g, i))
                    for c in (2 * i, 2 * i + 1):
                        r = 64 * (c % 2)
                        pe.matmul(bk[r:r + 64, 0:HV], am[r:r + 64, b, 64 * i:64 * i + 64], gv[r:r + 64, i, gcol],
                                  start=True, stop=False)
                        ins = pe.matmul(bk[r:r + 64, 0:HV], gq[:, g, CH * c:CH * c + CH], Sp[:, c, :], start=False,
                                        stop=True)
                    full(ins)
                pe.wait_ge(s0_in, 16 * (g + 1))
                pe.wait_ge(kes_ready, g + 1)
                bk = open_bank(("gso", g))
                pe.matmul(bk[0:NS, 0:HV], am[0:NS, b, 256:320], gv[0:NS, 4, gcol], start=True, stop=False)
                for s in range(8):
                    ins = pe.matmul(bk[0:NS, 0:HV], qz[:, 64 * s:64 * s + 64], s0[:, s, :], start=False, stop=(s == 7))
                full(ins)
                for x in range(4):
                    bk = open_bank(("sU", g, x))
                    for s in range(2):
                        ins = pe.matmul(bk[:, s * HV:s * HV + HV], kes[0:NS, 2 * x + s, :], gv[0:NS, 4, gcol], start=True,
                                        stop=True)
                    full(ins)

            for t in range(8):
                if t % 4 == 0:
                    wait_chunk(pe, f"gr{t // 4}")
                    w = chunk(f"gr{t // 4}")
                for x in range(2):
                    feature_job(("gr", t, x), w, slice(t % 4 * P, t % 4 * P + P), x * HQ, HQ)
            for i in range(TILES):
                r = ROWS[i]
                pe.wait_ge(y_norm, i + 1)
                for x in range(2):
                    bk = open_bank(("yT", i, x))
                    for k in range(4):
                        c = (4 * x + k) * P
                        ins = pe.transpose(bk[:, k * P:k * P + r], osb[0:r, i, c:c + P], ident[0:r, 0:r])
                    full(ins)
            wait_job(pe, ("yT", 4, 1))
            for m in range(8):
                y, c = m // 2, m % 2 * P
                if m % 2 == 0:
                    wait_chunk(pe, f"gates{y}")
                    wait_chunk(pe, f"branch{y}")
                for x in range(2):
                    feature_job(("gA", m, x), chunk(f"gates{y}"), slice(c, c + P), x * HQ, HQ)
                    feature_job(("gB", m, x), chunk(f"gates{y}"), slice(256 + c, 256 + c + P), x * HQ, HQ)
                    w = chunk(f"branch{y}")
                    for nme, src, k0, nk in (("a", yaT, 0, 4), ("b", ygT, 4, 8)):
                        key = ("b" + nme.upper(), m, x)
                        bk = open_bank(key)
                        for kc in range(nk):
                            ins = pe.matmul(bk[:, 0:HQ], w[:, k0 + kc, c:c + P], src[:, kc, x * HQ:x * HQ + HQ],
                                            start=(kc == 0), stop=(kc == nk - 1))
                        full(ins)
            wait_job(pe, ("bB", 7, 1))
            for x in range(2):
                wait_chunk(pe, f"wo{x}")
            pe.wait_ge(wrt_in, 16 * 2)
            for i in range(TILES + 1):
                if i < TILES:
                    r = ROWS[i]
                    for x in range(2):
                        w = chunk(f"wo{x}")
                        bk = open_bank(("mix", x, i))
                        for kc in range(KC):
                            ins = pe.matmul(bk[0:r, :], mixT[:, kc, i * P:i * P + r], w[:, kc, :], start=(kc == 0),
                                            stop=(kc == KC - 1))
                        full(ins)
                if i:
                    j = i - 1
                    r = ROWS[j]
                    pe.wait_ge(h1_ready, j + 1)
                    for x in range(2):
                        bk = open_bank(("h1T", j, x))
                        for k in range(4):
                            c = (4 * x + k) * P
                            ins = pe.transpose(bk[:, k * P:k * P + r], h1[0:r, j, c:c + P], ident[0:r, 0:r])
                        full(ins)
                    wait_job(pe, ("h1T", j, 1))
                    bk = open_bank(("rt", j))
                    for kc in range(KC):
                        ins = pe.matmul(bk[0:r, 0:36], h1T[:, kc, j * P:j * P + r], wrt[:, kc, :], start=(kc == 0),
                                        stop=(kc == KC - 1))
                    full(ins)
            pe.wait_ge(mask_ready, 1)
            M = R["M"].rearrange("p (i e) -> p i e", e=32)
            bk = open_bank(("cnt",))
            for i in range(TILES):
                ins = pe.matmul(bk[:, 0:32], ones, M[:, i, :], start=(i == 0), stop=(i == TILES - 1))
            full(ins)
            bk = open_bank(("pos",))
            for i in range(TILES):
                for j in range(i + 1):
                    ins = pe.matmul(bk[:, 32 * i:32 * i + 32], tri if j == i else ones, M[:, j, :], start=(j == 0),
                                    stop=(j == i))
            full(ins)
            pe.wait_ge(ids_ready, 1)
            full(pe.matmul(open_bank(("lst",))[0:1, 0:128], R["eg1"], ident, start=True, stop=True))

            wait_job(pe, ("lst",))
            pe.wait_ge(list_ready, 1)
            last = pe.value_load(lst[0:1, 128:129], min_val=N_EXP - 2, max_val=MAX_TILES - 4)
            pe.sem_inc(dn_full, 1)
            pe.sem_inc(dn_act, 1)
            pe.sem_inc(dn_dve, 1)

            def turn_x(b, s):
                pe.wait_ge(gathered[s], earlier(b) + 16)
                for k in range(KC):
                    ins = pe.transpose(psum[k // 4][:, k % 4 * P:k % 4 * P + P], Xg[:, s, k:D:KC], ident)
                ins.then_inc(xt_full, 1)

            def gate_up(b, s):
                g = b + s
                pe.wait_ge(xt_act, g + 1)
                pe.wait_ge(xt_dve, g + 1)
                pe.wait_ge(wg_in[s], earlier(b) * 2 + 32)
                for kc in range(KC):
                    ins = pe.matmul(psum[2 + s][:, :], XT[:, s, kc, :], wgu[s][:, kc, :], start=(kc == 0),
                                    stop=(kc == KC - 1))
                ins.then_inc(gu_full, 1)

            def tile(b, s, left):
                g = b + s
                if left:
                    gate_up(b + 2 * s, 1 - s)
                pe.wait_ge(act_done, g + 1)
                for k in range(2):
                    ins = pe.transpose(psum[4][:, k * P:k * P + P], act_[:, s, k:F:2], ident)
                ins.then_inc(at_full, 1)
                if left > 1:
                    pe.wait_ge(xt_act, g + 2)
                    turn_x(b + 2, s)
                pe.wait_ge(at_done, g + 1)
                pe.wait_ge(wd_in[s], earlier(b) + 16)
                pe.wait_ge(dn_act, g + 1)
                pe.wait_ge(dn_dve, g + 1)
                for half in range(2):
                    for k in range(2):
                        ins = pe.matmul(psum[5 + half][:, :], aT[:, s, k, :], wd[s][:, k, 512 * half:512 * half + 512],
                                        start=(k == 0), stop=(k == 1))
                ins.then_inc(dn_full, 1)

            turn_x(0, 0)
            gate_up(0, 0)
            turn_x(0, 1)
            with pe.Fori(0, last, 2) as g0:
                for s in range(2):
                    tile(g0, s, 2)
            for s in range(2):
                tile(last, s, 1 - s)


def constants():
    import numpy as np

    c = np.zeros((P, CONST_W), np.float32)

    def put(n, a):
        o, w = CONST[n]
        c[:, o:o + w] = np.asarray(a, np.float32).reshape(a.shape[0], -1) if a.shape[0] == P else a

    p = np.arange(P)
    put("ident", np.eye(P))
    put("tri", (p[:, None] < p[None, :]) * 1.0)
    put("ones", np.ones((P, P)))
    scan = np.ones(T)
    scan[0:SEQ:CH] = 0
    scan[SEQ:TQ:T_S] = 0
    scan[TQ] = 0
    put("scan", np.tile(scan, (P, 1)))
    slope = 2.0 ** -np.arange(1, HEADS + 1)

    def alibi(dist, s):
        return np.where((dist >= 0) & (dist < WINDOW), -s * dist, -1e30)

    dist = p[:, None] + WINDOW - np.arange(256)[None, :]
    b = np.zeros((P, HEADS, 256))
    for n in range(HEADS):
        b[:, n] = alibi(dist, slope[n])
    put("bias", b)
    rows_t, rows_h = p % T_S, p // T_S % 4
    dist = rows_t[:, None] + WINDOW - np.arange(WINDOW + T_S)[None, :]
    b = np.zeros((P, 2, WINDOW + T_S))
    for kv in range(2):
        b[:, kv] = alibi(dist, slope[4 * kv + rows_h][:, None])
    put("sbias", b)
    t = np.arange(64)
    put("cmask", (p[:, None] % 64 <= t[None, :]) * 1.0)
    put("smask", ((p[:, None] // T_S == t[None, :] // T_S) & (p[:, None] <= t[None, :])) * 1.0)
    put("bmask", (p[:, None] // T_S == np.arange(8)[None, :]) * 1.0)
    put("i4", np.tile(np.arange(4) - 99.0, (P, 1)))
    put("i8", np.tile(np.arange(8) - 99.0, (P, 1)))
    tok = p[:, None] + P * np.arange(TILES)[None, :]
    put("valid", (tok < TQ) * 1.0)
    put("tok", tok)
    put("pid", p[:, None] - N_EXP)
    put("plow", np.where(p < N_EXP, p, 0)[:, None])
    put("evens", np.tile(2.0 * np.arange(5), (P, 1)))
    put("eid", np.tile(np.arange(N_EXP), (P, 1)))
    put("e31", np.tile(31 - np.arange(N_EXP), (P, 1)))
    return c


_INS = ["x_prompt", "x_sample", "state_swa_k", "state_swa_v", "state_gla", "meta_tokens", "ln_emb_g", "ln_emb_b", "w_in",
        "w_alpha2", "w_attn_br", "w_gla_br", "w_out", "ln1_g", "ln1_b", "w_router_group", "w_router_expert", "w_exp_gate",
        "w_exp_up", "w_exp_down", "ln2_g", "ln2_b"]
_OUTS = [(1, SEQ, D), (NB_S, T_S, D), (1, 1, WINDOW, N_KV, HD), (1, 1, WINDOW, N_KV, HD), (1, 1, GH, HK, HV),
         (1, NB_S, WINDOW, N_KV, HD), (1, NB_S, WINDOW, N_KV, HD), (1, NB_S, GH, HK, HV)]


def kernel(**inputs):
    import numpy as _np
    import concourse.bacc as _bacc
    from concourse import mybir as _mybir
    from concourse.bass_utils import run_bass_kernel_spmd as _run

    arrays = {n: _np.ascontiguousarray(inputs[n]) for n in _INS}
    arrays["const"] = constants()
    arrays["w_q"] = _np.ascontiguousarray(_np.asarray(inputs["w_in"])[0, :, 0:512].reshape(D, 2, 4, HD)
                                          .transpose(0, 2, 1, 3).reshape(D, 512))
    v = _np.zeros((P, VEC_W), _np.float32)

    def put(n, a):
        v[:, VEC[n][0]:VEC[n][0] + VEC[n][1]] = a

    sink = _np.asarray(inputs["attn_sink"])[0]
    put("sink", _np.broadcast_to(sink, (P, HEADS)))
    put("ssink", _np.tile(_np.repeat(sink.reshape(2, 4), T_S, axis=1), (1, 4)).T)
    put("balpha", _np.asarray(inputs["b_alpha"])[0].reshape(4, P).T)
    put("bgate", _np.asarray(inputs["b_gate"])[0].reshape(16, P).T)
    put("normg", _np.asarray(inputs["gla_norm_g"])[0].reshape(8, P).T)
    put("embg", _np.asarray(inputs["ln_emb_g"]).reshape(8, P).T)
    put("embb", _np.asarray(inputs["ln_emb_b"]).reshape(8, P).T)
    put("brout", _np.broadcast_to(_np.concatenate([_np.asarray(inputs["b_router_group"])[0],
                                                   _np.asarray(inputs["b_router_expert"])[0]]), (P, 36)))
    arrays["vec"] = v
    nc = _bacc.Bacc("TRN2", target_bir_lowering=False, num_devices=1)
    A = {n: nc.dram_tensor(f"in_{n}", a.shape, _mybir.dt.from_np(a.dtype), kind="ExternalInput").ap()
         for n, a in arrays.items()}
    O = [nc.dram_tensor(f"out_{i}", shape, _mybir.dt.float32, kind="ExternalOutput").ap()
         for i, shape in enumerate(_OUTS)]
    decoder_kernel(nc, A, O)
    r = _run(nc, [{f"in_{n}": a for n, a in arrays.items()}], core_ids=[0])
    return tuple(r.results[0][f"out_{i}"] for i in range(len(_OUTS)))
```

```python
import concourse.bass as bass
from concourse import mybir
from contextlib import ExitStack

P = 128
D = 1024
KC = D // P
SEQ, NB_S, T_S, N_META = 512, 8, 8, 16
NS = NB_S * T_S
TQ = SEQ + NS
T = TQ + N_META
TILES = 5
ROWS = [P, P, P, P, NS]
ROWS_ALL = [P, P, P, P, NS + N_META]
HQ = TQ // 2
HA = T // 2
HEADS, N_KV, HD, WINDOW = 8, 2, 64, 128
GH, HK, HV = 4, 128, 256
CH = 64
NCH = SEQ // CH
RANK = 16
N_EXP, N_GRP, EPG, F = 32, 4, 8, 256
EPS = 1e-5
ALPHA = 2.0 ** 0.25
C_Q, C_K, C_V, C_GQ, C_GK, C_GV, C_GA, C_GR, C_GATE = 0, 512, 640, 768, 1280, 1792, 2816, 2832, 3856
MAX_TILES = 44
PAD_ROW = 4096
NBANK = 8
RING = 4
SLOT = KC * 256

CONST = {}
_at = 0
for _n, _w in (("ident", 128), ("tri", 128), ("ones", 128), ("scan", T), ("bias", 2048), ("sbias", 272),
               ("cmask", 64), ("smask", 64), ("bmask", 8), ("i4", 4), ("i8", 8), ("valid", 5), ("tok", 5), ("pid", 1), ("plow", 1), ("eid", 32), ("e31", 32), ("evens", 5)):
    CONST[_n] = (_at, _w)
    _at += _w
CONST_W = _at
VEC = {}
_at = 0
for _n, _w in (("sink", 8), ("ssink", 2), ("balpha", 4), ("bgate", 16), ("normg", 8), ("brout", 36), ("embg", 8), ("embb", 8)):
    VEC[_n] = (_at, _w)
    _at += _w
VEC_W = _at

UNITS = [("p", j, pair) for j in range(4) for pair in range(4)] + [("s", bg, kv) for bg in range(2) for kv in range(2)]


def job_order():
    o = []
    for i in range(TILES):
        o += [(("hT", i, 0), "A"), (("hT", i, 1), "V")]
    o += [(("ga", x), "V") for x in range(2)]
    for n, g in (("la", 0), ("la", 1), ("q", 0), ("q", 1), ("la", 2), ("q", 2), ("la", 3), ("q", 3)):
        o += [((n, g, x), "A") for x in range(2)]
    o += [(("k", x), "A") for x in range(2)]
    o += [(("v", i), "V") for i in range(TILES)]
    o += [(("gq", g, x), "V") for g in range(GH) for x in range(2)]
    o += [(("gk", g, x), "V") for g in range(GH) for x in range(2)]
    o += [(("gv", x, i), "V") for x in (0, 2, 3) for i in range(TILES)]
    o += [(("ktok", 0), "V"), (("ktok", 1), "V")]
    o += [(("kbT", x), "A") for x in range(2)]
    n = len(UNITS)
    for u in range(n + 3):
        if u < n:
            o.append((("s", u), "V"))
        if 0 <= u - 2 < n:
            o.append((("pT", u - 2), "A"))
        if 0 <= u - 3 < n:
            o.append((("o", u - 3), "V"))
    for g in range(GH):
        o += [(("keT", g, 0), "A"), (("keT", g, 1), "A"), (("att", g), "V")]
        o += [(("U", g, c), "V") for c in range(-1, NCH)]
        if g == 0:
            o += [(("gv", 1, i), "V") for i in range(TILES)]
        if g:
            o += [(("gr", t, x), "A") for t in (g - 1, g + 3) for x in range(2)]
        o += [(("go", g, i), "A") for i in range(4)]
        o += [(("gso", g), "A")]
        o += [(("sU", g, x), "V") for x in range(4)]
    o += [(("gr", t, x), "A") for t in (3, 7) for x in range(2)]
    o += [(("yT", i, x), "V") for i in range(TILES) for x in range(2)]
    for y in range(4):
        for n, eng in (("gA", "A"), ("gB", "A"), ("bA", "V"), ("bB", "V")):
            o += [((n, m, x), eng) for m in (2 * y, 2 * y + 1) for x in range(2)]
    for i in range(TILES + 1):
        if i < TILES:
            o.append((("mix", 0, i), "V"))
        if i >= 2:
            o.append((("rt", i - 2), "V"))
        if i < TILES:
            o.append((("mix", 1, i), "V"))
        if i:
            o += [(("h1T", i - 1, 0), "A"), (("h1T", i - 1, 1), "A")]
    o.append((("rt", TILES - 1), "V"))
    o += [(("cnt",), "V"), (("pos",), "V"), (("lst",), "V")]
    return o


def weight_chunks():
    return ([("ga", ("ga", 1)), ("q0", ("q", 1, 1)), ("q1", ("q", 3, 1)), ("kv", ("v", 4)),
             ("gq0", ("gq", 1, 1)), ("gq1", ("gq", 3, 1)), ("gk0", ("gk", 1, 1)), ("gk1", ("gk", 3, 1))]
            + [(f"gv{x}", ("gv", x, 4)) for x in (0, 2, 3, 1)] + [(f"gr{x}", ("gr", x + 4, 1)) for x in range(4)]
            + [(n + str(y), (job, 2 * y + 1, 1)) for y in range(4)
               for n, job in (("gatesA", "gA"), ("gatesB", "gB"), ("brA", "bA"), ("brB", "bB"))])


def layout():
    at = {}
    top = 0
    for n, w in (("const", CONST_W), ("vec", VEC_W), ("lng", D), ("lnb", D), ("wrt", KC * 36), ("small", 256),
                 ("ring", (RING + 2) * SLOT), ("hT", KC * T), ("gq", GH * TQ), ("gk", GH * T), ("gv", TILES * D),
                 ("yaT", 4 * TQ), ("osb", TILES * D), ("R", 11200)):
        at[n] = top
        top += -(-w * 4 // 32) * 32
    at["end"] = top

    def inside(base, items):
        x = at[base]
        for n, w in items:
            at[n] = x
            x += -(-w * 4 // 32) * 32
        return x

    gla_end = inside("R", [("kem", 2 * 5 * P), ("am", 2 * 5 * 64), ("Sp", 9 * 256), ("s0", 8 * 256), ("kes", 8 * P),
                           ("qz", 576), ("junk", 256)])
    assert gla_end <= at["R"] + 4 * (11200 - 5 * T)
    at["hlo_r"] = at["R"] + 4 * (11200 - 5 * T)
    at["hlo_ln"] = at["lng"]
    e1 = inside("R", [("qT", 4 * SEQ), ("qs", 4 * NS), ("kT", T), ("v", TILES * P), ("vm", P), ("vn", 8 * P), ("ktok", 2 * P), ("X", 0)])
    assert inside("X", [("dx", 2 * T), ("dt", 2 * T), ("den", 2 * T)]) <= top
    assert inside("X", [("S", 3 * 512), ("PT", 3 * 512), ("sbk", 8 * P), ("sbv", 8 * P), ("kbT", 8 * P), ("stat", 3 * 16)]) <= top
    assert inside("R", [("sgA", 4 * HQ), ("sgB", 4 * HQ), ("ya_hi", 4 * TQ)]) <= top
    assert inside("R", [("h1", TILES * D), ("h1T", 8 * TQ)]) <= top
    at["gaT"] = at["yaT"]
    inside("yaT", [("rs", 4 * TQ)])
    inside("hT", [("wgu0", KC * 512)])
    assert inside("gq", [("wd0", 2048), ("wd1", 2048)]) <= at["gv"]
    inside("gv", [("wgu1", KC * 512)])
    assert SLOT == 2 * D
    inside("ring", [("XT", 2 * D), ("sil", 2 * F), ("act", 2 * F), ("aT", 2 * F)])
    at["Xg"], at["Yt"] = at["ring"] + 4 * 3 * SLOT, at["ring"] + 4 * 5 * SLOT
    inside("hT", [("y0", TILES * D)])
    inside("osb", [("y1", TILES * D)])
    return at


def decoder_kernel(nc, A, O):
    f32, i32 = mybir.dt.float32, mybir.dt.int32
    ALU, ACT, AX = mybir.AluOpType, mybir.ActivationFunctionType, mybir.AxisListType
    ORDER = job_order()
    INDEX = {k: n for n, (k, _) in enumerate(ORDER)}
    DRAINER = dict(ORDER)
    DRAINS = {}
    for eng in "AV":
        for n, k in enumerate([k for k, e in ORDER if e == eng]):
            DRAINS[k] = n + 1
    f32r = mybir.dt.float32r
    LAST_USE = weight_chunks()
    CHUNKS = [n for n, _ in LAST_USE]
    AT = layout()
    ctx = ExitStack()
    with ctx:
        arena_base = -(-nc.sbuf_base // 32) * 32
        ctx.enter_context(nc.sbuf_tensor("arena", [P, AT["end"] // 4], f32))

        views = []

        def sb(name, shape, dt=f32):
            n = 1
            for x in shape[1:]:
                n *= x
            views.append(name)
            ap = nc.alloc_sbuf_tensor_at(f"{name}_{len(views)}", [P, n], dt, offset=arena_base + AT[name])[:, :]
            if len(shape) == 3:
                ap = ap.rearrange("p (a b) -> p a b", b=shape[2])
            if len(shape) == 4:
                ap = ap.rearrange("p (a b c) -> p a b c", b=shape[2], c=shape[3])
            return ap

        def rounded(name, shape):
            return sb(name, shape, f32r)

        def sem(name):
            return ctx.enter_context(nc.semaphore(name))

        const = sb("const", [P, CONST_W])
        vec = sb("vec", [P, VEC_W])

        def cst(n):
            return const[:, CONST[n][0]:CONST[n][0] + CONST[n][1]]

        def vc(n):
            return vec[:, VEC[n][0]:VEC[n][0] + VEC[n][1]]

        ident, tri, ones = cst("ident"), cst("tri"), cst("ones")
        bias = cst("bias").rearrange("p (h k c) -> p h k c", h=4, k=2)
        sbias = cst("sbias").rearrange("p (k c) -> p k c", k=2)
        lng, lnb = sb("lng", [P, D]), sb("lnb", [P, D])
        wrt = sb("wrt", [P, KC, 36])
        small = sb("small", [P, 256])
        ring = sb("ring", [P, RING + 2, SLOT])
        hx = sb("osb", [P, KC, T])
        ring_r = rounded("ring", [P, RING + 2, SLOT])
        hT_hi, hT_lo = rounded("hT", [P, KC, T]), rounded("osb", [P, KC, T])
        lo_r, lo_ln = rounded("hlo_r", [P, 5, T]), rounded("hlo_ln", [P, 3, T])
        gq, gk = sb("gq", [P, GH, TQ]), sb("gk", [P, GH, T])
        sg = sb("gq", [P, 8, TQ])
        gv = sb("gv", [P, TILES, D])
        yg_hi, yg_lo = rounded("gv", [P, 8, TQ]), rounded("gq", [P, 8, TQ])
        h, osb, mixT = sb("gv", [P, TILES, D]), sb("osb", [P, TILES, D]), sb("osb", [P, 8, TQ])
        h1T = sb("h1T", [P, 8, TQ])
        yaT = sb("yaT", [P, 4, TQ])
        ya_hi, ya_lo = rounded("ya_hi", [P, 4, TQ]), rounded("yaT", [P, 4, TQ])
        qs = sb("qs", [P, NB_S, 4 * T_S])
        qT, kT, v, vm = sb("qT", [P, 4, SEQ]), sb("kT", [P, T]), sb("v", [P, TILES, P]), sb("vm", [P, P])
        vn, ktok = sb("vn", [P, 8, P]), sb("ktok", [P, 2, P])
        gaT = sb("gaT", [P, T])
        dx, dt_, den = sb("dx", [P, 2, T]), sb("dt", [P, 2, T]), sb("den", [P, 2, T])
        S, PT = sb("S", [P, 3, 512]), sb("PT", [P, 3, 4 * P])
        sbk, sbv, kbT = sb("sbk", [P, 8, P]), sb("sbv", [P, 8, P]), sb("kbT", [P, 8, P])
        stat = sb("stat", [P, 3, 16])
        kem, am = sb("kem", [P, 2, 5, P]), sb("am", [P, 2, 5 * 64])
        Sp, s0, kes = sb("Sp", [P, 9, 256]), sb("s0", [P, 8, 256]), sb("kes", [P, 8, P])
        qz, junk = sb("qz", [P, 576]), sb("junk", [P, 256])
        sgA, sgB = sb("sgA", [P, 4, HQ]), sb("sgB", [P, 4, HQ])
        h1 = sb("h1", [P, TILES, D])
        fin, em = small[:, 0:68].rearrange("p (g c) -> p g c", c=17), small[:, 68:104].rearrange("p (g c) -> p g c", c=9)
        ss, rr = small[:, 104:124], small[:, 124:144]
        bst = small[:, 144:144 + 60].rearrange("p (i c) -> p i c", c=12)
        mv = small[:, 204:214].rearrange("p (i c) -> p i c", c=2)
        rstd = small[:, 214:224]
        epsc = small[:, 224:225]
        wgu = [sb("wgu0", [P, KC, 512]), sb("wgu1", [P, KC, 512])]
        wd = [sb("wd0", [P, 2, D]), sb("wd1", [P, 2, D])]
        Xg, XT, Yt = sb("Xg", [P, 2, D]), sb("XT", [P, 2, KC, P]), sb("Yt", [P, 2, D])
        sil, act_, aT = sb("sil", [P, 2, F]), sb("act", [P, 2, F]), sb("aT", [P, 2, 2, P])
        tb = ctx.enter_context(nc.sbuf_tensor("tb", [P, MAX_TILES, 4], i32))
        w2 = ctx.enter_context(nc.sbuf_tensor("w2", [RANK, GH * HK], f32))
        y0, y1 = sb("y0", [P, TILES, D]), sb("y1", [P, TILES, D])
        lst = ctx.enter_context(nc.sbuf_tensor("lst", [1, 132], i32))
        idx = ctx.enter_context(nc.sbuf_tensor("idx", [P, 4, 4], i32))
        wsel = ctx.enter_context(nc.sbuf_tensor("wsel", [P, 2], f32))
        ent = ctx.enter_context(nc.sbuf_tensor("ent", [P, 2 * TILES, 4], i32))
        rowi = ctx.enter_context(nc.sbuf_tensor("rowi", [P, 2 * TILES], i32))

        rs_off = [0]
        rs_base = sb("rs", [P, 4 * TQ])

        def scratch(n):
            o = rs_off[0]
            rs_off[0] += n
            assert rs_off[0] <= 4 * TQ
            return rs_base[:, o:o + n]

        R = {}
        for n, w in (("lg", 5 * 36), ("gmax", 5), ("gt", 20), ("gmin", 5), ("goh", 20), ("eg", 20), ("gsum", 5),
                     ("pr", 160), ("ein", 40), ("m1", 5), ("t8", 40), ("mn", 5), ("oh1", 40), ("oh2", 40), ("m2", 5),
                     ("ex", 5), ("w1", 5), ("w2", 5), ("M1", 160), ("M2", 160), ("M", 160), ("cnt", 32), ("nt", 32),
                     ("inc", 32), ("Mp", 192), ("pos", 160), ("q", 160), ("t160", 160), ("r1", 10), ("eg1", 1), ("t5", 5)):
            R[n] = scratch(w)

        psum = [ctx.enter_context(nc.psum_tensor(f"bank{n}", [P, 512], f32)) for n in range(NBANK)]

        def bank(key):
            return psum[INDEX[key] % NBANK]

        tbl_d = nc.dram_tensor("slot_table", [P * MAX_TILES, 4], i32, kind="Internal").ap()
        h_d = nc.dram_tensor("h_spill", [TILES * P, D], f32, kind="Internal").ap()
        h1_d = nc.dram_tensor("h1_rows", [TQ, D], f32, kind="Internal").ap()
        y_d = nc.dram_tensor("expert_rows", [2 * TQ, D], f32, kind="Internal").ap()

        w2_in = sem("w2_in")
        h_scaled = sem("h_scaled")
        xn_ready = sem("xn_ready")
        y_part = sem("y_part")
        y_sum = sem("y_sum")
        y_sq = sem("y_sq")
        y_scale = sem("y_scale")
        y_xn = sem("y_xn")
        y_g = sem("y_g")
        h1_scaled = sem("h1_scaled")
        wrt_in = sem("wrt_in")
        pool_held = sem("pool_held")
        x_in = [sem(f"x_in{i}") for i in range(TILES)]
        const_in = sem("const_in")
        tables_in = sem("tables_in")
        ln_in = sem("ln_in")
        wchunk = [sem(f"wchunk{n}") for n in range(RING)]
        psum_full = sem("psum_full")
        act_drained = sem("act_drained")
        dve_drained = sem("dve_drained")
        dve_chain = sem("dve_chain")
        act_chain = sem("act_chain")
        ln_var = sem("ln_var")
        ln_std = sem("ln_std")
        h_hi = sem("h_hi")
        h_split = sem("h_split")
        h_split2 = sem("h_split2")
        h_hi2 = sem("h_hi2")
        w_hi = sem("w_hi")
        w_split = sem("w_split")
        lo_moved = sem("lo_moved")
        state_scaled = sem("state_scaled")
        yg_high = sem("yg_high")
        yg_split = sem("yg_split")
        ya_high = sem("ya_high")
        ya_split = sem("ya_split")
        wo_in = [sem("wo_in0"), sem("wo_in1")]
        spilled = sem("spilled")
        h_back = sem("h_back")
        log_ready = sem("log_ready")
        dec_ready = sem("dec_ready")
        exp_ready = sem("exp_ready")
        qk_ready = sem("qk_ready")
        state_in = sem("state_in")
        rows_moved = sem("rows_moved")
        max_ready = sem("max_ready")
        p_exp = sem("p_exp")
        p_norm = sem("p_norm")
        s0_in = sem("s0_in")
        s0_out = sem("s0_out")
        sp_out = sem("sp_out")
        kes_ready = sem("kes_ready")
        ss_ready = sem("ss_ready")
        rms_ready = sem("rms_ready")
        sp_final = sem("sp_final")
        s0_final = sem("s0_final")
        y_norm = sem("y_norm")
        h1_ready = sem("h1_ready")
        h1_stored = sem("h1_stored")
        tbl_init = sem("tbl_init")
        pad_ready = sem("pad_ready")
        rt_exp_in = sem("rt_exp_in")
        rt_exp = sem("rt_exp")
        mask_ready = sem("mask_ready")
        ids_ready = sem("ids_ready")
        rows_ready = sem("rows_ready")
        list_ready = sem("list_ready")
        scattered = sem("scattered")
        tb_in = sem("tb_in")
        wg_in = [sem(f"wg_in{n}") for n in range(2)]
        wd_in = [sem(f"wd_in{n}") for n in range(2)]
        gathered = [sem(f"gathered{n}") for n in range(2)]
        y_sent = [sem(f"y_sent{n}") for n in range(2)]
        gidx_ready, sidx_ready = sem("gidx_ready"), sem("sidx_ready")
        xt_full, gu_full, at_full, dn_full = sem("xt_full"), sem("gu_full"), sem("at_full"), sem("dn_full")
        xt_act, xt_dve = sem("xt_act"), sem("xt_dve")
        silu_done, act_done, at_done = sem("silu_done"), sem("act_done"), sem("at_done")
        w_ready = sem("w_ready")
        dn_act, dn_dve = sem("dn_act"), sem("dn_dve")
        y_back = [sem(f"y_back{i}") for i in range(TILES)]
        y_out = sem("y_out")
        out_done = sem("out_done")
        y_ready, y_ready2 = sem("y_ready"), sem("y_ready2")
        loop_done = sem("loop_done")
        x_zero = sem("x_zero")
        OUTS = [0]

        block = ctx.enter_context(nc.Block())

        def wait_job(eng, key):
            eng.wait_ge(act_drained if DRAINER[key] == "A" else dve_drained, DRAINS[key])

        def wait_inputs(eng):
            for i in range(TILES):
                eng.wait_ge(x_in[i], 32 if i == TILES - 1 else 16)

        def wait_full(eng, key):
            eng.wait_ge(psum_full, INDEX[key] + 1)

        def chunk_parts(n):
            slot = ring[:, CHUNKS.index(n) % RING, :]
            w_in = A["w_in"][0].rearrange("(k p) n -> p k n", p=P)
            place = slot.rearrange("p (k n) -> p k n", n=256)
            y = int(n[-1]) if n[-1].isdigit() else 0
            x = 256 * y
            if n[0] == "q":
                return place, [(place, A["w_q"].rearrange("(k p) n -> p k n", p=P)[:, :, x:x + 256])]
            if n == "ga":
                place = slot[:, 0:KC * RANK].rearrange("p (k n) -> p k n", n=RANK)
                return place, [(place, w_in[:, :, C_GA:C_GA + RANK])]
            cols = {"kv": C_K, "gq": C_GQ, "gk": C_GK, "gv": C_GV, "gatesA": C_GATE, "gatesB": C_GATE + D}
            name = n if n == "kv" else n[:-1]
            if name == "gr":
                return place, [(place[:, :, P * i:P * i + P], w_in[:, :, C_GR + P * (y + 4 * i):C_GR + P * (y + 4 * i) + P])
                               for i in range(2)]
            if name in cols:
                return place, [(place, w_in[:, :, cols[name] + x:cols[name] + x + 256])]
            if name == "brB":
                return place, [(place, A["w_gla_br"][0].rearrange("(k p) n -> p k n", p=P)[:, :, x:x + 256])]
            wa = A["w_attn_br"][0].rearrange("(v t p) n -> v p t n", v=2, p=HD)
            return place[:, 0:4, :], [(place[HD * kv:HD * kv + HD, 0:4, :], wa[kv][:, :, x:x + 256]) for kv in range(2)]

        def chunk(n):
            return chunk_parts(n)[0]

        def flat(n):
            w = KC * RANK if n == "ga" else 4 * 256 if n[:3] == "brA" else SLOT
            c = CHUNKS.index(n) % RING
            return ring[:, c, 0:w], ring_r[:, c, 0:w], ring_r[:, RING + CHUNKS.index(n) % 2, 0:w]

        def parts(n):
            w = RANK if n == "ga" else 256
            _, low, high = flat(n)
            return [ap.rearrange("p (k n) -> p k n", n=w) for ap in (high, low)]

        def wait_split(eng, n):
            eng.wait_ge(w_split, CHUNKS.index(n) + 1)

        wo_places = [[ring[:, 0, :], ring[:, 1, :]], [ring[:, 2, :], ring[:, RING, :]]]

        def wo(x, kc):
            return wo_places[x][kc // 4][:, kc % 4 * 512:kc % 4 * 512 + 512]

        def wait_chunk(eng, n):
            c = CHUNKS.index(n)
            total = sum(len(chunk_parts(m)[1]) for k, m in enumerate(CHUNKS[:c + 1]) if k % RING == c % RING)
            eng.wait_ge(wchunk[c % RING], 16 * total)

        @block.sync
        def _(sp):
            def wo_half_in(x):
                w = A["w_out"][0].rearrange("(k p) n -> p k n", p=P)[:, :, 512 * x:512 * x + 512]
                for i in range(2):
                    sp.dma_start(wo_places[x][i].rearrange("p (k n) -> p k n", n=512), w[:, 4 * i:4 * i + 4, :])\
                      .then_inc(wo_in[x], 16)

            for c, n in enumerate(CHUNKS):
                if c == 1:
                    wait_inputs(sp)
                if c >= RING:
                    wait_full(sp, LAST_USE[c - RING][1])
                for place, src in chunk_parts(n)[1]:
                    sp.dma_start(place, src).then_inc(wchunk[c % RING], 16)
                if n == "q0":
                    sp.dma_start(const[:, 384:CONST_W], A["const"][:, 384:CONST_W]).then_inc(tables_in, 16)
            wait_full(sp, ("gB", 7, 1))
            wo_half_in(0)
            wait_full(sp, ("bA", 7, 1))
            wo_half_in(1)

            def gate_up_in(e, s):
                for half, w in enumerate(("w_exp_gate", "w_exp_up")):
                    sp.dma_start(wgu[s][:, :, half * F:half * F + F],
                                 A[w][0][e, :, :].rearrange("e (p k) f -> p (e k) f", p=P)).then_inc(wg_in[s], 16)

            def down_in(e, s):
                sp.dma_start(wd[s][:, :, :], A["w_exp_down"][0][e, :, :].rearrange("e (p k) n -> p (e k) n", p=P))\
                  .then_inc(wd_in[s], 16)

            def expert_of(g):
                return bass.ds(sp.value_load(lst[0:1, bass.ds(g, 1)], min_val=0, max_val=N_EXP - 1), 1)

            def step(g, s, more):
                here, after = expert_of(g), expert_of(g + 1)
                if more:
                    sp.wait_ge(gu_full, g)
                    gate_up_in(after, 1 - s)
                sp.wait_ge(dn_full, g)
                down_in(here, s)

            wait_full(sp, ("bB", 7, 1))
            sp.wait_ge(h_back, 16 * TILES)
            for s in range(2):
                gate_up_in(slice(s, s + 1), s)
                down_in(slice(s, s + 1), s)
            sp.wait_ge(gu_full, 1)
            gate_up_in(slice(2, 3), 0)
            sp.wait_ge(list_ready, 1)
            last = sp.value_load(lst[0:1, 128:129], min_val=N_EXP - 2, max_val=MAX_TILES - 4)
            with sp.Fori(2, last, 2) as g0:
                for s in range(2):
                    step(g0 + s, s, True)
            step(last, 0, True)
            step(last + 1, 1, False)
            sp.wait_ge(loop_done, 1)
            for i in range(TILES):
                r = ROWS[i]
                sp.dma_start(y0[0:r, i, :], y_d[i * P:i * P + r, :]).then_inc(y_back[i], 16)
                sp.dma_start(y1[0:r, i, :], y_d[TQ + i * P:TQ + i * P + r, :]).then_inc(y_back[i], 16)
            for i in range(TILES):
                sp.wait_ge(*((y_ready, i + 1) if i < 3 else (y_ready2, i - 2)))
                dst = O[0][0, i * P:i * P + P, :] if i < 4 else O[1].rearrange("b t d -> (b t) d")
                sp.dma_start(dst, h1[0:ROWS[i], i, :]).then_inc(y_out, 16)
            sp.wait_ge(y_out, 16 * TILES)

        def earlier(b):
            return b * 8

        @block.gpsimd
        def _(pool):
            pool.memset(tb[:, :, :], PAD_ROW).then_inc(pad_ready, 1)
            wait_inputs(pool)
            pool.dma_start(w2[:, :], A["w_alpha2"][0]).then_inc(w2_in, 16)
            pool.dma_start(lng, A["ln_emb_g"].partition_broadcast(P)).then_inc(ln_in, 16)
            pool.dma_start(lnb, A["ln_emb_b"].partition_broadcast(P)).then_inc(ln_in, 16)
            for i in range(TILES):
                cols = slice(i * P, i * P + ROWS_ALL[i])
                pool.wait_ge(h_hi2, i + 1)
                pool.tensor_tensor(hT_lo[:, 4:8, cols], hx[:, 4:8, cols], hT_hi[:, 4:8, cols], ALU.subtract)\
                    .then_inc(h_split2, 1)
            pool.wait_ge(ln_in, 32)
            for i in range(TILES):
                r = ROWS[i]
                wait_full(pool, ("hT", i, 1))
                pool.tensor_tensor(h[0:r, i, :], h[0:r, i, :], lng[0:r, :], ALU.mult).then_inc(h_scaled, 1)
                pool.wait_ge(h_scaled, 2 * i + 1)
                pool.tensor_tensor(h[0:r, i, :], h[0:r, i, :], lnb[0:r, :], ALU.add).then_inc(h_scaled, 1)
                pool.wait_ge(h_scaled, 2 * i + 2)
                pool.dma_start(h_d[i * P:i * P + r, :], h[0:r, i, :]).then_inc(spilled, 16)
            pool.wait_ge(pad_ready, 1)
            pool.dma_start(tbl_d.rearrange("(p g) c -> p g c", p=P), tb[:, :, :]).then_inc(tbl_init, 16)
            pool.dma_start(wrt[:, :, 0:4], A["w_router_group"][0].rearrange("(k p) n -> p k n", p=P)).then_inc(wrt_in, 16)
            pool.dma_start(wrt[:, :, 4:36], A["w_router_expert"][0].rearrange("(k p) n -> p k n", p=P)).then_inc(wrt_in, 16)
            for b in range(2):
                k, vv = (("state_swa_k", 5), ("state_swa_v", 6))[b]
                s_in = A[k][0]
                pool.dma_start(O[vv][0][:, 0:WINDOW - T_S], s_in[:, T_S:WINDOW]).then_inc(out_done, 16)
                OUTS[0] += 1
            wait_job(pool, ("v", 4))
            pool.dma_start(vm[0:N_META, :], v[NS:NS + N_META, 4, :]).then_inc(rows_moved, 16)
            for b in range(8):
                pool.dma_start(vn[0:T_S, b, :], v[b * T_S:b * T_S + T_S, 4, :]).then_inc(rows_moved, 16)
            wait_job(pool, ("v", 3))
            pool.dma_start(O[3][0, 0].rearrange("t k d -> t (k d)"), v[:, 3, :]).then_inc(out_done, 16)
            pool.dma_start(O[6][0][:, WINDOW - T_S:WINDOW].rearrange("b t k d -> b t (k d)"), v[0:NS, 4, :])\
                .then_inc(out_done, 16)
            pool.wait_ge(qk_ready, GH)
            pool.dma_start(sbk[:, :, :], A["state_swa_k"][0].rearrange("b s k d -> s b (k d)")).then_inc(state_in, 16)
            pool.dma_start(sbv[:, :, :], A["state_swa_v"][0].rearrange("b s k d -> s b (k d)")).then_inc(state_in, 16)
            wait_job(pool, ("ktok", 1))
            pool.dma_start(O[2][0, 0].rearrange("t k d -> t (k d)"), ktok[:, 0, :]).then_inc(out_done, 16)
            pool.dma_start(O[5][0][:, WINDOW - T_S:WINDOW].rearrange("b t k d -> b t (k d)"), ktok[0:NS, 1, :])\
                .then_inc(out_done, 16)
            OUTS[0] += 4
            wait_job(pool, ("o", 19))
            pool.wait_ge(out_done, 16 * OUTS[0])
            for g in range(GH):
                if g:
                    pool.wait_ge(s0_out, 16 * g)
                pool.dma_start(s0[:, :, :], A["state_gla"][0][:, g].rearrange("b k v -> k b v")).then_inc(s0_in, 16)
                pool.wait_ge(sp_final, g + 1)
                pool.dma_start(O[4][0, 0, g], Sp[:, 8, :]).then_inc(sp_out, 16)
                for x in range(4):
                    wait_job(pool, ("sU", g, x))
                    sv = s0[:, 2 * x:2 * x + 2, :]
                    pool.tensor_tensor(sv, sv, fin[:, g, 8 + 2 * x:10 + 2 * x].rearrange("p (b c) -> p b c", c=1)
                                       .broadcast_to([P, 2, HV]), ALU.mult).then_inc(s0_final, 1)
                pool.wait_ge(s0_final, 4 * (g + 1))
                pool.dma_start(O[7][0][:, g].rearrange("b k v -> k b v"), s0[:, :, :]).then_inc(s0_out, 16)
            wait_full(pool, ("gB", 7, 1))
            pool.dma_start(lng, A["ln1_g"][0].partition_broadcast(P)).then_inc(ln_in, 16)
            pool.dma_start(lnb, A["ln1_b"][0].partition_broadcast(P)).then_inc(ln_in, 16)
            wait_job(pool, ("bB", 7, 1))
            for i in range(TILES):
                pool.dma_start(h1[0:ROWS[i], i, :], h_d[i * P:i * P + ROWS[i], :]).then_inc(h_back, 16)
            pool.memset(Xg[:, :, :], 0.0).then_inc(x_zero, 1)
            pool.memset(idx[:, :, :], PAD_ROW).then_inc(x_zero, 1)
            pool.memset(Yt[:, :, :], 0.0).then_inc(x_zero, 1)
            pool.wait_ge(x_zero, 3)
            for s in range(2):
                pool.indirect_dma_start(out=y_d[:, :], out_offset=bass.IndirectOffsetOnAxis(ap=idx[:, 2 + s, 1:2], axis=0),
                                        in_=Yt[:, s, :], in_offset=None,
                                        bounds_check=2 * TQ - 1, oob_is_err=False).then_inc(y_sent[s], 16)
            for i in range(TILES):
                pool.wait_ge(h1_ready, i + 1)
                pool.dma_start(h1_d[i * P:i * P + ROWS[i], :], h1[0:ROWS[i], i, :]).then_inc(h1_stored, 16)
            pool.dma_start(lng, A["ln2_g"][0].partition_broadcast(P)).then_inc(ln_in, 16)
            pool.dma_start(lnb, A["ln2_b"][0].partition_broadcast(P)).then_inc(ln_in, 16)
            pool.wait_ge(tbl_init, 16)
            for n in range(2 * TILES):
                pool.wait_ge(rows_ready, n // TILES + 1)
                r = ROWS[n % TILES]
                pool.indirect_dma_start(out=tbl_d[:, :], out_offset=bass.IndirectOffsetOnAxis(ap=rowi[0:r, n:n + 1], axis=0),
                                        in_=ent[0:r, n, :], in_offset=None).then_inc(scattered, 16)
            pool.wait_ge(scattered, 16 * 2 * TILES)
            pool.dma_start(tb[:, :, :], tbl_d.rearrange("(p g) c -> p g c", p=P)).then_inc(tb_in, 16)
            pool.wait_ge(tb_in, 16)
            pool.wait_ge(h1_stored, 16 * TILES)

            def hold():
                pool.sem_inc(pool_held, 1)

            def gather(g, s):
                pool.tensor_copy(idx[:, s:s + 1, :], tb[:, bass.ds(g, 1), :]).then_inc(gidx_ready, 1)
                pool.wait_ge(gidx_ready, g + 1)
                hold()
                pool.indirect_dma_start(out=Xg[:, s, :], out_offset=None, in_=h1_d[:, :],
                                        in_offset=bass.IndirectOffsetOnAxis(ap=idx[:, s, 0:1], axis=0),
                                        bounds_check=TQ - 1, oob_is_err=False).then_inc(gathered[s], 16)

            def send(b, s):
                g = b + s
                pool.wait_ge(y_sent[s], earlier(b) + 16)
                hold()
                pool.tensor_copy(idx[:, 2 + s:3 + s, :], tb[:, bass.ds(g, 1), :]).then_inc(sidx_ready, 1)
                pool.wait_ge(sidx_ready, g + 1)
                pool.wait_ge(dn_act, g + 2)
                pool.wait_ge(dn_dve, g + 2)
                hold()
                pool.indirect_dma_start(out=y_d[:, :], out_offset=bass.IndirectOffsetOnAxis(ap=idx[:, 2 + s, 1:2], axis=0),
                                        in_=Yt[:, s, :], in_offset=None,
                                        bounds_check=2 * TQ - 1, oob_is_err=False).then_inc(y_sent[s], 16)

            gather(0, 0)
            gather(1, 1)
            pool.wait_ge(xt_full, 1)
            gather(2, 0)
            last = pool.value_load(lst[0:1, 128:129], min_val=N_EXP - 2, max_val=MAX_TILES - 4)
            with pool.Fori(0, last, 2) as g0:
                for s in range(2):
                    pool.wait_ge(xt_full, g0 + s + 2)
                    hold()
                    gather(g0 + s + 3, 1 - s)
                    send(g0, s)
            for s in range(2):
                send(last, s)
            pool.wait_ge(gathered[0], earlier(last) + 32)
            hold()
            for s in range(2):
                pool.wait_ge(y_sent[s], earlier(last) + 32)
                hold()
            pool.sem_inc(loop_done, 1)
            for i in range(TILES):
                r = ROWS[i]
                pool.wait_ge(y_back[i], 32)
                pool.tensor_tensor(y0[0:r, i, :], y0[0:r, i, :], y1[0:r, i, :], ALU.add).then_inc(y_part, 1)
            for i in range(3):
                r = ROWS[i]
                pool.wait_ge(y_g, i + 1)
                pool.tensor_tensor(h1[0:r, i, :], h1[0:r, i, :], lnb[0:r, :], ALU.add).then_inc(y_ready, 1)
            pool.wait_ge(out_done, 16 * OUTS[0])
            pool.wait_ge(sp_out, 16 * GH)
            pool.wait_ge(s0_out, 16 * GH)

        @block.scalar
        def _(act):
            chain = [0]

            def link(ins):
                chain[0] += 1
                ins.then_inc(act_chain, 1)
                act.wait_ge(act_chain, chain[0])

            for i in range(TILES):
                if i < 4:
                    act.dma_start(h[:, i, :], A["x_prompt"][0, i * P:i * P + P, :]).then_inc(x_in[i], 16)
                else:
                    act.dma_start(h[0:NS, i, :], A["x_sample"].rearrange("b t d -> (b t) d")).then_inc(x_in[i], 16)
                    act.dma_start(h[NS:NS + N_META, i, :], A["meta_tokens"]).then_inc(x_in[i], 16)
            act.dma_start(const[:, 0:384], A["const"][:, 0:384]).then_inc(const_in, 16)
            act.dma_start(vec, A["vec"]).then_inc(const_in, 16)

            def drain(key, out, in_, **kw):
                func = kw.pop("func", ACT.Copy)
                wait_full(act, key)
                act.activation(out, in_, func, **kw).then_inc(act_drained, 1)

            def std(n, i):
                act.wait_ge(ln_var, TILES * n + i + 1)
                act.activation(rstd[:, 5 + i:6 + i], rstd[:, i:i + 1], ACT.Sqrt).then_inc(ln_std, 1)

            for i in range(TILES):
                std(0, i)
            act.wait_ge(const_in, 16 * 2)
            def high(n):
                k = CHUNKS.index(n)
                wait_chunk(act, n)
                if k >= 2:
                    wait_full(act, dict(LAST_USE)[CHUNKS[k - 2]])
                src, _, dst = flat(n)
                act.activation(dst, src, ACT.Copy).then_inc(w_hi, 1)

            for i in range(TILES):
                r = ROWS_ALL[i]
                wait_full(act, ("hT", i, 0))
                for k in range(4):
                    ins = act.activation(hx[:, k, i * P:i * P + r], bank(("hT", i, 0))[:, k * P:k * P + r], ACT.Identity,
                                         scale=vc("embg")[:, k:k + 1], bias=vc("embb")[:, k:k + 1])
                ins.then_inc(act_drained, 1)
                wait_job(act, ("hT", i, 0))
                act.activation(hT_hi[:, 0:4, i * P:i * P + r], hx[:, 0:4, i * P:i * P + r], ACT.Copy).then_inc(h_hi, 1)
                if i == 2:
                    high("ga")
            high("q0")

            def drain_q(t):
                drain(("q", t, 0), qT[:, t, 0:HQ], bank(("q", t, 0))[:, 0:HQ], scale=HD ** -0.5)
                wait_full(act, ("q", t, 1))
                act.activation(qT[:, t, HQ:SEQ], bank(("q", t, 1))[:, 0:SEQ - HQ], ACT.Copy, scale=HD ** -0.5)
                act.activation(qs[:, :, t * T_S:t * T_S + T_S],
                               bank(("q", t, 1))[:, SEQ - HQ:HQ].rearrange("p (b t) -> p b t", t=T_S), ACT.Copy,
                               scale=HD ** -0.5).then_inc(act_drained, 1)

            def exps(g):
                b = g % 2
                act.wait_ge(dec_ready, g + 1)
                act.activation(em[:, g, 0:8], dt_[:, b, 31:512:64], ACT.Exp, scale=1 / 16.0)
                link(act.activation(em[:, g, 8:9], dt_[:, b, TQ + 7:TQ + 8], ACT.Exp, scale=1 / 16.0))
                act.activation(den[:, b, :], dx[:, b, :], ACT.Exp, scale=-1 / 16.0)
                act.activation(dt_[:, b, :], dx[:, b, :], ACT.Exp, scale=1 / 16.0).then_inc(exp_ready, 1)

            def logs(g):
                b = g % 2
                if g >= 2:
                    act.wait_ge(qk_ready, g - 1)
                for x in range(2):
                    key = ("la", g, x)
                    wait_full(act, key)
                    act.activation(dx[:, b, x * HA:x * HA + HA], bank(key)[:, 0:HA], ACT.Identity,
                                   bias=vc("balpha")[:, g:g + 1]).then_inc(act_drained, 1)
                act.wait_ge(act_drained, DRAINS[("la", g, 1)])
                link(act.activation(dt_[:, b, :], dx[:, b, :], ACT.Abs))
                link(act.activation(dt_[:, b, :], dt_[:, b, :], ACT.Exp, scale=-1.0))
                act.activation(dt_[:, b, :], dt_[:, b, :], ACT.Ln, bias=1.0).then_inc(log_ready, 1)

            logs(0)
            high("q1")
            logs(1)
            exps(0)
            drain_q(0)
            exps(1)
            drain_q(1)
            high("kv")
            logs(2)
            drain_q(2)
            exps(2)
            logs(3)
            drain_q(3)
            exps(3)
            high("gq0")
            for x in range(2):
                drain(("k", x), kT[:, x * HA:x * HA + HA], bank(("k", x))[:, 0:HA])
            for n in ("gq1", "gk0", "gk1", "gv0", "gv2", "gv3", "gv1", "gr0"):
                high(n)
            for x in range(2):
                drain(("kbT", x), kbT[:, 4 * x:4 * x + 4, :], bank(("kbT", x))[:, :].rearrange("p (k c) -> p k c", k=4))

            n = len(UNITS)
            for u in range(n + 2):
                if u < n:
                    kind, a, b = UNITS[u]
                    st = stat[:, u % 3, :]
                    act.wait_ge(max_ready, u + 1)
                    if kind == "p":
                        lo = 0 if a else WINDOW - N_META
                        for kv in range(2):
                            pv = S[:, u % 3, kv * 256 + lo:kv * 256 + 256]
                            act.activation(pv, pv, ACT.Exp, bias=st[:, 2 + kv:3 + kv], accum_out=st[:, 6 + kv:7 + kv])
                        act.activation(st[:, 8:10], st[:, 4:6], ACT.Exp).then_inc(p_exp, 1)
                    else:
                        pv = S[:, u % 3, 0:136]
                        act.activation(pv, pv, ACT.Exp, bias=st[:, 2:3], accum_out=st[:, 6:7])
                        act.activation(st[:, 8:9], st[:, 4:5], ACT.Exp).then_inc(p_exp, 1)
                w = u - 2
                if 0 <= w < n:
                    kind, a, b = UNITS[w]
                    key = ("pT", w)
                    wait_full(act, key)
                    bk = bank(key)[:, :].rearrange("p (a c) -> p a c", a=4)
                    pt = PT[:, w % 3, :].rearrange("p (a c) -> p a c", a=4)
                    if kind == "p" and a:
                        act.activation(pt, bk, ACT.Copy).then_inc(act_drained, 1)
                    elif kind == "p":
                        act.activation(pt[0:N_META, 0:3:2], bk[0:N_META, 0:3:2], ACT.Copy)
                        act.activation(pt[:, 1:4:2], bk[:, 1:4:2], ACT.Copy).then_inc(act_drained, 1)
                    else:
                        act.activation(pt[0:T_S, 1], bk[0:T_S, 1], ACT.Copy)
                        act.activation(pt[:, 0], bk[:, 0], ACT.Copy).then_inc(act_drained, 1)

            wait_job(act, ("o", 19))
            act.wait_ge(out_done, 16 * 6)
            act.wait_ge(spilled, 16 * TILES)

            def output_gate(t):
                for x in range(2):
                    drain(("gr", t, x), sg[:, t, x * HQ:x * HQ + HQ], bank(("gr", t, x))[:, 0:HQ], func=ACT.Silu)

            for g in range(GH):
                if g >= 2:
                    act.wait_ge(kes_ready, g - 1)
                drain(("keT", g, 0), kem[:, g % 2, 0:4, :], bank(("keT", g, 0))[:, :].rearrange("p (k c) -> p k c", k=4))
                r = ROWS_ALL[4]
                drain(("keT", g, 1), kem[0:r, g % 2, 4, :], bank(("keT", g, 1))[0:r, 0:P])
                if g == 0:
                    act.activation(lo_r, hT_lo[:, 0:5, :], ACT.Copy)
                    act.activation(lo_ln, hT_lo[:, 5:8, :], ACT.Copy).then_inc(lo_moved, 1)
                    act.wait_ge(lo_moved, 1)
                if g:
                    output_gate(g - 1)
                    output_gate(g + 3)
                high(("gr1", "gr2", "gr3", "gatesA0")[g])
                for i in range(5):
                    key = ("go", g, i) if i < 4 else ("gso", g)
                    r = ROWS[i]
                    drain(key, osb[0:r, i, g * HV:g * HV + HV], bank(key)[0:r, 0:HV])
                    act.wait_ge(act_drained, DRAINS[key])
                    ins = act.activation(junk[0:r, :], osb[0:r, i, g * HV:g * HV + HV], ACT.Square,
                                         accum_out=ss[0:r, 4 * i + g:4 * i + g + 1])
            ins.then_inc(ss_ready, 1)
            act.wait_ge(rms_ready, 1)
            act.activation(rr[:, :], rr[:, :], ACT.Sqrt).then_inc(ss_ready, 1)
            output_gate(3)
            output_gate(7)
            high("gatesB0")
            for i in range(TILES):
                cols = slice(i * P, i * P + ROWS[i])
                wait_job(act, ("yT", i, 1))
                act.activation(yg_hi[:, :, cols], sg[:, :, cols], ACT.Copy).then_inc(yg_high, 1)
            act.wait_ge(sp_out, 16 * GH)
            act.wait_ge(s0_out, 16 * GH)
            act.activation(ya_hi, yaT, ACT.Copy).then_inc(ya_high, 1)
            for y in range(4):
                if y:
                    high(f"gatesB{y}")
                for name, dst, o in (("gA", sgA, 0), ("gB", sgB, 8)):
                    for n in range(4):
                        m, x = 2 * y + n // 2, n % 2
                        if y:
                            wait_job(act, ("bB", m - 2, x))
                        drain((name, m, x), dst[:, n, :], bank((name, m, x))[:, 0:HQ], func=ACT.Sigmoid,
                              bias=vc("bgate")[:, o + m:o + m + 1])
                    high(f"br{name[1]}{y}")
                if y < 3:
                    high(f"gatesA{y + 1}")
            for i in range(TILES + 1):
                if i:
                    r = ROWS[i - 1]
                    for x in range(2):
                        drain(("h1T", i - 1, x), h1T[:, 4 * x:4 * x + 4, (i - 1) * P:(i - 1) * P + r],
                              bank(("h1T", i - 1, x))[:, :].rearrange("p (k c) -> p k c", k=4)[:, :, 0:r])
                if i < TILES:
                    std(1, i)
            act.wait_ge(rt_exp_in, 1)
            act.activation(R["eg"], R["eg"], ACT.Exp)
            act.activation(R["ex"], R["ex"], ACT.Exp).then_inc(rt_exp, 1)

            act.wait_ge(list_ready, 1)
            last = act.value_load(lst[0:1, 128:129], min_val=N_EXP - 2, max_val=MAX_TILES - 4)

            def drain_xt(g, s):
                act.wait_ge(xt_full, g + 1)
                act.activation(XT[:, s, 0:4, :], psum[0][:, :].rearrange("p (k c) -> p k c", k=4), ACT.Copy)\
                   .then_inc(xt_act, 1)

            def silu(g, s):
                act.wait_ge(gu_full, g + 1)
                act.activation(sil[:, s, :], psum[2 + s][:, 0:F], ACT.Silu).then_inc(silu_done, 1)

            def tile(b, s, left):
                g = b + s
                if left:
                    silu(g + 1, 1 - s)
                act.wait_ge(at_full, g + 1)
                act.activation(aT[:, s, :, :], psum[4][:, 0:F].rearrange("p (k c) -> p k c", k=2), ACT.Copy)\
                   .then_inc(at_done, 1)
                if left > 1:
                    drain_xt(g + 2, s)
                act.wait_ge(dn_full, g + 2)
                act.wait_ge(w_ready, g + 1)
                act.wait_ge(y_sent[s], earlier(b) + 16)
                act.activation(Yt[:, s, 0:512], psum[5][:, :], ACT.Copy, scale=wsel[:, s:s + 1]).then_inc(dn_act, 1)

            drain_xt(0, 0)
            silu(0, 0)
            drain_xt(1, 1)
            with act.Fori(0, last, 2) as g0:
                for s in range(2):
                    tile(g0, s, 2)
            for s in range(2):
                tile(last, s, 1 - s)
            for i in range(TILES + 1):
                if i < TILES:
                    r = ROWS[i]
                    act.wait_ge(y_sum, i + 1)
                    link(act.activation(y1[0:r, i, :], y0[0:r, i, :], ACT.Square, bias=mv[0:r, i, 0:1],
                                        accum_out=mv[0:r, i, 1:2]))
                    act.activation(rstd[0:r, i:i + 1], mv[0:r, i, 1:2], ACT.Sqrt, scale=1.0 / D, bias=epsc[0:r, :])\
                       .then_inc(y_sq, 1)
                if i:
                    r = ROWS[i - 1]
                    act.wait_ge(y_scale, i)
                    act.activation(h1[0:r, i - 1, :], y0[0:r, i - 1, :], ACT.Identity, scale=rstd[0:r, 4 + i:5 + i],
                                   bias=mv[0:r, i - 1, 0:1]).then_inc(y_xn, 1)

        @block.vector
        def _(dve):
            chain = [0]

            def link(ins):
                chain[0] += 1
                ins.then_inc(dve_chain, 1)
                dve.wait_ge(dve_chain, chain[0])

            def statistics(buf, i, r):
                for x in range(2):
                    link(dve.bn_stats(bst[0:r, i, 6 * x:6 * x + 6], buf[0:r, i, 512 * x:512 * x + 512]))
                link(dve.bn_aggr(mv[0:r, i, :], bst[0:r, i, :]))
                dve.tensor_scalar(rstd[0:r, i:i + 1], mv[0:r, i, 1:2], EPS, None, ALU.add).then_inc(ln_var, 1)

            def normalise(n, buf, i, r):
                dve.wait_ge(ln_std, TILES * n + i + 1)
                link(dve.reciprocal(rstd[0:r, i:i + 1], rstd[0:r, 5 + i:6 + i]))
                return dve.tensor_scalar(buf[0:r, i, :], buf[0:r, i, :], mv[0:r, i, 0:1], rstd[0:r, i:i + 1],
                                         ALU.subtract, ALU.mult)

            def drain(key, out, in_):
                wait_full(dve, key)
                dve.tensor_copy(out, in_).then_inc(dve_drained, 1)

            link(dve.memset(rstd[:, :], 1.0))
            dve.memset(epsc[:, :], EPS)
            for i in range(TILES):
                dve.wait_ge(x_in[i], 32 if i == TILES - 1 else 16)
                statistics(h, i, ROWS_ALL[i])
                if i:
                    normalise(0, h, i - 1, ROWS_ALL[i - 1]).then_inc(xn_ready, 1)
            normalise(0, h, TILES - 1, ROWS_ALL[TILES - 1]).then_inc(xn_ready, 1)
            dve.wait_ge(const_in, 16 * 2)
            def low(n):
                dve.wait_ge(w_hi, CHUNKS.index(n) + 1)
                src, dst, high = flat(n)
                dve.tensor_tensor(dst, src, high, ALU.subtract).then_inc(w_split, 1)

            for i in range(TILES):
                r = ROWS_ALL[i]
                wait_full(dve, ("hT", i, 1))
                cols = slice(i * P, i * P + r)
                for k in range(4):
                    ins = dve.tensor_scalar(hx[:, 4 + k, cols], bank(("hT", i, 1))[:, k * P:k * P + r],
                                            vc("embg")[:, 4 + k:5 + k], vc("embb")[:, 4 + k:5 + k], ALU.mult, ALU.add)
                ins.then_inc(dve_drained, 1)
                wait_job(dve, ("hT", i, 1))
                dve.tensor_copy(hT_hi[:, 4:8, cols], hx[:, 4:8, cols]).then_inc(h_hi2, 1)
                dve.wait_ge(h_hi, i + 1)
                dve.tensor_tensor(hT_lo[:, 0:4, cols], hx[:, 0:4, cols], hT_hi[:, 0:4, cols], ALU.subtract)\
                   .then_inc(h_split, 1)
                if i == 2:
                    low("ga")
            low("q0")
            for x in range(2):
                drain(("ga", x), gaT[0:RANK, x * HA:x * HA + HA], bank(("ga", x))[0:RANK, 0:HA])
            low("q1")
            dve.wait_ge(tables_in, 16)

            def decay(g):
                b = g % 2
                dve.wait_ge(log_ready, g + 1)
                link(dve.scalar_tensor_tensor(dx[:, b, :], dx[:, b, :], 0.0, dt_[:, b, :], ALU.min, ALU.subtract))
                link(dve.tensor_tensor_scan(dt_[:, b, :], cst("scan"), dx[:, b, :], 0.0, ALU.mult, ALU.add))
                bp = dt_[:, b, 0:SEQ].rearrange("p (c t) -> p c t", t=CH)
                dve.tensor_tensor(dx[:, b, 0:SEQ].rearrange("p (c t) -> p c t", t=CH), bp,
                                  bp[:, :, 31:32].broadcast_to([P, NCH, CH]), ALU.subtract)
                dve.tensor_tensor(dx[:, b, TQ:T], dt_[:, b, TQ:T], dt_[:, b, TQ + 7:TQ + 8].broadcast_to([P, N_META]),
                                  ALU.subtract)
                link(dve.tensor_copy(dx[:, b, SEQ:TQ], dt_[:, b, SEQ:TQ]))
                dve.tensor_scalar(dx[:, b, :], dx[:, b, :], 1200.0, -1200.0, ALU.min, ALU.max).then_inc(dec_ready, 1)

            def apply_decay(g):
                b = g % 2
                dve.wait_ge(exp_ready, g + 1)
                dve.tensor_copy(fin[:, g, 0:8], dt_[:, b, 63:512:64])
                dve.tensor_copy(fin[:, g, 8:16], dt_[:, b, 519:576:8])
                dve.tensor_copy(fin[:, g, 16:17], dt_[:, b, T - 1:T])
                dve.tensor_copy(gq[:, g, :], dt_[:, b, 0:TQ])
                dve.tensor_copy(gk[:, g, :], den[:, b, :]).then_inc(qk_ready, 1)

            decay(0)
            decay(1)
            apply_decay(0)
            apply_decay(1)
            low("kv")
            for g in range(2, 4):
                decay(g)
                apply_decay(g)
            low("gq0")
            for i in range(TILES):
                r = ROWS_ALL[i]
                drain(("v", i), v[0:r, i, :], bank(("v", i))[0:r, 0:P])
            low("gq1")
            dve.wait_ge(qk_ready, GH)
            for n, dst, w in (("gq", gq, HQ), ("gk", gk, HA)):
                for g in range(GH):
                    for x in range(2):
                        key = (n, g, x)
                        wait_full(dve, key)
                        c = dst[:, g, x * w:x * w + w]
                        dve.scalar_tensor_tensor(c, bank(key)[:, 0:w], HK ** -0.5 if n == "gq" else 1.0, c, ALU.mult,
                                                 ALU.mult).then_inc(dve_drained, 1)
                    if g % 2:
                        low({("gq", 1): "gk0", ("gq", 3): "gk1", ("gk", 1): "gv0", ("gk", 3): "gv2"}[(n, g)])
            dve.wait_ge(spilled, 16 * TILES)

            def gla_values(x):
                for i in range(TILES):
                    r = ROWS_ALL[i]
                    drain(("gv", x, i), gv[0:r, i, 256 * x:256 * x + 256], bank(("gv", x, i))[0:r, 0:256])

            for x, after in ((0, "gv3"), (2, "gv1"), (3, "gr0")):
                gla_values(x)
                low(after)
            drain(("ktok", 0), ktok[:, 0, :], bank(("ktok", 0))[:, 0:P])
            drain(("ktok", 1), ktok[0:NS, 1, :], bank(("ktok", 1))[0:NS, 0:P])

            n = len(UNITS)
            for u in range(n + 3):
                if u < n:
                    kind, a, b = UNITS[u]
                    st = stat[:, u % 3, :]
                    key = ("s", u)
                    wait_full(dve, key)
                    if kind == "p":
                        lo = 0 if a else WINDOW - N_META
                        sv = S[:, u % 3, :].rearrange("p (k c) -> p k c", k=2)[:, :, lo:256]
                        dve.tensor_tensor(sv, bank(key)[:, :].rearrange("p (k c) -> p k c", k=2)[:, :, lo:256],
                                          bias[:, b, :, lo:256], ALU.add).then_inc(dve_drained, 1)
                        m, sink = 2, vc("sink")[:, 2 * b:2 * b + 2]
                    else:
                        sv = S[:, u % 3, 0:136].rearrange("p (k c) -> p k c", k=1)
                        dve.tensor_tensor(sv[:, 0, :], bank(key)[:, 0:136], sbias[:, b, :], ALU.add)\
                           .then_inc(dve_drained, 1)
                        m, sink = 1, vc("ssink")[:, b:b + 1]
                    dve.wait_ge(dve_drained, DRAINS[key])
                    link(dve.tensor_reduce(st[:, 0:m], sv, AX.X, ALU.max))
                    link(dve.tensor_tensor(st[:, 0:m], st[:, 0:m], sink, ALU.max))
                    dve.tensor_tensor(st[:, 4:4 + m], sink, st[:, 0:m], ALU.subtract)
                    dve.tensor_scalar(st[:, 2:2 + m], st[:, 0:m], -1.0, None, ALU.mult).then_inc(max_ready, 1)
                w = u - 1
                if 0 <= w < n:
                    kind, a, b = UNITS[w]
                    st = stat[:, w % 3, :]
                    dve.wait_ge(p_exp, w + 1)
                    m = 2 if kind == "p" else 1
                    link(dve.tensor_tensor(st[:, 10:10 + m], st[:, 6:6 + m], st[:, 8:8 + m], ALU.add))
                    link(dve.reciprocal(st[:, 12:12 + m], st[:, 10:10 + m]))
                    if kind == "p":
                        lo = 0 if a else WINDOW - N_META
                        sv = S[:, w % 3, :].rearrange("p (k c) -> p k c", k=2)[:, :, lo:256]
                        dve.tensor_tensor(sv, sv, st[:, 12:14].rearrange("p (k c) -> p k c", c=1)
                                          .broadcast_to([P, 2, 256 - lo]), ALU.mult).then_inc(p_norm, 1)
                    else:
                        dve.tensor_scalar(S[:, w % 3, 0:136], S[:, w % 3, 0:136], st[:, 12:13], None, ALU.mult)\
                           .then_inc(p_norm, 1)
                w = u - 3
                if 0 <= w < n:
                    kind, a, b = UNITS[w]
                    kv = b // 2 if kind == "p" else b
                    rows = slice(HD * kv, HD * kv + HD)
                    src = bank(("o", w))
                    if kind == "p":
                        hl = 2 * (b % 2)
                        drain(("o", w), yaT[rows, hl:hl + 2, a * P:a * P + P],
                              src[rows, 0:2 * P].rearrange("p (x c) -> p x c", x=2))
                    else:
                        dst = yaT[rows, :, SEQ + 32 * a:SEQ + 32 * a + 32].rearrange("p h (b t) -> p b h t", t=T_S)
                        src = src[rows, 0:P].rearrange("p (b h t) -> p b h t", h=4, t=T_S)
                        wait_full(dve, ("o", w))
                        for bb in range(4):
                            ins = dve.tensor_copy(dst[:, bb], src[:, bb])
                        ins.then_inc(dve_drained, 1)

            dve.wait_ge(out_done, 16 * 6)
            link(dve.memset(qz[:, :], 0.0))
            dve.memset(ss[:, :], 1.0)
            link(dve.memset(am[:, :, :], 0.0))
            for g in range(GH):
                b = g % 2
                wait_job(dve, ("keT", g, 1))
                if g:
                    wait_full(dve, ("sU", g - 1, 3))
                dve.tensor_tensor(kes[0:NS, :, :], kem[0:NS, b, 4:5, :].broadcast_to([NS, 8, P]),
                                  cst("bmask")[0:NS, :].rearrange("p (b c) -> p b c", c=1).broadcast_to([NS, 8, P]),
                                  ALU.mult)
                dve.tensor_copy(qz[:, :].rearrange("p (b r) -> p b r", r=72)[:, :, 0:T_S],
                                gq[:, g, SEQ:TQ].rearrange("p (b t) -> p b t", t=T_S)).then_inc(kes_ready, 1)
                key = ("att", g)
                wait_full(dve, key)
                bk = bank(key)[:, 0:320].rearrange("p (i t) -> p i t", t=64)
                av = am[:, b, :].rearrange("p (i t) -> p i t", t=64)
                dve.tensor_tensor(av[:, 0:4, :], bk[:, 0:4, :],
                                  cst("cmask").rearrange("p (a t) -> p a t", a=1).broadcast_to([P, 4, 64]), ALU.mult)
                dve.tensor_tensor(av[0:NS, 4, :], bk[0:NS, 4, :], cst("smask")[0:NS, :], ALU.mult)\
                   .then_inc(dve_drained, 1)
                if g:
                    wait_full(dve, ("gso", g - 1))
                for c in range(-1, NCH):
                    key = ("U", g, c)
                    wait_full(dve, key)
                    if c < 0:
                        dve.tensor_scalar(Sp[:, 0, :], bank(key)[:, 0:HV], fin[:, g, 16:17], em[:, g, 0:1], ALU.mult,
                                          ALU.mult).then_inc(dve_drained, 1)
                        dve.wait_ge(dve_drained, DRAINS[key])
                    else:
                        if c == 7 and g:
                            dve.wait_ge(sp_out, 16 * g)
                        dve.tensor_tensor(Sp[:, c + 1, :], bank(key)[:, 0:HV], Sp[:, c, :], ALU.add)\
                           .then_inc(dve_drained, 1)
                        dve.wait_ge(dve_drained, DRAINS[key])
                        if c < NCH - 1:
                            dve.tensor_scalar(Sp[:, c + 1, :], Sp[:, c + 1, :], fin[:, g, c:c + 1],
                                              em[:, g, c + 1:c + 2], ALU.mult, ALU.mult).then_inc(state_scaled, 1)
                            dve.wait_ge(state_scaled, 7 * g + c + 1)
                        else:
                            dve.tensor_scalar(Sp[:, 8, :], Sp[:, 8, :], fin[:, g, 7:8], None, ALU.mult)\
                               .then_inc(sp_final, 1)
                if g == 0:
                    gla_values(1)
                dve.wait_ge(s0_in, 16 * (g + 1))
                for x in range(4):
                    key = ("sU", g, x)
                    wait_full(dve, key)
                    sv = s0[:, 2 * x:2 * x + 2, :]
                    dve.tensor_tensor(sv, bank(key)[:, :].rearrange("p (b c) -> p b c", b=2), sv, ALU.add)\
                       .then_inc(dve_drained, 1)
                low(("gr1", "gr2", "gr3", "gatesA0")[g])
            dve.wait_ge(ss_ready, 1)
            dve.tensor_scalar(rr[:, :], ss[:, :], 1.0 / HV, EPS, ALU.mult, ALU.add).then_inc(rms_ready, 1)
            dve.wait_ge(ss_ready, 2)
            link(dve.reciprocal(rr[:, :], rr[:, :]))
            for i in range(TILES):
                r = ROWS[i]
                ov = osb[0:r, i, :].rearrange("p (g c) -> p g c", g=GH)
                dve.tensor_tensor(ov, ov, rr[0:r, 4 * i:4 * i + 4].rearrange("p (g c) -> p g c", c=1)
                                  .broadcast_to([r, GH, HV]), ALU.mult).then_inc(y_norm, 1)
            for t in (0, 4, 1, 5, 2, 6, 3, 7):
                wait_job(dve, ("gr", t, 1))
                link(dve.tensor_scalar(sg[:, t, :], sg[:, t, :], vc("normg")[:, t:t + 1], None, ALU.mult))
            low("gatesB0")
            for i in range(TILES):
                r = ROWS[i]
                for x in range(2):
                    key = ("yT", i, x)
                    wait_full(dve, key)
                    sv = sg[:, 4 * x:4 * x + 4, i * P:i * P + r]
                    dve.tensor_tensor(sv, bank(key)[:, :].rearrange("p (k c) -> p k c", k=4)[:, :, 0:r], sv, ALU.mult)\
                       .then_inc(dve_drained, 1)
            for i in range(TILES):
                cols = slice(i * P, i * P + ROWS[i])
                dve.wait_ge(yg_high, i + 1)
                dve.tensor_tensor(yg_lo[:, :, cols], sg[:, :, cols], yg_hi[:, :, cols], ALU.subtract).then_inc(yg_split, 1)
            dve.wait_ge(ya_high, 1)
            dve.tensor_tensor(ya_lo, yaT, ya_hi, ALU.subtract).then_inc(ya_split, 1)
            for y in range(4):
                low(f"brA{y}")
                low(f"brB{y}")
                for n in range(4):
                    key = ("bA", 2 * y + n // 2, n % 2)
                    wait_full(dve, key)
                    wait_job(dve, ("gA", 2 * y + n // 2, n % 2))
                    dve.tensor_tensor(sgA[:, n, :], bank(key)[:, 0:HQ], sgA[:, n, :], ALU.mult).then_inc(dve_drained, 1)
                if y < 3:
                    low(f"gatesA{y + 1}")
                for n in range(4):
                    m, x = 2 * y + n // 2, n % 2
                    key = ("bB", m, x)
                    wait_full(dve, key)
                    wait_job(dve, ("gB", m, x))
                    wait_job(dve, ("bA", m, x))
                    link(dve.tensor_tensor(sgB[:, n, :], bank(key)[:, 0:HQ], sgB[:, n, :], ALU.mult))
                    dve.tensor_tensor(mixT[:, m, x * HQ:x * HQ + HQ], sgA[:, n, :], sgB[:, n, :], ALU.add)\
                       .then_inc(dve_drained, 1)
                if y < 3:
                    low(f"gatesB{y + 1}")
            lg = R["lg"].rearrange("p (i b) -> p i b", b=36)
            wait_full(dve, ("mix", 0, 0))
            dve.memset(R["Mp"][:, 0:32], 0.0)
            link(dve.memset(R["lg"], 0.0))
            dve.wait_ge(h_back, 16 * TILES)
            dve.wait_ge(ln_in, 64)

            def logits(i):
                r = ROWS[i]
                key = ("rt", i)
                wait_full(dve, key)
                dve.tensor_tensor(lg[0:r, i, :], bank(key)[0:r, 0:36], vc("brout")[0:r, :], ALU.add)\
                   .then_inc(dve_drained, 1)

            for i in range(TILES):
                r = ROWS[i]
                for x in range(2):
                    key = ("mix", x, i)
                    wait_full(dve, key)
                    hv = h1[0:r, i, 512 * x:512 * x + 512]
                    dve.scalar_tensor_tensor(hv, hv, ALPHA, bank(key)[0:r, :], ALU.mult, ALU.add)\
                       .then_inc(dve_drained, 1)
                    if x == 0 and i >= 2:
                        logits(i - 2)
                wait_job(dve, ("mix", 1, i))
                statistics(h1, i, r)
                link(normalise(1, h1, i, r))
                link(dve.tensor_tensor(h1[0:r, i, :], h1[0:r, i, :], lng[0:r, :], ALU.mult))
                dve.tensor_tensor(h1[0:r, i, :], h1[0:r, i, :], lnb[0:r, :], ALU.add).then_inc(h1_ready, 1)
            logits(3)
            logits(4)
            wait_job(dve, ("rt", 4))

            def v3(n, b):
                return R[n].rearrange("p (i b) -> p i b", b=b)

            def bc(n, b):
                return R[n].rearrange("p (i b) -> p i b", b=1).broadcast_to([P, TILES, b])

            def tab(n, b):
                return cst(n).rearrange("p (i b) -> p i b", i=1).broadcast_to([P, TILES, b])

            def first_max(vals, w, mx, tmp, mn, oh, table):
                link(dve.tensor_reduce(R[mx], vals, AX.X, ALU.max))
                link(dve.tensor_tensor(v3(tmp, w), vals, bc(mx, w), ALU.is_equal))
                link(dve.tensor_tensor(v3(tmp, w), v3(tmp, w), tab(table, w), ALU.mult))
                link(dve.tensor_reduce(R[mn], v3(tmp, w), AX.X, ALU.min))
                link(dve.tensor_tensor(v3(oh, w), bc(mn, w), tab(table, w), ALU.is_equal))

            first_max(lg[:, :, 0:4], 4, "gmax", "gt", "gmin", "goh", "i4")
            link(dve.tensor_tensor(v3("eg", 4), lg[:, :, 0:4], bc("gmax", 4), ALU.subtract))
            def group_hot():
                return R["goh"].rearrange("p (i g e) -> p i g e", g=4, e=1).broadcast_to([P, TILES, 4, 8])

            def by_group(n):
                return R[n].rearrange("p (i g e) -> p i g e", g=4, e=8)

            link(dve.tensor_tensor(by_group("pr"), lg[:, :, 4:36].rearrange("p i (g e) -> p i g e", g=4), group_hot(),
                                   ALU.mult))
            link(dve.tensor_reduce(v3("ein", 8), R["pr"].rearrange("p (i g e) -> p i e g", g=4, e=8), AX.X, ALU.add))
            first_max(v3("ein", 8), 8, "m1", "t8", "mn", "oh1", "i8")
            link(dve.scalar_tensor_tensor(R["ein"], R["oh1"], -1e30, R["ein"], ALU.mult, ALU.add))
            first_max(v3("ein", 8), 8, "m2", "t8", "mn", "oh2", "i8")
            dve.tensor_tensor(R["ex"], R["m2"], R["m1"], ALU.subtract).then_inc(rt_exp_in, 1)
            for n, oh in (("M1", "oh1"), ("M2", "oh2")):
                link(dve.tensor_tensor(by_group(n), group_hot(), R[oh].rearrange("p (i g e) -> p i g e", g=1, e=8)
                                       .broadcast_to([P, TILES, 4, 8]), ALU.mult))
            link(dve.tensor_tensor(R["M"], R["M1"], R["M2"], ALU.add))
            link(dve.tensor_tensor(v3("M", 32), v3("M", 32), cst("valid").rearrange("p (i b) -> p i b", b=1)
                                   .broadcast_to([P, TILES, 32]), ALU.mult))
            for i in range(TILES):
                ins = dve.tensor_tensor(R["Mp"][:, 32 * i + 32:32 * i + 64], R["Mp"][:, 32 * i:32 * i + 32],
                                        R["M"][:, 32 * i:32 * i + 32], ALU.add)
                if i < TILES - 1:
                    link(ins)
            ins.then_inc(mask_ready, 1)
            dve.wait_ge(rt_exp, 1)
            link(dve.tensor_reduce(R["gsum"], v3("eg", 4), AX.X, ALU.add))
            link(dve.tensor_scalar(R["w1"], R["ex"], 1.0, None, ALU.add))
            link(dve.tensor_tensor(R["w1"], R["w1"], R["gsum"], ALU.mult))
            link(dve.reciprocal(R["w1"], R["w1"]))
            link(dve.tensor_tensor(R["w2"], R["w1"], R["ex"], ALU.mult))
            dve.memset(ent[:, :, 3], 0)
            for n in range(2):
                dve.tensor_copy(ent[:, 5 * n:5 * n + 5, 0], cst("tok"))
                dve.tensor_scalar(ent[:, 5 * n:5 * n + 5, 1], cst("tok"), float(TQ * n), None, ALU.add)
                dve.tensor_copy(ent[:, 5 * n:5 * n + 5, 2].bitcast(f32), R[f"w{n + 1}"])
            key = ("cnt",)
            wait_full(dve, key)
            dve.tensor_copy(R["cnt"], bank(key)[:, 0:32]).then_inc(dve_drained, 1)
            wait_job(dve, key)
            link(dve.tensor_scalar(R["nt"], R["cnt"], 128.0, None, ALU.is_gt))
            for k in range(2, 5):
                link(dve.scalar_tensor_tensor(R["nt"], R["cnt"], 128.0 * k, R["nt"], ALU.is_gt, ALU.add))
            link(dve.tensor_tensor_scan(R["inc"], ones[:, 0:32], R["nt"], 0.0, ALU.mult, ALU.add))
            link(dve.tensor_scalar(R["t5"], cst("evens"), R["inc"][:, 31:32], None, ALU.is_lt))
            link(dve.tensor_reduce(R["r1"][:, 0:1], R["t5"], AX.X, ALU.add))
            dve.tensor_scalar(lst[0:1, 128:129], R["r1"][0:1, 0:1], 2.0, float(N_EXP - 2), ALU.mult, ALU.add)
            link(dve.tensor_scalar(R["cnt"], R["inc"], cst("pid"), None, ALU.is_le))
            link(dve.tensor_reduce(R["eg1"], R["cnt"], AX.X, ALU.add))
            dve.tensor_scalar(R["eg1"], R["eg1"], cst("plow"), float(N_EXP - 1), ALU.add, ALU.min).then_inc(ids_ready, 1)
            wait_full(dve, ("pos",))
            dve.tensor_copy(R["pos"], bank(("pos",))[:, 0:160]).then_inc(dve_drained, 1)
            wait_job(dve, ("pos",))
            link(dve.tensor_scalar(R["q"], R["pos"], 128.0, None, ALU.is_ge))
            link(dve.tensor_tensor(R["inc"], R["inc"], R["nt"], ALU.subtract))
            link(dve.tensor_tensor(R["inc"], R["inc"], cst("e31"), ALU.add))
            dve.tensor_tensor(v3("t160", 32), v3("q", 32), R["inc"].rearrange("p (i b) -> p i b", i=1)
                              .broadcast_to([P, TILES, 32]), ALU.mult)
            for k in range(2, 5):
                link(dve.scalar_tensor_tensor(R["q"], R["pos"], 128.0 * k, R["q"], ALU.is_ge, ALU.add))
            link(dve.scalar_tensor_tensor(R["q"], R["q"], 1.0 - 128.0 * MAX_TILES, R["t160"], ALU.mult, ALU.add))
            link(dve.scalar_tensor_tensor(R["q"], R["pos"], float(MAX_TILES), R["q"], ALU.mult, ALU.add))
            link(dve.tensor_tensor(v3("q", 32), v3("q", 32), cst("eid").rearrange("p (i b) -> p i b", i=1)
                                   .broadcast_to([P, TILES, 32]), ALU.add))
            for n, m in enumerate(("M1", "M2")):
                link(dve.tensor_tensor(R["t160"], R["q"], R[m], ALU.mult))
                link(dve.tensor_reduce(R["r1"][:, 5 * n:5 * n + 5], v3("t160", 32), AX.X, ALU.add))
                dve.tensor_copy(rowi[:, 5 * n:5 * n + 5], R["r1"][:, 5 * n:5 * n + 5]).then_inc(rows_ready, 1)
            key = ("lst",)
            wait_full(dve, key)
            dve.tensor_copy(lst[0:1, 0:128], bank(key)[0:1, 0:128]).then_inc(dve_drained, 1)
            wait_job(dve, key)
            dve.sem_inc(list_ready, 1)

            last = dve.value_load(lst[0:1, 128:129], min_val=N_EXP - 2, max_val=MAX_TILES - 4)

            def drain_xt(g, s):
                dve.wait_ge(xt_full, g + 1)
                dve.tensor_copy(XT[:, s, 4:8, :], psum[1][:, :].rearrange("p (k c) -> p k c", k=4)).then_inc(xt_dve, 1)

            def gate(g, s):
                dve.wait_ge(silu_done, g + 1)
                dve.tensor_tensor(act_[:, s, :], psum[2 + s][:, F:2 * F], sil[:, s, :], ALU.mult).then_inc(act_done, 1)

            def tile(b, s, left):
                g = b + s
                if left:
                    gate(g + 1, 1 - s)
                dve.tensor_copy(wsel[:, s:s + 1], tb[:, bass.ds(g, 1), 2].bitcast(f32)).then_inc(w_ready, 1)
                if left > 1:
                    drain_xt(g + 2, s)
                dve.wait_ge(dn_full, g + 2)
                dve.wait_ge(w_ready, g + 1)
                dve.wait_ge(y_sent[s], earlier(b) + 16)
                dve.tensor_scalar(Yt[:, s, 512:1024], psum[6][:, :], wsel[:, s:s + 1], None, ALU.mult)\
                   .then_inc(dn_dve, 1)

            dve.wait_ge(h1_stored, 16 * TILES)
            for i in range(TILES):
                r = ROWS[i]
                dve.tensor_scalar(h1[0:r, i, :], h1[0:r, i, :], ALPHA, None, ALU.mult).then_inc(h1_scaled, 1)
            dve.wait_ge(tb_in, 16)
            drain_xt(0, 0)
            gate(0, 0)
            drain_xt(1, 1)
            with dve.Fori(0, last, 2) as g0:
                for s in range(2):
                    tile(g0, s, 2)
            for s in range(2):
                tile(last, s, 1 - s)
            dve.wait_ge(h1_scaled, TILES)
            dve.wait_ge(ln_in, 96)
            for i in range(TILES + 2):
                if i < TILES:
                    r = ROWS[i]
                    dve.wait_ge(y_part, i + 1)
                    link(dve.scalar_tensor_tensor(y0[0:r, i, :], h1[0:r, i, :], 1.0, y0[0:r, i, :], ALU.mult, ALU.add,
                                                  accum_out=mv[0:r, i, 0:1]))
                    dve.tensor_scalar(mv[0:r, i, 0:1], mv[0:r, i, 0:1], -1.0 / D, None, ALU.mult).then_inc(y_sum, 1)
                if 1 <= i <= TILES:
                    j = i - 1
                    r = ROWS[j]
                    dve.wait_ge(y_sq, j + 1)
                    link(dve.reciprocal(rstd[0:r, 5 + j:6 + j], rstd[0:r, j:j + 1]))
                    dve.tensor_tensor(mv[0:r, j, 0:1], mv[0:r, j, 0:1], rstd[0:r, 5 + j:6 + j], ALU.mult)\
                       .then_inc(y_scale, 1)
                if i >= 2:
                    j = i - 2
                    r = ROWS[j]
                    dve.wait_ge(y_xn, j + 1)
                    dve.tensor_tensor(h1[0:r, j, :], h1[0:r, j, :], lng[0:r, :], ALU.mult).then_inc(y_g, 1)
            for i in (3, 4):
                r = ROWS[i]
                dve.wait_ge(y_g, i + 1)
                dve.tensor_tensor(h1[0:r, i, :], h1[0:r, i, :], lnb[0:r, :], ALU.add).then_inc(y_ready2, 1)

        @block.tensor
        def _(pe):
            def open_bank(key):
                n = INDEX[key]
                if n >= NBANK:
                    wait_job(pe, ORDER[n - NBANK][0])
                return bank(key)

            def full(ins):
                ins.then_inc(psum_full, 1)

            phase = {"lo": lambda k: hT_lo[:, k, :]}

            def split_product(out, stat, mov, first, last):
                (sh, sl), (mh, ml) = stat, mov
                pe.matmul(out, sh, mh, start=first, stop=False)
                pe.matmul(out, sh, ml, start=False, stop=False)
                return pe.matmul(out, sl, mh, start=False, stop=last)

            def feature_job(key, w, cols, lo, n):
                bk = open_bank(key)
                m = cols.stop - cols.start
                for kc in range(KC):
                    ins = split_product(bk[0:m, 0:n], (w[0][:, kc, cols], w[1][:, kc, cols]),
                                        (hT_hi[:, kc, lo:lo + n], phase["lo"](kc)[:, lo:lo + n]), kc == 0, kc == KC - 1)
                full(ins)

            def token_job(key, w, cols, i):
                bk = open_bank(key)
                r = ROWS_ALL[i]
                t = slice(i * P, i * P + r)
                for kc in range(KC):
                    ins = split_product(bk[0:r, 0:cols.stop - cols.start], (hT_hi[:, kc, t], phase["lo"](kc)[:, t]),
                                        (w[0][:, kc, cols], w[1][:, kc, cols]), kc == 0, kc == KC - 1)
                full(ins)

            pe.wait_ge(const_in, 16 * 2)
            for i in range(TILES):
                r = ROWS_ALL[i]
                pe.wait_ge(xn_ready, i + 1)
                for x in range(2):
                    bk = open_bank(("hT", i, x))
                    for k in range(4):
                        c = (4 * x + k) * P
                        ins = pe.transpose(bk[:, k * P:k * P + r], h[0:r, i, c:c + P], ident[0:r, 0:r])
                    full(ins)
            wait_split(pe, "ga")
            w = parts("ga")
            for x in range(2):
                pe.wait_ge(h_split, 5 if x else 3)
                pe.wait_ge(h_split2, 5 if x else 3)
                feature_job(("ga", x), w, slice(0, RANK), x * HA, HA)
            wait_job(pe, ("ga", 1))
            pe.wait_ge(w2_in, 16)
            def decay_job(g):
                for x in range(2):
                    bk = open_bank(("la", g, x))
                    full(pe.matmul(bk[:, 0:HA], w2[0:RANK, g * P:g * P + P], gaT[0:RANK, x * HA:x * HA + HA], start=True,
                                   stop=True))

            decay_job(0)
            decay_job(1)
            for t in range(4):
                if t % 2 == 0:
                    wait_split(pe, f"q{t // 2}")
                    w = parts(f"q{t // 2}")
                if t >= 2:
                    decay_job(t)
                for x in range(2):
                    feature_job(("q", t, x), w, slice(t % 2 * P, t % 2 * P + P), x * HQ, HQ)
            wait_split(pe, "kv")
            w = parts("kv")
            for x in range(2):
                feature_job(("k", x), w, slice(0, P), x * HA, HA)
            for i in range(TILES):
                token_job(("v", i), w, slice(P, 2 * P), i)
            for n, wd_ in (("gq", HQ), ("gk", HA)):
                for g in range(GH):
                    if g % 2 == 0:
                        wait_split(pe, f"{n}{g // 2}")
                        w = parts(f"{n}{g // 2}")
                    for x in range(2):
                        feature_job((n, g, x), w, slice(g % 2 * P, g % 2 * P + P), x * wd_, wd_)

            def gla_values(x):
                wait_split(pe, f"gv{x}")
                for i in range(TILES):
                    token_job(("gv", x, i), parts(f"gv{x}"), slice(0, 256), i)

            for x in (0, 2, 3):
                gla_values(x)
            wait_job(pe, ("k", 1))
            full(pe.transpose(open_bank(("ktok", 0))[:, 0:P], kT[:, 384:512], ident[:, :]))
            full(pe.transpose(open_bank(("ktok", 1))[0:NS, 0:P], kT[:, SEQ:TQ], ident[:, :]))
            pe.wait_ge(state_in, 32)
            for x in range(2):
                bk = open_bank(("kbT", x))
                for b in range(4):
                    ins = pe.transpose(bk[:, b * P:b * P + P], sbk[:, 4 * x + b, :], ident[:, :])
                full(ins)

            def scores(u):
                kind, a, b = UNITS[u]
                bk = open_bank(("s", u))
                if kind == "p":
                    rows = slice(HD * (b // 2), HD * (b // 2) + HD)
                    for x in range(2):
                        q = qT[rows, 2 * (b % 2) + x, a * P:a * P + P]
                        c = x * 256
                        if a:
                            ins = pe.matmul(bk[:, c:c + 256], q, kT[rows, (a - 1) * P:(a + 1) * P], start=True, stop=True)
                        else:
                            pe.matmul(bk[:, c + P - N_META:c + P], q, kT[rows, TQ:T], start=True, stop=True)
                            ins = pe.matmul(bk[:, c + P:c + 256], q, kT[rows, 0:P], start=True, stop=True)
                else:
                    for bb in range(4):
                        s = 4 * a + bb
                        q = qs[HD * b:HD * b + HD, s, :]
                        pe.matmul(bk[32 * bb:32 * bb + 32, 0:P], q, kbT[HD * b:HD * b + HD, s, :], start=True, stop=True)
                        ins = pe.matmul(bk[32 * bb:32 * bb + 32, P:P + T_S], q,
                                        kT[HD * b:HD * b + HD, SEQ + T_S * s:SEQ + T_S * s + T_S], start=True, stop=True)
                full(ins)

            def turn(u):
                kind, a, b = UNITS[u]
                pe.wait_ge(p_norm, u + 1)
                bk = open_bank(("pT", u))
                if kind == "p":
                    for kv in range(2):
                        c = kv * 256
                        if a:
                            pe.transpose(bk[:, c:c + P], S[:, u % 3, c:c + P], ident[:, :])
                        else:
                            pe.transpose(bk[0:N_META, c:c + P], S[:, u % 3, c + P - N_META:c + P], ident[:, :])
                        ins = pe.transpose(bk[:, c + P:c + 256], S[:, u % 3, c + P:c + 256], ident[:, :])
                else:
                    pe.transpose(bk[:, 0:P], S[:, u % 3, 0:P], ident[:, :])
                    ins = pe.transpose(bk[0:T_S, P:2 * P], S[:, u % 3, P:P + T_S], ident[:, :])
                full(ins)

            def values(u):
                kind, a, b = UNITS[u]
                wait_job(pe, ("pT", u))
                bk = open_bank(("o", u))
                kv = b // 2 if kind == "p" else b
                rows = bk[HD * kv:HD * kv + HD, :]
                cols = slice(HD * kv, HD * kv + HD)
                if kind == "p":
                    for x in range(2):
                        pt = PT[:, u % 3, x * 256:x * 256 + 256]
                        out = rows[:, x * P:x * P + P]
                        if a:
                            pe.matmul(out, v[:, a - 1, cols], pt[:, 0:P], start=True, stop=False)
                        else:
                            pe.matmul(out, vm[0:N_META, cols], pt[0:N_META, 0:P], start=True, stop=False)
                        ins = pe.matmul(out, v[:, a, cols], pt[:, P:2 * P], start=False, stop=True)
                else:
                    pt = PT[:, u % 3, :]
                    for bb in range(4):
                        s = 4 * a + bb
                        o = rows[:, 32 * bb:32 * bb + 32]
                        pe.matmul(o, sbv[:, s, cols], pt[:, 32 * bb:32 * bb + 32], start=True, stop=False)
                        ins = pe.matmul(o, vn[0:T_S, s, cols], pt[0:T_S, P + 32 * bb:P + 32 * bb + 32], start=False,
                                        stop=True)
                full(ins)

            wait_job(pe, ("kbT", 1))
            pe.wait_ge(rows_moved, 16 * 9)
            n = len(UNITS)
            for u in range(n + 3):
                if u < n:
                    scores(u)
                if 0 <= u - 2 < n:
                    turn(u - 2)
                if 0 <= u - 3 < n:
                    values(u - 3)

            phase["lo"] = lambda k: lo_r[:, k, :] if k < 5 else lo_ln[:, k - 5, :]

            def output_gate(y):
                pe.wait_ge(lo_moved, 1)
                wait_split(pe, f"gr{y}")
                for n, t in enumerate((y, y + 4)):
                    for x in range(2):
                        feature_job(("gr", t, x), parts(f"gr{y}"), slice(n * P, n * P + P), x * HQ, HQ)

            for g in range(GH):
                b = g % 2
                wait_job(pe, ("gk", g, 1))
                bk = open_bank(("keT", g, 0))
                for i in range(4):
                    ins = pe.transpose(bk[:, i * P:i * P + P], gk[:, g, i * P:i * P + P], ident[:, :])
                full(ins)
                full(pe.transpose(open_bank(("keT", g, 1))[0:NS + N_META, 0:P], gk[:, g, SEQ:T], ident[:, :]))
                bk = open_bank(("att", g))
                for c in range(NCH):
                    r, i = 64 * (c % 2), c // 2
                    pe.matmul(bk[r:r + 64, 64 * i:64 * i + 64], gk[:, g, CH * c:CH * c + CH], gq[:, g, CH * c:CH * c + CH],
                              start=True, stop=True)
                full(pe.matmul(bk[0:NS, 256:320], gk[:, g, SEQ:TQ], gq[:, g, SEQ:TQ], start=True, stop=True))
                wait_job(pe, ("keT", g, 1))
                gcol = slice(g * HV, g * HV + HV)
                for c in range(-1, NCH):
                    bk = open_bank(("U", g, c))
                    if c < 0:
                        ins = pe.matmul(bk[:, 0:HV], kem[NS:NS + N_META, b, 4, :], gv[NS:NS + N_META, 4, gcol], start=True,
                                        stop=True)
                    else:
                        r = 64 * (c % 2)
                        ins = pe.matmul(bk[:, 0:HV], kem[r:r + 64, b, c // 2, :], gv[r:r + 64, c // 2, gcol], start=True,
                                        stop=True)
                    full(ins)
                if g:
                    output_gate(g - 1)
                else:
                    pe.wait_ge(lo_moved, 1)
                    gla_values(1)
                for i in range(4):
                    if i == 0:
                        wait_job(pe, ("U", g, -1))
                    pe.wait_ge(state_scaled, 7 * g + 2 * i + 1)
                    bk = open_bank(("go", g, i))
                    for c in (2 * i, 2 * i + 1):
                        r = 64 * (c % 2)
                        pe.matmul(bk[r:r + 64, 0:HV], am[r:r + 64, b, 64 * i:64 * i + 64], gv[r:r + 64, i, gcol],
                                  start=True, stop=False)
                        ins = pe.matmul(bk[r:r + 64, 0:HV], gq[:, g, CH * c:CH * c + CH], Sp[:, c, :], start=False,
                                        stop=True)
                    full(ins)
                pe.wait_ge(s0_in, 16 * (g + 1))
                pe.wait_ge(kes_ready, g + 1)
                bk = open_bank(("gso", g))
                pe.matmul(bk[0:NS, 0:HV], am[0:NS, b, 256:320], gv[0:NS, 4, gcol], start=True, stop=False)
                for s in range(8):
                    ins = pe.matmul(bk[0:NS, 0:HV], qz[:, 64 * s:64 * s + 64], s0[:, s, :], start=False, stop=(s == 7))
                full(ins)
                for x in range(4):
                    bk = open_bank(("sU", g, x))
                    for s in range(2):
                        ins = pe.matmul(bk[:, s * HV:s * HV + HV], kes[0:NS, 2 * x + s, :], gv[0:NS, 4, gcol], start=True,
                                        stop=True)
                    full(ins)

            output_gate(3)
            for i in range(TILES):
                r = ROWS[i]
                pe.wait_ge(y_norm, i + 1)
                for x in range(2):
                    bk = open_bank(("yT", i, x))
                    for k in range(4):
                        c = (4 * x + k) * P
                        ins = pe.transpose(bk[:, k * P:k * P + r], osb[0:r, i, c:c + P], ident[0:r, 0:r])
                    full(ins)
            for y in range(4):
                blocks = [(m, x, slice(m % 2 * P, m % 2 * P + P)) for m in (2 * y, 2 * y + 1) for x in range(2)]
                for n in ("A", "B"):
                    wait_split(pe, f"gates{n}{y}")
                    for m, x, cols in blocks:
                        feature_job(("g" + n, m, x), parts(f"gates{n}{y}"), cols, x * HQ, HQ)
                for n, (high, low), nk in (("A", (ya_hi, ya_lo), 4), ("B", (yg_hi, yg_lo), 8)):
                    if n == "A":
                        pe.wait_ge(ya_split, 1)
                    else:
                        pe.wait_ge(yg_split, TILES)
                    wait_split(pe, f"br{n}{y}")
                    wh, wl = parts(f"br{n}{y}")
                    for m, x, cols in blocks:
                        bk = open_bank(("b" + n, m, x))
                        t = slice(x * HQ, x * HQ + HQ)
                        for kc in range(nk):
                            ins = split_product(bk[:, 0:HQ], (wh[:, kc, cols], wl[:, kc, cols]),
                                                (high[:, kc, t], low[:, kc, t]), kc == 0, kc == nk - 1)
                        full(ins)
            wait_job(pe, ("bB", 7, 1))
            pe.wait_ge(wrt_in, 16 * 2)

            def mix_job(x, i):
                bk = open_bank(("mix", x, i))
                r = ROWS[i]
                if i == 0:
                    pe.wait_ge(wo_in[x], 32)
                for kc in range(KC):
                    ins = pe.matmul(bk[0:r, :], mixT[:, kc, i * P:i * P + r], wo(x, kc), start=(kc == 0),
                                    stop=(kc == KC - 1))
                full(ins)

            def router_job(i):
                wait_job(pe, ("h1T", i, 1))
                bk = open_bank(("rt", i))
                r = ROWS[i]
                for kc in range(KC):
                    ins = pe.matmul(bk[0:r, 0:36], h1T[:, kc, i * P:i * P + r], wrt[:, kc, :], start=(kc == 0),
                                    stop=(kc == KC - 1))
                full(ins)

            for i in range(TILES + 1):
                if i < TILES:
                    mix_job(0, i)
                if i >= 2:
                    router_job(i - 2)
                if i < TILES:
                    mix_job(1, i)
                if i:
                    j = i - 1
                    r = ROWS[j]
                    pe.wait_ge(h1_ready, j + 1)
                    for x in range(2):
                        bk = open_bank(("h1T", j, x))
                        for k in range(4):
                            c = (4 * x + k) * P
                            ins = pe.transpose(bk[:, k * P:k * P + r], h1[0:r, j, c:c + P], ident[0:r, 0:r])
                        full(ins)
            router_job(TILES - 1)
            pe.wait_ge(mask_ready, 1)
            full(pe.matmul(open_bank(("cnt",))[:, 0:32], ones, R["Mp"][:, 160:192], start=True, stop=True))
            bk = open_bank(("pos",))
            pe.matmul(bk[:, 0:160], tri, R["M"], start=True, stop=False)
            full(pe.matmul(bk[:, 0:160], ones, R["Mp"][:, 0:160], start=False, stop=True))
            pe.wait_ge(ids_ready, 1)
            full(pe.matmul(open_bank(("lst",))[0:1, 0:128], R["eg1"], ident, start=True, stop=True))

            wait_job(pe, ("lst",))
            pe.wait_ge(list_ready, 1)
            last = pe.value_load(lst[0:1, 128:129], min_val=N_EXP - 2, max_val=MAX_TILES - 4)
            pe.sem_inc(dn_full, 1)
            pe.sem_inc(dn_act, 1)
            pe.sem_inc(dn_dve, 1)

            def turn_x(b, s):
                pe.wait_ge(gathered[s], earlier(b) + 16)
                for k in range(KC):
                    ins = pe.transpose(psum[k // 4][:, k % 4 * P:k % 4 * P + P], Xg[:, s, k:D:KC], ident)
                ins.then_inc(xt_full, 1)

            def gate_up(b, s):
                g = b + s
                pe.wait_ge(xt_act, g + 1)
                pe.wait_ge(xt_dve, g + 1)
                pe.wait_ge(wg_in[s], earlier(b) * 2 + 32)
                for kc in range(KC):
                    ins = pe.matmul(psum[2 + s][:, :], XT[:, s, kc, :], wgu[s][:, kc, :], start=(kc == 0),
                                    stop=(kc == KC - 1))
                ins.then_inc(gu_full, 1)

            def tile(b, s, left):
                g = b + s
                if left:
                    gate_up(b + 2 * s, 1 - s)
                pe.wait_ge(act_done, g + 1)
                for k in range(2):
                    ins = pe.transpose(psum[4][:, k * P:k * P + P], act_[:, s, k:F:2], ident)
                ins.then_inc(at_full, 1)
                if left > 1:
                    pe.wait_ge(xt_act, g + 2)
                    turn_x(b + 2, s)
                pe.wait_ge(at_done, g + 1)
                pe.wait_ge(wd_in[s], earlier(b) + 16)
                pe.wait_ge(dn_act, g + 1)
                pe.wait_ge(dn_dve, g + 1)
                for half in range(2):
                    for k in range(2):
                        ins = pe.matmul(psum[5 + half][:, :], aT[:, s, k, :], wd[s][:, k, 512 * half:512 * half + 512],
                                        start=(k == 0), stop=(k == 1))
                ins.then_inc(dn_full, 1)

            turn_x(0, 0)
            gate_up(0, 0)
            turn_x(0, 1)
            with pe.Fori(0, last, 2) as g0:
                for s in range(2):
                    tile(g0, s, 2)
            for s in range(2):
                tile(last, s, 1 - s)


def constants():
    import numpy as np

    c = np.zeros((P, CONST_W), np.float32)

    def put(n, a):
        o, w = CONST[n]
        c[:, o:o + w] = np.asarray(a, np.float32).reshape(a.shape[0], -1) if a.shape[0] == P else a

    p = np.arange(P)
    put("ident", np.eye(P))
    put("tri", (p[:, None] < p[None, :]) * 1.0)
    put("ones", np.ones((P, P)))
    scan = np.ones(T)
    scan[0:SEQ:CH] = 0
    scan[SEQ:TQ:T_S] = 0
    scan[TQ] = 0
    put("scan", np.tile(scan, (P, 1)))
    slope = 2.0 ** -np.arange(1, HEADS + 1)

    def alibi(dist, s):
        return np.where((dist >= 0) & (dist < WINDOW), -s * dist, -1e30)

    dist = p[:, None] + WINDOW - np.arange(256)[None, :]
    b = np.zeros((P, HEADS, 256))
    for n in range(HEADS):
        b[:, n] = alibi(dist, slope[n])
    put("bias", b)
    rows_t, rows_h = p % T_S, p // T_S % 4
    dist = rows_t[:, None] + WINDOW - np.arange(WINDOW + T_S)[None, :]
    b = np.zeros((P, 2, WINDOW + T_S))
    for kv in range(2):
        b[:, kv] = alibi(dist, slope[4 * kv + rows_h][:, None])
    put("sbias", b)
    t = np.arange(64)
    put("cmask", (p[:, None] % 64 <= t[None, :]) * 1.0)
    put("smask", ((p[:, None] // T_S == t[None, :] // T_S) & (p[:, None] <= t[None, :])) * 1.0)
    put("bmask", (p[:, None] // T_S == np.arange(8)[None, :]) * 1.0)
    put("i4", np.tile(np.arange(4) - 99.0, (P, 1)))
    put("i8", np.tile(np.arange(8) - 99.0, (P, 1)))
    tok = p[:, None] + P * np.arange(TILES)[None, :]
    put("valid", (tok < TQ) * 1.0)
    put("tok", tok)
    put("pid", p[:, None] - N_EXP)
    put("plow", np.where(p < N_EXP, p, 0)[:, None])
    put("evens", np.tile(2.0 * np.arange(5), (P, 1)))
    put("eid", np.tile(np.arange(N_EXP), (P, 1)))
    put("e31", np.tile(31 - np.arange(N_EXP), (P, 1)))
    return c


_INS = ["x_prompt", "x_sample", "state_swa_k", "state_swa_v", "state_gla", "meta_tokens", "ln_emb_g", "ln_emb_b", "w_in",
        "w_alpha2", "w_attn_br", "w_gla_br", "w_out", "ln1_g", "ln1_b", "w_router_group", "w_router_expert", "w_exp_gate",
        "w_exp_up", "w_exp_down", "ln2_g", "ln2_b"]
_OUTS = [(1, SEQ, D), (NB_S, T_S, D), (1, 1, WINDOW, N_KV, HD), (1, 1, WINDOW, N_KV, HD), (1, 1, GH, HK, HV),
         (1, NB_S, WINDOW, N_KV, HD), (1, NB_S, WINDOW, N_KV, HD), (1, NB_S, GH, HK, HV)]


def kernel(**inputs):
    import numpy as _np
    import concourse.bacc as _bacc
    from concourse import mybir as _mybir
    from concourse.bass_utils import run_bass_kernel_spmd as _run

    arrays = {n: _np.ascontiguousarray(inputs[n]) for n in _INS}
    arrays["const"] = constants()
    arrays["w_q"] = _np.ascontiguousarray(_np.asarray(inputs["w_in"])[0, :, 0:512].reshape(D, 2, 4, HD)
                                          .transpose(0, 2, 1, 3).reshape(D, 512))
    v = _np.zeros((P, VEC_W), _np.float32)

    def put(n, a):
        v[:, VEC[n][0]:VEC[n][0] + VEC[n][1]] = a

    sink = _np.asarray(inputs["attn_sink"])[0]
    put("sink", _np.broadcast_to(sink, (P, HEADS)))
    put("ssink", _np.tile(_np.repeat(sink.reshape(2, 4), T_S, axis=1), (1, 4)).T)
    put("balpha", _np.asarray(inputs["b_alpha"])[0].reshape(4, P).T)
    put("bgate", _np.asarray(inputs["b_gate"])[0].reshape(16, P).T)
    put("normg", _np.asarray(inputs["gla_norm_g"])[0].reshape(8, P).T)
    put("embg", _np.asarray(inputs["ln_emb_g"]).reshape(8, P).T)
    put("embb", _np.asarray(inputs["ln_emb_b"]).reshape(8, P).T)
    put("brout", _np.broadcast_to(_np.concatenate([_np.asarray(inputs["b_router_group"])[0],
                                                   _np.asarray(inputs["b_router_expert"])[0]]), (P, 36)))
    arrays["vec"] = v
    nc = _bacc.Bacc("TRN2", target_bir_lowering=False, num_devices=1)
    A = {n: nc.dram_tensor(f"in_{n}", a.shape, _mybir.dt.from_np(a.dtype), kind="ExternalInput").ap()
         for n, a in arrays.items()}
    O = [nc.dram_tensor(f"out_{i}", shape, _mybir.dt.float32, kind="ExternalOutput").ap()
         for i, shape in enumerate(_OUTS)]
    decoder_kernel(nc, A, O)
    r = _run(nc, [{f"in_{n}": a for n, a in arrays.items()}], core_ids=[0])
    return tuple(r.results[0][f"out_{i}"] for i in range(len(_OUTS)))
```
